# Optimizing a Trainium2 kernel written in Bass

```python
import math
import jax, jax.numpy as jnp
from jax import lax
import numpy as np

D_MODEL = 1024
BATCH = 1
SEQ = 2048
DEPTH = 1

CHUNK = 64
MEM_LEN = 256
EPS = 1e-6

SB_HEADS = 8
SB_HEAD_DIM = 64
SB_WIDTH = SB_HEADS * SB_HEAD_DIM
SB_Q_BLOCK = 128

DN_HEADS = 4
DN_HEAD_DIM = 128
DN_WIDTH = DN_HEADS * DN_HEAD_DIM
DN_CONV = 4

XA_HEADS = 4
XA_HEAD_DIM = 64
XA_WIDTH = XA_HEADS * XA_HEAD_DIM

N_GROUPS = 4
EXPERTS_PER_GROUP = 8
N_EXPERTS = N_GROUPS * EXPERTS_PER_GROUP
TOP_K = 2
D_EXPERT = 512
MOE_BLOCK = 128

N_BRANCHES = 2
IN_SPLIT_SIZES = (3 * SB_WIDTH, 3 * DN_WIDTH, DN_HEADS, DN_HEADS, DN_WIDTH, N_BRANCHES * D_MODEL)
IN_WIDTH = 3 * SB_WIDTH + 3 * DN_WIDTH + 2 * DN_HEADS + DN_WIDTH + N_BRANCHES * D_MODEL
MIX_WIDTH = SB_WIDTH + DN_WIDTH

kernel_name = "hybrid_stickbreak_gdn_hiermoe_block"

def rmsnorm(x, g):
    xf = x.astype(jnp.float32)
    r = lax.rsqrt(jnp.mean(xf * xf, axis=-1, keepdims=True) + EPS)
    return (xf * r * g.astype(jnp.float32)).astype(x.dtype)

def l2norm(x):
    xf = x.astype(jnp.float32)
    return (xf * lax.rsqrt(jnp.sum(xf * xf, axis=-1, keepdims=True) + EPS)).astype(x.dtype)

def causal_depthwise_conv(x, w):
    k = w.shape[0]
    return lax.conv_general_dilated(
        x, w[:, None, :].astype(x.dtype), window_strides=(1,), padding=[(k - 1, 0)],
        dimension_numbers=('NWC', 'WIO', 'NWC'), feature_group_count=x.shape[-1])

def stick_breaking_attention(q, k, v):
    b, h, s, dh = q.shape
    nb = s // SB_Q_BLOCK
    scale = dh ** -0.5
    qb = jnp.moveaxis(q.reshape(b, h, nb, SB_Q_BLOCK, dh), 2, 0)
    key_pos = jnp.arange(s)

    def block(args):
        qi, i = args
        q_pos = i * SB_Q_BLOCK + jnp.arange(SB_Q_BLOCK)
        z = jnp.einsum('bhqd,bhkd->bhqk', qi, k).astype(jnp.float32) * scale
        mask = key_pos[None, :] < q_pos[:, None]
        log_beta = jax.nn.log_sigmoid(z)
        log_keep = jnp.where(mask, jax.nn.log_sigmoid(-z), 0.0)
        later = lax.cumsum(log_keep, axis=3, reverse=True) - log_keep
        a = jnp.where(mask, jnp.exp(log_beta + later), 0.0)
        return jnp.einsum('bhqk,bhkd->bhqd', a.astype(v.dtype), v)

    out = lax.map(block, (qb, jnp.arange(nb)))
    return jnp.moveaxis(out, 0, 2).reshape(b, h, s, dh)

def gated_delta_rule(q, k, v, g, beta):
    out_dtype = v.dtype
    b, h, s, dk = q.shape
    dv = v.shape[-1]
    n, c = s // CHUNK, CHUNK
    f32 = jnp.float32
    q = (q.astype(f32) * dk ** -0.5).reshape(b, h, n, c, dk)
    k = k.astype(f32).reshape(b, h, n, c, dk)
    v = v.astype(f32).reshape(b, h, n, c, dv)
    beta = beta.astype(f32).reshape(b, h, n, c, 1)
    g = lax.cumsum(g.astype(f32).reshape(b, h, n, c), axis=3)
    incl = jnp.tril(jnp.ones((c, c), dtype=bool))
    strict = jnp.tril(jnp.ones((c, c), dtype=bool), -1)
    gamma = jnp.exp(jnp.where(incl, g[..., :, None] - g[..., None, :], -jnp.inf))
    kk = jnp.einsum('bhncd,bhnjd->bhncj', k, k)
    a = jnp.where(strict, beta * kk * gamma, 0.0)
    rhs = jnp.concatenate([v * beta, k * beta * jnp.exp(g)[..., None]], axis=-1)
    sol = lax.linalg.triangular_solve(a, rhs, left_side=True, lower=True, unit_diagonal=True)
    u, w = sol[..., :dv], sol[..., dv:]
    qk = jnp.where(incl, jnp.einsum('bhncd,bhnjd->bhncj', q, k) * gamma, 0.0)
    g_last = g[..., -1]
    q_dec = q * jnp.exp(g)[..., None]
    k_dec = k * jnp.exp(g_last[..., None] - g)[..., None]

    def step(state, inp):
        q_i, k_i, u_i, w_i, qk_i, gl_i = inp
        v_new = u_i - jnp.einsum('bhck,bhkv->bhcv', w_i, state)
        o_i = jnp.einsum('bhck,bhkv->bhcv', q_i, state) + jnp.einsum('bhcj,bhjv->bhcv', qk_i, v_new)
        state = state * jnp.exp(gl_i)[..., None, None] + jnp.einsum('bhck,bhcv->bhkv', k_i, v_new)
        return state, o_i

    state0 = jnp.zeros((b, h, dk, dv), f32)
    xs = tuple(jnp.moveaxis(t, 2, 0) for t in (q_dec, k_dec, u, w, qk, g_last))
    _, o = lax.scan(step, state0, xs)
    return jnp.moveaxis(o, 0, 2).reshape(b, h, s, dv).astype(out_dtype)

def memory_cross_attention(h, mem_n, wq, wkv, wo):
    b, s, _ = h.shape
    m = mem_n.shape[1]
    q = (h @ wq).reshape(b, s, XA_HEADS, XA_HEAD_DIM)
    kv = (mem_n @ wkv).reshape(b, m, 2, XA_HEADS, XA_HEAD_DIM)
    k, v = kv[:, :, 0], kv[:, :, 1]
    scores = jnp.einsum('bshd,bmhd->bhsm', q, k).astype(jnp.float32) * XA_HEAD_DIM ** -0.5
    p = jax.nn.softmax(scores, axis=-1).astype(v.dtype)
    o = jnp.einsum('bhsm,bmhd->bshd', p, v).reshape(b, s, XA_WIDTH)
    return o @ wo

def hierarchical_route(h, w_grp, b_grp, w_exp, b_exp):
    t = h.shape[0]
    grp_logits = (h @ w_grp).astype(jnp.float32) + b_grp.astype(jnp.float32)
    p_grp = jax.nn.softmax(grp_logits, axis=-1)
    g_sel = jnp.argmax(grp_logits, axis=-1)
    p_g = jnp.take_along_axis(p_grp, g_sel[:, None], axis=-1)
    exp_logits = ((h @ w_exp).astype(jnp.float32) + b_exp.astype(jnp.float32)).reshape(t, N_GROUPS, EXPERTS_PER_GROUP)
    in_grp = jnp.take_along_axis(exp_logits, g_sel[:, None, None], axis=1)[:, 0]
    top_val, top_loc = lax.top_k(in_grp, TOP_K)
    wts = jax.nn.softmax(top_val, axis=-1) * p_g
    idx = g_sel[:, None] * EXPERTS_PER_GROUP + top_loc
    return idx, wts

def routed_experts(h, idx, wts, w_gate, w_up, w_down):
    t, d = h.shape
    n = t * TOP_K
    flat_e = idx.reshape(n)
    order = jnp.argsort(flat_e)
    e_sorted = flat_e[order]
    tok = order // TOP_K
    counts = jnp.bincount(flat_e, length=N_EXPERTS)
    padded = (counts + MOE_BLOCK - 1) // MOE_BLOCK * MOE_BLOCK
    p_end = jnp.cumsum(padded)
    p_start = p_end - padded
    start = jnp.cumsum(counts) - counts
    dest = p_start[e_sorted] + jnp.arange(n) - start[e_sorted]
    n_blocks = n // MOE_BLOCK + N_EXPERTS
    buf = jnp.zeros((n_blocks * MOE_BLOCK, d), h.dtype).at[dest].set(h[tok])
    block_start = jnp.arange(n_blocks) * MOE_BLOCK
    block_e = jnp.clip(jnp.searchsorted(p_end, block_start, side='right'), 0, N_EXPERTS - 1)

    def expert_block(args):
        xb, e = args
        return (jax.nn.silu(xb @ w_gate[e]) * (xb @ w_up[e])) @ w_down[e]

    yb = lax.map(expert_block, (buf.reshape(n_blocks, MOE_BLOCK, d), block_e))
    y_rows = yb.reshape(n_blocks * MOE_BLOCK, d)[dest]
    w_sorted = wts.reshape(n)[order].astype(h.dtype)
    return jnp.zeros((t, d), h.dtype).at[tok].add(y_rows * w_sorted[:, None])

def setup_inputs(seed: int = 0) -> dict:
    key = jax.random.key(seed)
    ks = jax.random.split(key, 24)
    L, D = DEPTH, D_MODEL

    def nrm(k, shape, scale):
        return jax.random.normal(k, shape, jnp.float32) * scale

    dt = jnp.exp(jax.random.uniform(ks[6], (L, DN_HEADS), jnp.float32, math.log(1e-3), math.log(1e-1)))
    return {
        "x": nrm(ks[0], (BATCH, SEQ, D), 1.0),
        "mem": nrm(ks[1], (BATCH, MEM_LEN, D), 1.0),
        "g_mix": 1.0 + nrm(ks[2], (L, D), 0.02),
        "w_in": nrm(ks[3], (L, D, IN_WIDTH), D ** -0.5),
        "dn_conv_w": nrm(ks[4], (L, DN_CONV, 3 * DN_WIDTH), DN_CONV ** -0.5),
        "dn_a_log": jnp.log(jax.random.uniform(ks[5], (L, DN_HEADS), jnp.float32, 1.0, 16.0)),
        "dn_dt_bias": dt + jnp.log(-jnp.expm1(-dt)),
        "dn_norm_g": 1.0 + nrm(ks[7], (L, DN_HEAD_DIM), 0.02),
        "w_out": nrm(ks[8], (L, MIX_WIDTH, D), MIX_WIDTH ** -0.5),
        "g_xattn": 1.0 + nrm(ks[9], (L, D), 0.02),
        "g_mem": 1.0 + nrm(ks[10], (L, D), 0.02),
        "xa_wq": nrm(ks[11], (L, D, XA_WIDTH), D ** -0.5),
        "xa_wkv": nrm(ks[12], (L, D, 2 * XA_WIDTH), D ** -0.5),
        "xa_wo": nrm(ks[13], (L, XA_WIDTH, D), XA_WIDTH ** -0.5),
        "g_ffn": 1.0 + nrm(ks[14], (L, D), 0.02),
        "w_grp": nrm(ks[15], (L, D, N_GROUPS), D ** -0.5),
        "b_grp": nrm(ks[16], (L, N_GROUPS), 0.01),
        "w_exp": nrm(ks[17], (L, D, N_EXPERTS), D ** -0.5),
        "b_exp": nrm(ks[18], (L, N_EXPERTS), 0.01),
        "we_gate": nrm(ks[19], (L, N_EXPERTS, D, D_EXPERT), D ** -0.5),
        "we_up": nrm(ks[20], (L, N_EXPERTS, D, D_EXPERT), D ** -0.5),
        "we_down": nrm(ks[21], (L, N_EXPERTS, D_EXPERT, D), D_EXPERT ** -0.5),
        "g_final": 1.0 + nrm(ks[22], (D,), 0.02),
    }

def reference(x, mem, g_mix, w_in, dn_conv_w, dn_a_log, dn_dt_bias, dn_norm_g, w_out,
              g_xattn, g_mem, xa_wq, xa_wkv, xa_wo, g_ffn, w_grp, b_grp, w_exp, b_exp,
              we_gate, we_up, we_down, g_final):
    b, s, d = x.shape
    offsets = np.cumsum(IN_SPLIT_SIZES)[:-1].tolist()
    for l in range(DEPTH):
        h = rmsnorm(x, g_mix[l])
        proj = h @ w_in[l]
        sb_qkv, dn_qkv, dn_b, dn_a, dn_z, gates = jnp.split(proj, offsets, axis=-1)

        sb = jnp.transpose(sb_qkv.reshape(b, s, 3, SB_HEADS, SB_HEAD_DIM), (2, 0, 3, 1, 4))
        o_sb = stick_breaking_attention(sb[0], sb[1], sb[2])
        o_sb = jnp.transpose(o_sb, (0, 2, 1, 3)).reshape(b, s, SB_WIDTH)

        dn_qkv = jax.nn.silu(causal_depthwise_conv(dn_qkv, dn_conv_w[l]))
        dn = jnp.transpose(dn_qkv.reshape(b, s, 3, DN_HEADS, DN_HEAD_DIM), (2, 0, 3, 1, 4))
        q_dn, k_dn, v_dn = l2norm(dn[0]), l2norm(dn[1]), dn[2]
        beta = jnp.transpose(jax.nn.sigmoid(dn_b.astype(jnp.float32)), (0, 2, 1))
        g_log = -jnp.exp(dn_a_log[l].astype(jnp.float32)) * jax.nn.softplus(
            dn_a.astype(jnp.float32) + dn_dt_bias[l].astype(jnp.float32))
        g_log = jnp.transpose(g_log, (0, 2, 1))
        o_dn = gated_delta_rule(q_dn, k_dn, v_dn, g_log, beta)
        o_dn = jnp.transpose(o_dn, (0, 2, 1, 3))
        z = dn_z.reshape(b, s, DN_HEADS, DN_HEAD_DIM)
        o_dn = (rmsnorm(o_dn, dn_norm_g[l]) * jax.nn.silu(z)).reshape(b, s, DN_WIDTH)

        gate = jax.nn.sigmoid(gates.reshape(b, s, N_BRANCHES, d))
        w_o = w_out[l]
        y = gate[:, :, 0] * (o_sb @ w_o[:SB_WIDTH]) + gate[:, :, 1] * (o_dn @ w_o[SB_WIDTH:])
        x = x + y

        x = x + memory_cross_attention(rmsnorm(x, g_xattn[l]), rmsnorm(mem, g_mem[l]),
                                       xa_wq[l], xa_wkv[l], xa_wo[l])

        hf = rmsnorm(x, g_ffn[l]).reshape(b * s, d)
        idx, wts = hierarchical_route(hf, w_grp[l], b_grp[l], w_exp[l], b_exp[l])
        x = x + routed_experts(hf, idx, wts, we_gate[l], we_up[l], we_down[l]).reshape(b, s, d)
    return rmsnorm(x, g_final)


_drawn_inputs = setup_inputs


def setup_inputs(seed=0):
    import zlib

    import numpy as np

    out = dict(_drawn_inputs(seed))
    spreads = {}
    factors = {'dn_norm_g': 4.136,
     'g_xattn': 4.712,
     'g_mem': 5.885,
     'b_grp': 46.4,
     'b_exp': 26.568,
     'g_final': 7.999,
     'g_ffn': 8.0}
    for name, (base, spread) in spreads.items():
        noise = np.random.default_rng([zlib.crc32(name.encode()), seed]).standard_normal(out[name].shape)
        drawn = base * np.exp(spread * noise) if base else spread * noise
        out[name] = __import__('jax').numpy.asarray(drawn.astype(out[name].dtype))
    for name, factor in factors.items():
        out[name] = (out[name] * factor).astype(out[name].dtype)
    return out
```

```python
import concourse.bass as bass
from concourse import mybir
from contextlib import ExitStack

F32 = mybir.dt.float32
F32R = mybir.dt.float32r
I32 = mybir.dt.int32
U32 = mybir.dt.uint32
ALU = mybir.AluOpType
ACT = mybir.ActivationFunctionType
AX = mybir.AxisListType
ds = bass.ds

P = 128
SEQ, D, MEM = 2048, 1024, 256
KD = D // P
BLK = 512
NBLK = SEQ // BLK
NT = SEQ // P
EPS = 1e-6
SB_HEADS, SB_DIM = 8, 64
DN_HEADS, DN_DIM, DN_CONV = 4, 128, 4
XA_HEADS, XA_DIM = 4, 64
N_GRP, PER_GRP, DE = 4, 8, 512
NE = N_GRP * PER_GRP
NR = N_GRP + NE
TOP_K = 2
MAX_MOE = SEQ * TOP_K // P + NE
NLEV = 7

G_DNQ, G_DNK, G_DNV, G_SBQ, G_SBK, G_SBV, G_Z, G_GA, G_GB, NGRP = 0, 4, 8, 12, 16, 20, 24, 28, 36, 44
C_DN = 3 * SB_HEADS * SB_DIM
C_BA = C_DN + 3 * DN_HEADS * DN_DIM
C_Z = C_BA + 2 * DN_HEADS
IN_W = C_Z + DN_HEADS * DN_DIM + 2 * D

K_ID, K_ONE, K_INC, K_EXC, K_LOW, K_NEG, K_IOTA, K_TOK, K_PAD, K_LEV = 0, 128, 256, 384, 512, 640, 768, 800, 832, 960
NCONST = K_LEV + 2 * NLEV * P
MASKED = -1.0e5


class Phase:

    def __init__(self, nc, name):
        self.nc, self.name, self.stack, self.sems = nc, name, ExitStack(), []

    def __enter__(self):
        return self

    def __exit__(self, *a):
        if self.sems and not a[0]:
            with self.nc.Block() as block:

                @block.gpsimd
                def _(pool):
                    ids = sorted(sem.num for sem in self.sems)
                    first = ids[0]
                    for at, after in zip(ids, ids[1:] + [None]):
                        if after != at + 1:
                            pool.sem_clear(range(first, at + 1))
                            first = after

        self.stack.close()

    def sb(self, name, shape, dt=F32):
        return self.stack.enter_context(self.nc.sbuf_tensor(f"{self.name}_{name}", shape, dt))

    def bank(self, name):
        return self.stack.enter_context(self.nc.psum_tensor(f"{self.name}_bank_{name}", [P, BLK], F32))

    def sem(self, name):
        sem = self.stack.enter_context(self.nc.semaphore(f"{self.name}_{name}"))
        self.sems.append(sem)
        return sem

    def pool_dma_sem(self, name):
        return self.nc.alloc_semaphore(f"{self.name}_{name}")


def bc(ap, n):
    return ap.unsqueeze(2).to_broadcast([ap.shape[0], ap.shape[1], n])


def bc_mid(ap, n):
    return ap.unsqueeze(1).to_broadcast([ap.shape[0], n, ap.shape[1]])


def quad(ap, n=P):
    return ap.rearrange("p (h f) -> p h f", f=n)


def phase_norm_x(nc, t, h_hi, h_lo):
    with Phase(nc, "A") as ph:
        TB = BLK // P
        x_in = [ph.sb(f"x{i}", [P, D]) for i in range(TB)]
        xT = [ph.sb(f"xT{i}", [P, KD, BLK]) for i in range(2)]
        sq = [ph.sb(f"sq{i}", [P, BLK]) for i in range(2)]
        h = [ph.sb(f"h{i}", [P, BLK]) for i in range(2)]
        lnr, rB, g = ph.sb("lnr", [P, BLK]), ph.sb("rB", [P, BLK]), ph.sb("g", [P, KD])
        pT = [ph.bank(f"pT{i}") for i in range(4)]
        pS = [ph.bank(f"pS{i}") for i in range(2)]
        const_in, g_in = ph.sem("const_in"), ph.sem("g_in")
        x_loaded = [ph.sem(f"x_loaded{i}") for i in range(TB)]
        xT_stored = [ph.pool_dma_sem(f"xT_stored{i}") for i in range(2)]
        trans, copied, squared, summed, ln_done, r_done, h_done, hi_done, lo_done = (
            ph.sem(s) for s in ("trans", "copied", "squared", "summed", "ln_done", "r_done", "h_done", "hi_done", "lo_done"))
        ident, ones = t["const"][:, K_ID:K_ID + P], t["const"][:, K_ONE:K_ONE + P]
        x_d = t["x"].rearrange("b (j p) d -> (b j) p d", p=P)
        xT_d = t["xT_d"].rearrange("k p (c n) -> c p k n", n=BLK)

        with nc.Block() as block:

            @block.sync
            def _(sp):
                sp.dma_start(x_in[0][:, :], x_d[0]).then_inc(x_loaded[0], 16)
                sp.dma_start(t["const"][:, :], t["const_d"]).then_inc(const_in, 16)
                for j in range(1, NT):
                    if j >= TB:
                        sp.wait_ge(trans, 2 * (j - TB + 1))
                    sp.dma_start(x_in[j % TB][:, :], x_d[j]).then_inc(x_loaded[j % TB], 16)
                    if j == 1:
                        sp.dma_start(g[:, :], t["g_mix"].rearrange("o (k p) -> p (o k)", p=P)).then_inc(g_in, 16)

            @block.tensor
            def _(pe):
                pe.wait_ge(const_in, 16)

                def transposes(b):
                    for j in range(TB * b, TB * b + TB):
                        pe.wait_ge(x_loaded[j % TB], 16 * (j // TB + 1))
                        for half in range(2):
                            n = 2 * j + half
                            if n >= 4:
                                pe.wait_ge(copied, n - 3)
                            for m in range(4):
                                k = 4 * half + m
                                last = nc.tensor.transpose(pT[n % 4][:, m * P:(m + 1) * P], x_in[j % TB][:, k * P:(k + 1) * P], ident)
                            last.then_inc(trans, 1)

                transposes(0)
                for b in range(NBLK):
                    if b + 1 < NBLK:
                        transposes(b + 1)
                    if b >= 2:
                        pe.wait_ge(ln_done, b - 1)
                    for k in range(KD):
                        pe.wait_ge(squared, KD * b + k + 1)
                        last = nc.tensor.matmul(pS[b % 2][:, :], ones, sq[k % 2][:, :], start=(k == 0), stop=(k == KD - 1))
                        last.then_inc(summed, 1)

            @block.scalar
            def _(act):
                for b in range(NBLK):
                    for k in range(KD):
                        n = KD * b + k
                        act.wait_ge(copied, KD * (b + 1))
                        if n >= 2:
                            act.wait_ge(summed, n - 1)
                        nc.scalar.activation(sq[k % 2][:, :], xT[b % 2][:, k, :], ACT.Square).then_inc(squared, 1)
                    act.wait_ge(summed, KD * (b + 1))
                    nc.scalar.activation(lnr[:, :], pS[b % 2][:, :], ACT.Ln, bias=t["eps"][:, 0:1],
                                         scale=1.0 / D).then_inc(ln_done, 1)
                    act.wait_ge(ln_done, b + 1)
                    act.wait_ge(h_done, KD * b)
                    nc.scalar.activation(rB[:, :], lnr[:, :], ACT.Exp, scale=-0.5).then_inc(r_done, 1)
                    for k in range(KD):
                        n = KD * b + k
                        act.wait_ge(h_done, n + 1)
                        nc.scalar.activation(h_hi[:, k, b * BLK:(b + 1) * BLK], h[n % 2][:, :], ACT.Copy).then_inc(hi_done, 1)

            @block.gpsimd
            def _(pool):
                for n in range(KD * NBLK):
                    b, k = divmod(n, KD)
                    part = slice(b * BLK, (b + 1) * BLK)
                    if k == 0:
                        pool.wait_ge(copied, KD * (b + 1))
                        pool.dma_start(xT_d[b], xT[b % 2][:, :, :]).then_inc(xT_stored[b % 2], 16)
                    pool.wait_ge(hi_done, n + 1)
                    nc.gpsimd.tensor_tensor(h_lo[:, k, part], h[n % 2][:, :], h_hi[:, k, part].bitcast(F32),
                                            ALU.subtract).then_inc(lo_done, 1)
                for i in range(2):
                    pool.wait_ge(xT_stored[i], 16 * NBLK // 2)

            @block.vector
            def _(dve):
                nc.vector.memset(t["eps"][:, :], EPS)

                def copies(b):
                    if b >= 2:
                        dve.wait_ge(xT_stored[b % 2], 16 * (b // 2))
                        dve.wait_ge(squared, KD * (b - 1))
                        dve.wait_ge(h_done, KD * (b - 1))
                    for j in range(TB):
                        for half in range(2):
                            n = 2 * (TB * b + j) + half
                            dve.wait_ge(trans, n + 1)
                            nc.vector.tensor_copy(xT[b % 2][:, 4 * half:4 * half + 4, j * P:(j + 1) * P],
                                                  quad(pT[n % 4][:, :])).then_inc(copied, 1)

                copies(0)
                dve.wait_ge(g_in, 16)
                for b in range(NBLK):
                    if b + 1 < NBLK:
                        copies(b + 1)
                    dve.wait_ge(r_done, b + 1)
                    for k in range(KD):
                        n = KD * b + k
                        if n >= 2:
                            dve.wait_ge(lo_done, n - 1)
                        nc.vector.scalar_tensor_tensor(h[n % 2][:, :], xT[b % 2][:, k, :], g[:, k:k + 1],
                                                       rB[:, :], ALU.mult, ALU.mult).then_inc(h_done, 1)


def phase_project(nc, t, h_hi, h_lo):
    with Phase(nc, "B") as ph:
        w = ph.sb("w", [P, KD, P])
        w_hi, w_lo = ([ph.sb(f"{n}{i}", [P, KD, P], F32R) for i in range(2)] for n in ("w_hi", "w_lo"))
        w_ba = ph.sb("w_ba", [P, KD, 2 * DN_HEADS])
        ba_hi, ba_lo = (ph.sb(n, [P, KD, 2 * DN_HEADS], F32R) for n in ("ba_hi", "ba_lo"))
        stage = [ph.sb(f"stage{i}", [P, SEQ]) for i in range(2)]
        PAD = DN_CONV
        raw = ph.sb("raw", [P, PAD + SEQ])
        conv = [ph.sb(f"conv{i}", [P, SEQ]) for i in range(2)]
        cw = ph.sb("cw", [P, 12, DN_CONV])
        alog = ph.sb("alog", [P, DN_HEADS])
        dtb = ph.sb("dtb", [P, DN_HEADS])
        cw_flat = cw[:, :, :].rearrange("p g j -> p (g j)")
        expA = ph.sb("expA", [P, DN_HEADS])
        a_in, a_pos, a_abs, e_abs, ln_e = (
            ph.sb(s, [P, NT, DN_HEADS]) for s in ("a_in", "a_pos", "a_abs", "e_abs", "ln_e"))
        acc = [[ph.bank(f"acc{i}{j}") for j in range(NBLK)] for i in range(2)]
        def per_slot(name):
            return [ph.sem(f"{name}{i}") for i in range(2)]

        mm_done, evac_done, staged, stored = (per_slot(s) for s in ("mm_done", "evac_done", "staged", "stored"))
        split_begun, w_loaded, w_hi_done, w_split, ba_split = (ph.sem(s) for s in ("split_begun", "w_loaded", "w_hi_done", "w_split", "ba_split"))
        conv_step, conv_done, silu_done, sq_done, ssq_done, ln_done, r_done = (
            per_slot(s) for s in ("conv_step", "conv_done", "silu_done", "sq_done", "ssq_done", "ln_done", "r_done"))
        padded, misc_in, ba_done, ba_act, ba_dve = (
            ph.sem(s) for s in ("padded", "misc_in", "ba_done", "ba_act", "ba_dve"))
        ones = t["const"][:, K_ONE:K_ONE + P]
        w_d = t["w_in"].rearrange("o (k p) n -> p (o k) n", p=P)
        proj_d = t["proj_d"]
        QK, V, SBG, Z, GT = "qk", "v", "copy", ACT.Silu, ACT.Sigmoid
        runs = [(QK, C_DN, 4), (V, C_DN + 8 * P, 2), (SBG, 0, 6), (Z, C_Z, 2), (GT, C_Z + 4 * P, 8)]
        before = [sum(r[2] for r in runs[:i]) for i in range(len(runs))]
        RUNS = [(*r, b) for r, b in zip(runs, before)]

        with nc.Block() as block:

            @block.sync
            def _(sp):
                sp.dma_start(w_ba[:, :, :], w_d[:, :, C_BA:C_Z]).then_inc(misc_in, 16)
                for g in range(12):
                    sp.dma_start(cw[:, g, :], t["dn_conv_w"][0, :, g * P:(g + 1) * P].rearrange("j p -> p j")).then_inc(misc_in, 16)
                sp.dma_start(alog[:, :], t["dn_a_log"].to_broadcast([P, DN_HEADS])).then_inc(misc_in, 16)
                sp.dma_start(dtb[:, :], t["dn_dt_bias"].to_broadcast([P, DN_HEADS])).then_inc(misc_in, 16)

                def store(turn, s):
                    sp.wait_ge(staged[s], turn * NBLK + NBLK)
                    sp.dma_start(proj_d[ds(turn * 2 + s, 1), :, :], stage[s][:, :]).then_inc(stored[s], 16)

                for kind, col, turns, at in RUNS:
                    first = 1 if at == 0 else 0
                    if first:
                        for s in range(2):
                            sp.wait_ge(w_split, s)
                            sp.dma_start(w[:, :, :], w_d[:, :, col + s * P:col + (s + 1) * P]).then_inc(w_loaded, 16)
                    with sp.Fori(first, turns) as i:
                        for s in range(2):
                            sp.wait_ge(w_split, i * 2 + (2 * at + s))
                            sp.dma_start(w[:, :, :], w_d[:, :, ds(i * (2 * P) + (col + s * P), P)]).then_inc(w_loaded, 16)
                        for s in range(2):
                            store(i + (at - 1), s)
                for s in range(2):
                    store(NGRP // 2 - 1, s)
                for s in range(2):
                    sp.wait_ge(stored[s], 16 * NGRP // 2)

            @block.gpsimd
            def _(pool):
                pool.wait_ge(misc_in, 240)
                nc.gpsimd.tensor_copy(ba_hi[:, :, :], w_ba[:, :, :]).then_inc(ba_split, 1)
                pool.wait_ge(ba_split, 1)
                nc.gpsimd.tensor_tensor(ba_lo[:, :, :], w_ba[:, :, :], ba_hi[:, :, :].bitcast(F32), ALU.subtract).then_inc(ba_split, 1)
                with pool.Fori(0, NGRP // 2) as i:
                    for s in range(2):
                        pool.wait_ge(w_loaded, i * 32 + 16 * (s + 1))
                        pool.wait_ge(mm_done[s], i)
                        pool.sem_inc(split_begun, 1)
                        nc.gpsimd.tensor_copy(w_hi[s][:, :, :], w[:, :, :]).then_inc(w_hi_done, 1)
                        pool.wait_ge(w_hi_done, i * 2 + (s + 1))
                        nc.gpsimd.tensor_tensor(w_lo[s][:, :, :], w[:, :, :], w_hi[s][:, :, :].bitcast(F32),
                                                ALU.subtract).then_inc(w_split, 1)

            @block.tensor
            def _(pe):
                pe.wait_ge(ba_split, 2)
                for j in range(NT):
                    for k in range(KD):
                        for n, (x, y) in enumerate(((h_hi, ba_hi), (h_hi, ba_lo), (h_lo, ba_hi))):
                            last = nc.tensor.matmul(acc[1][3][:, j * 8:(j + 1) * 8], x[:, k, j * P:(j + 1) * P], y[:, k, :],
                                                    start=(k == 0 and n == 0), stop=(k == KD - 1 and n == 2))
                last.then_inc(ba_done, 1)
                pe.wait_ge(ba_dve, 1)
                for kind, col, turns, at in RUNS:
                    with pe.Fori(0, turns) as i:
                        for s in range(2):
                            pe.wait_ge(w_split, i * 2 + (2 * at + s + 1))
                            pe.wait_ge((evac_done if kind in (QK, V) else staged)[s], i * NBLK + NBLK * at)
                            if kind == QK:
                                pe.wait_ge(ln_done[s], i * NBLK)
                            elif kind == V:
                                pe.wait_ge(ln_done[s], NBLK * at)
                            for k in range(KD):
                                for n, (x, y) in enumerate(((w_hi, h_hi), (w_hi, h_lo), (w_lo, h_hi))):
                                    for j in range(NBLK):
                                        last = nc.tensor.matmul(acc[s][j][:, :], x[s][:, k, :], y[:, k, j * BLK:(j + 1) * BLK],
                                                                start=(k == 0 and n == 0), stop=(k == KD - 1 and n == 2))
                            last.then_inc(mm_done[s], 1)
                        if kind == QK:
                            for s in range(2):
                                pe.wait_ge(evac_done[s], i * NBLK + NBLK)
                                for j in range(NBLK):
                                    pe.wait_ge(sq_done[s], i * NBLK + (j + 1))
                                    nc.tensor.matmul(acc[s][j][:, :], ones, stage[s][:, j * BLK:(j + 1) * BLK],
                                                     start=True, stop=True).then_inc(ssq_done[s], 1)

            @block.scalar
            def _(act):
                b_cols = quad(acc[1][3][:, 0:NT * 8], 8)[:, :, 0:DN_HEADS]
                act.wait_ge(ba_done, 1)
                nc.scalar.activation(t["beta"][:, :, :], b_cols, ACT.Sigmoid).then_inc(ba_act, 1)
                act.wait_ge(misc_in, 240)
                nc.scalar.activation(expA[:, :], alog[:, :], ACT.Exp).then_inc(ba_act, 1)
                act.wait_ge(ba_dve, 3)
                nc.scalar.activation(e_abs[:, :, :], a_abs[:, :, :], ACT.Exp, scale=-1.0).then_inc(ba_act, 1)
                act.wait_ge(ba_act, 3)
                nc.scalar.activation(ln_e[:, :, :], e_abs[:, :, :], ACT.Ln, bias=1.0).then_inc(ba_act, 1)
                act.wait_ge(padded, 1)
                for kind, col, turns, at in RUNS:
                    with act.Fori(0, turns) as i:
                        for s in range(2):
                            act.wait_ge(mm_done[s], i + (at + 1))
                            if kind in (QK, V):
                                act.wait_ge(conv_done[1 - s], i + (at + s))
                                for j in range(NBLK):
                                    nc.scalar.activation(raw[:, PAD + j * BLK:PAD + (j + 1) * BLK], acc[s][j][:, :],
                                                         ACT.Copy).then_inc(evac_done[s], 1)
                                act.wait_ge(conv_done[s], i + (at + 1))
                                act.wait_ge(stored[s], i * 16 + 16 * at)
                                for j in range(NBLK):
                                    part = slice(j * BLK, (j + 1) * BLK)
                                    if kind == V:
                                        nc.scalar.activation(stage[s][:, part], conv[s][:, part],
                                                             ACT.Silu).then_inc(staged[s], 1)
                                    else:
                                        nc.scalar.activation(conv[s][:, part], conv[s][:, part],
                                                             ACT.Silu).then_inc(silu_done[s], 1)
                                        act.wait_ge(silu_done[s], i * NBLK + (j + 1))
                                        nc.scalar.activation(stage[s][:, part], conv[s][:, part],
                                                             ACT.Square).then_inc(sq_done[s], 1)
                            else:
                                act.wait_ge(stored[s], i * 16 + 16 * at)
                                for j in range(NBLK):
                                    nc.scalar.activation(stage[s][:, j * BLK:(j + 1) * BLK], acc[s][j][:, :],
                                                         ACT.Copy if kind == SBG else kind).then_inc(staged[s], 1)
                        if kind == QK:
                            for s in range(2):
                                for j in range(NBLK):
                                    part = slice(j * BLK, (j + 1) * BLK)
                                    act.wait_ge(ssq_done[s], i * NBLK + (j + 1))
                                    nc.scalar.activation(stage[s][:, part], acc[s][j][:, :], ACT.Ln,
                                                         bias=t["eps"][:, 0:1]).then_inc(ln_done[s], 1)
                                for j in range(NBLK):
                                    part = slice(j * BLK, (j + 1) * BLK)
                                    act.wait_ge(ln_done[s], i * NBLK + (j + 1))
                                    nc.scalar.activation(stage[s][:, part], stage[s][:, part], ACT.Exp,
                                                         scale=-0.5).then_inc(r_done[s], 1)

            @block.vector
            def _(dve):
                nc.vector.memset(raw[:, 0:PAD], 0.0).then_inc(padded, 1)
                a_cols = quad(acc[1][3][:, 0:NT * 8], 8)[:, :, DN_HEADS:2 * DN_HEADS]
                dve.wait_ge(misc_in, 240)
                dve.wait_ge(ba_done, 1)
                dve.wait_ge(ba_act, 1)
                nc.vector.tensor_tensor(a_in[:, :, :], a_cols, bc_mid(dtb[:, :], NT), ALU.add).then_inc(ba_dve, 1)
                dve.wait_ge(ba_dve, 1)
                nc.vector.tensor_scalar(a_pos[:, :, :], a_in[:, :, :], 0.0, None, ALU.max).then_inc(ba_dve, 1)
                nc.vector.scalar_tensor_tensor(a_abs[:, :, :], a_in[:, :, :], -1.0, a_in[:, :, :], ALU.mult, ALU.max).then_inc(ba_dve, 1)
                dve.wait_ge(ba_act, 4)
                dve.wait_ge(ba_dve, 3)
                nc.vector.tensor_tensor(a_in[:, :, :], a_pos[:, :, :], ln_e[:, :, :], ALU.add).then_inc(ba_dve, 1)
                dve.wait_ge(ba_dve, 4)
                nc.vector.scalar_tensor_tensor(t["glog"][:, :, :], a_in[:, :, :], -1.0, bc_mid(expA[:, :], NT),
                                               ALU.mult, ALU.mult).then_inc(ba_dve, 1)
                for kind, col, turns, at in RUNS[0:2]:
                    with dve.Fori(0, turns) as i:
                        for s in range(2):
                            dve.wait_ge(evac_done[s], i * NBLK + NBLK * (at + 1))
                            dve.wait_ge(staged[s], i * NBLK + NBLK * at)
                            for j in range(DN_CONV):
                                src = raw[:, PAD - DN_CONV + 1 + j:PAD - DN_CONV + 1 + j + SEQ]
                                wj = cw_flat[:, ds(i * (2 * DN_CONV) + ((2 * at + s) * DN_CONV + j), 1)]
                                if j == 0:
                                    ins = nc.vector.tensor_scalar(conv[s][:, :], src, wj, None, ALU.mult)
                                else:
                                    dve.wait_ge(conv_step[s], i * 3 + (3 * at + j))
                                    ins = nc.vector.scalar_tensor_tensor(conv[s][:, :], src, wj, conv[s][:, :],
                                                                         ALU.mult, ALU.add)
                                ins.then_inc(conv_done[s] if j == DN_CONV - 1 else conv_step[s], 1)
                        if kind == QK:
                            for s in range(2):
                                for j in range(NBLK):
                                    part = slice(j * BLK, (j + 1) * BLK)
                                    dve.wait_ge(r_done[s], i * NBLK + (j + 1))
                                    nc.vector.tensor_tensor(stage[s][:, part], conv[s][:, part], stage[s][:, part],
                                                            ALU.mult).then_inc(staged[s], 1)


def phase_stick(nc, t):
    with Phase(nc, "C") as ph:
        qT, kT, vT = (ph.sb(s, [P, SEQ]) for s in ("qT", "kT", "vT"))
        vn = ph.sb("vn", [P, NT, P])
        oT = [ph.sb(f"oT{i}", [P, SEQ]) for i in range(1)]
        NZB, NRING = 4, 4
        keep = [ph.sb(f"keep{i}", [P, BLK]) for i in range(NRING)]
        sig = [ph.sb(f"sig{i}", [P, BLK]) for i in range(NRING)]
        prod = [ph.sb(f"prod{i}", [P, SEQ + 4]) for i in range(2)]
        att = [ph.sb(f"att{i}", [P, BLK]) for i in range(NRING)]
        attT = [ph.sb(f"attT{i}", [P, BLK]) for i in range(2)]
        bz = [ph.bank(f"z{i}") for i in range(NZB)]
        bt = [ph.bank(f"t{i}") for i in range(2)]
        bo = [ph.bank(f"o{i}") for i in range(2)]
        (qk_in, v_in, v_trans, v_copied, z_done, keep_done, sig_done, scan_done, att_done, trans_done,
         attT_done, av_done, o_copied, one_set) = (
            ph.sem(s) for s in ("qk_in", "v_in", "v_trans", "v_copied", "z_done", "keep_done", "sig_done",
                                "scan_done", "att_done", "trans_done", "attT_done", "av_done", "o_copied",
                                "one_set"))
        o_out = ph.pool_dma_sem("o_out")
        ident = t["const"][:, K_ID:K_ID + P]
        neg = t["const"][:, K_NEG:K_NEG + P]
        proj, o_d = t["proj_d"], t["o_d"]
        PAIRS = SB_HEADS // 2
        END = SEQ

        steps = []
        for h in range(2):
            for i in range(NT):
                n = (i + 1) * P
                starts = list(range(0, n, BLK))[::-1]
                for k0 in starts:
                    steps.append((h, i, k0, min(BLK, n - k0), k0 == starts[0], k0 == 0))
        NS = len(steps)
        NOQ = 2 * NT // 4
        NVT = NT // 4

        with nc.Block() as block:

            @block.sync
            def _(sp):
                with sp.Fori(0, PAIRS) as pair:
                    sp.wait_ge(z_done, pair * NS)
                    sp.dma_start(qT[:, :], proj[ds(pair + G_SBQ, 1), :, :]).then_inc(qk_in, 16)
                    sp.dma_start(kT[:, :], proj[ds(pair + G_SBK, 1), :, :]).then_inc(qk_in, 16)
                    sp.wait_ge(v_trans, pair * NVT)
                    sp.dma_start(vT[:, :], proj[ds(pair + G_SBV, 1), :, :]).then_inc(v_in, 16)

            @block.gpsimd
            def _(pool):
                with pool.Fori(0, PAIRS) as pair:
                    for n, (h, i, k0, w, first, last) in enumerate(steps):
                        off = END - (i + 1) * P + k0
                        pool.wait_ge(sig_done, pair * NS + (n + 1))
                        pool.wait_ge(scan_done, pair * NS + (n + 1))
                        pool.wait_ge(trans_done, pair * NS + (n + 1 - NRING)) if n >= NRING else \
                            pool.wait_ge(trans_done, pair * NS)
                        nc.gpsimd.tensor_tensor(att[n % NRING][:, 0:w], sig[n % NRING][:, 0:w],
                                                prod[i % 2][:, off + 1:off + 1 + w], ALU.mult).then_inc(att_done, 1)
                    pool.wait_ge(o_copied, pair * NOQ + NOQ)
                    pool.dma_start(o_d[ds(pair, 1), :, :], oT[0][:, :]).then_inc(o_out, 16)
                pool.wait_ge(o_out, 16 * PAIRS)

            @block.scalar
            def _(act):
                with act.Fori(0, PAIRS) as pair:
                    act.wait_ge(o_out, pair * 16)
                    for n in range(NS + 2):
                        if n < NS:
                            h, i, k0, w, first, last = steps[n]
                            act.wait_ge(z_done, pair * NS + (n + 1))
                            if n >= NRING:
                                act.wait_ge(scan_done, pair * NS + (n + 1 - NRING))
                                act.wait_ge(att_done, pair * NS + (n + 1 - NRING))
                            else:
                                act.wait_ge(att_done, pair * NS)
                            nc.scalar.activation(keep[n % NRING][:, 0:w], bz[n % NZB][:, 0:w], ACT.Sigmoid,
                                                 scale=-SB_DIM ** -0.5).then_inc(keep_done, 1)
                            nc.scalar.activation(sig[n % NRING][:, 0:w], bz[n % NZB][:, 0:w], ACT.Sigmoid,
                                                 scale=SB_DIM ** -0.5).then_inc(sig_done, 1)
                        if n >= 2 and steps[n - 2][5] and steps[n - 2][1] % 4 == 3:
                            h, i = steps[n - 2][:2]
                            q = (h * NT + i) // 4
                            rows = slice(h * SB_DIM, (h + 1) * SB_DIM)
                            act.wait_ge(av_done, pair * NS + (n - 1))
                            nc.scalar.activation(oT[0][rows, (i - 3) * P:(i + 1) * P], bo[q % 2][rows, :],
                                                 ACT.Copy).then_inc(o_copied, 1)

            @block.vector
            def _(dve):
                for j in range(2):
                    nc.vector.memset(prod[j][:, END:END + 1], 1.0).then_inc(one_set, 1)
                dve.wait_ge(one_set, 2)
                with dve.Fori(0, PAIRS) as pair:
                    for j in range(NVT):
                        dve.wait_ge(v_trans, pair * NVT + (j + 1))
                        nc.vector.tensor_copy(vn[:, 4 * j:4 * j + 4, :], quad(bt[j % 2][:, :])).then_inc(v_copied, 1)

                    def scan(n):
                        h, i, k0, w, first, last = steps[n]
                        off = END - (i + 1) * P + k0
                        dve.wait_ge(keep_done, pair * NS + (n + 1))
                        dve.wait_ge(scan_done, pair * NS + n)
                        if first:
                            m = next((m for m in range(n - 1, -1, -1) if steps[m][1] % 2 == i % 2 and steps[m][:2] != (h, i)), None)
                            dve.wait_ge(att_done, pair * NS + (0 if m is None else m + 1))
                        nc.vector.tensor_tensor_scan(prod[i % 2][:, off:off + w][:, ::-1], keep[n % NRING][:, 0:w][:, ::-1],
                                                     keep[n % NRING][:, 0:w][:, ::-1], prod[i % 2][:, off + w:off + w + 1],
                                                     ALU.mult, ALU.bypass).then_inc(scan_done, 1)

                    def copy(n):
                        w = steps[n][3]
                        dve.wait_ge(trans_done, pair * NS + (n + 1))
                        if n >= 2:
                            dve.wait_ge(av_done, pair * NS + (n - 1))
                        else:
                            dve.wait_ge(av_done, pair * NS)
                        nc.vector.tensor_copy(attT[n % 2][:, 0:w], bt[n % 2][:, 0:w]).then_inc(attT_done, 1)

                    for n in range(NS + 2):
                        if n < NS:
                            scan(n)
                        if n >= 2:
                            copy(n - 2)

            @block.tensor
            def _(pe):
                with pe.Fori(0, PAIRS) as pair:
                    pe.wait_ge(v_in, pair * 16 + 16)
                    for j in range(NVT):
                        if j < 2:
                            pe.wait_ge(attT_done, pair * NS)
                        else:
                            pe.wait_ge(v_copied, pair * NVT + (j - 1))
                        for m in range(4):
                            last = nc.tensor.transpose(bt[j % 2][:, m * P:(m + 1) * P],
                                                       vT[:, (4 * j + m) * P:(4 * j + m + 1) * P], ident)
                        last.then_inc(v_trans, 1)
                    pe.wait_ge(qk_in, pair * 32 + 32)

                    def scores(n):
                        h, i, k0, w, first, last = steps[n]
                        rows = slice(h * SB_DIM, (h + 1) * SB_DIM)
                        if n >= NZB:
                            pe.wait_ge(sig_done, pair * NS + (n + 1 - NZB))
                            pe.wait_ge(keep_done, pair * NS + (n + 1 - NZB))
                        ins = nc.tensor.matmul(bz[n % NZB][:, 0:w], qT[rows, i * P:(i + 1) * P], kT[rows, k0:k0 + w],
                                               start=True, stop=not first)
                        if first:
                            ins = nc.tensor.matmul(bz[n % NZB][:, w - P:w], ident, neg, start=False, stop=True)
                        ins.then_inc(z_done, 1)

                    def transposes(n):
                        w = steps[n][3]
                        pe.wait_ge(att_done, pair * NS + (n + 1))
                        if n >= 2:
                            pe.wait_ge(attT_done, pair * NS + (n - 1))
                        else:
                            pe.wait_ge(v_copied, pair * NVT + (NVT - 1 + n))
                        for m in range(w // P):
                            ins = nc.tensor.transpose(bt[n % 2][:, m * P:(m + 1) * P], att[n % NRING][:, m * P:(m + 1) * P], ident)
                        ins.then_inc(trans_done, 1)

                    def values(n):
                        h, i, k0, w, first, last = steps[n]
                        q = (h * NT + i) // 4
                        rows = slice(h * SB_DIM, (h + 1) * SB_DIM)
                        pe.wait_ge(attT_done, pair * NS + (n + 1))
                        if first and i % 4 == 0:
                            pe.wait_ge(o_copied, pair * NOQ + max(0, q - 1))
                        for m in range(w // P):
                            ins = nc.tensor.matmul(bo[q % 2][rows, (i % 4) * P:(i % 4 + 1) * P],
                                                   vn[:, k0 // P + m, h * SB_DIM:(h + 1) * SB_DIM],
                                                   attT[n % 2][:, m * P:(m + 1) * P],
                                                   start=first and m == 0, stop=last and m == w // P - 1)
                        ins.then_inc(av_done, 1)

                    AHEAD = 3
                    for n in range(AHEAD):
                        scores(n)
                    for n in range(NS + 1):
                        if n + AHEAD < NS:
                            scores(n + AHEAD)
                        if n < NS:
                            transposes(n)
                        if n >= 1:
                            values(n - 1)


def phase_delta(nc, t):
    with Phase(nc, "D") as ph:
        H, W = DN_HEADS, DN_HEADS * P
        SCALE = DN_DIM ** -0.5
        TURNS = NT // 2

        def two(name, shape=(P, W)):
            return [ph.sb(f"{name}{c}", list(shape)) for c in range(2)]

        qkvT, zT = two("qkvT", (P, 3 * W)), two("zT")
        glB, E, gN, gT, EG = two("glB"), two("E"), two("gN"), two("gT"), two("EG")
        A, AT, X, XT, Y = two("A"), two("AT"), two("X"), two("XT"), two("Y")
        ATm = [[ph.sb(f"ATm{c}{l}", [P, W]) for l in range(1, NLEV)] for c in range(2)]
        qkT, qd, kd, vb = two("qkT"), two("qd"), two("kd"), two("vb")
        rhs, vnew, S, Sdec, o_raw, o_sq, rB, o_out = (
            two(s) for s in ("rhs", "vnew", "S", "Sdec", "o_raw", "o_sq", "rB", "o_out"))
        gc, gl, eg, egl, kdec, be = (ph.sb(s, [P, NT * H]) for s in ("gc", "gl", "eg", "egl", "kdec", "be"))
        gdn = ph.sb("gdn", [P, 1])
        b = [[ph.bank(f"b{c}{j}") for j in range(4)] for c in range(2)]
        const = t["const"]
        ident, ones = const[:, K_ID:K_ID + P], const[:, K_ONE:K_ONE + P]
        inc, low = const[:, K_INC:K_INC + P], const[:, K_LOW:K_LOW + P]

        def lev(l, transposed):
            at = K_LEV + (2 * l + transposed) * P
            return const[:, at:at + P]

        glog, beta = (t[s][:, :, :].rearrange("p t h -> p (t h)") for s in ("glog", "beta"))
        proj = t["proj_d"].rearrange("g p n -> p g n")
        o_d = t["o_d"].rearrange("g p n -> p g n")
        in_ = [ph.sem(f"in{c}") for c in range(2)]
        stored = [ph.pool_dma_sem(f"stored{c}") for c in range(2)]
        names = ("gdn_in", "g_sum", "g_copied", "g_exp", "g_dec", "s_zero", "glB_ok", "GR_ok", "E_ok", "EG_ok", "Emm_ok", "gNe_ok",
                 "gTe_ok", "gNl_ok", "gN_ok", "gT_ok", "KK_ok", "KQ_ok", "Tk_ok", "Tv_ok", "A_ok", "qkT_ok", "qd_ok", "kd_ok",
                 "vb_ok", "TA_ok", "AT_ok", "ATm_ok", "Xm_ok", "X_ok", "Y_mm", "Y_ok", "P2_mm", "P3_mm", "lev_ok",
                 "R_mm", "Rb_ok", "rhs_ok", "vn_mm", "vn_ok", "Sdec_ok", "dS_mm", "S_ok", "O_mm", "o_ok", "osq_ok",
                 "oss_mm", "oln_ok", "or_ok", "on_ok", "o_done")
        s = {n: ph.sem(n) for n in names}
        L = NLEV - 1

        def heads(c, j, lhs, rhs_of, **kw):
            for h in range(H):
                last = nc.tensor.matmul(b[c][j][:, h * P:(h + 1) * P], lhs(h), rhs_of(h), start=True, stop=True)
            return last

        def hs(tile, h, at=0):
            return tile[:, at + h * P:at + (h + 1) * P]

        with nc.Block() as block:

            @block.sync
            def _(sp):
                sp.dma_start(gdn[:, :], t["dn_norm_g"].rearrange("o p -> p o")).then_inc(s["gdn_in"], 16)
                with sp.Fori(0, TURNS) as i:
                    for c in range(2):
                        sp.wait_ge(s["R_mm"], i * 2)
                        sp.wait_ge(s["o_done"], i * 2)
                        cols = ds(i * (2 * P) + c * P, P)
                        sp.dma_start(quad(qkvT[c][:, :]), proj[:, G_DNQ:G_DNQ + 12, cols]).then_inc(in_[c], 16)
                        sp.dma_start(quad(zT[c][:, :]), proj[:, G_Z:G_Z + H, cols]).then_inc(in_[c], 16)

            @block.tensor
            def _(pe):
                nc.tensor.matmul(b[0][0][:, 0:NT * H], inc, glog, start=True, stop=True)
                nc.tensor.matmul(b[0][0][:, NT * H:2 * NT * H], ones, glog, start=True, stop=True).then_inc(s["g_sum"], 1)
                pe.wait_ge(s["g_copied"], 2)
                with pe.Fori(0, TURNS) as i:
                    n = [i * 2 + 1, i * 2 + 2]
                    for c in range(2):
                        qT = lambda h, c=c: hs(qkvT[c], h)
                        kT = lambda h, c=c: hs(qkvT[c], h, W)
                        vT = lambda h, c=c: hs(qkvT[c], h, 2 * W)
                        pe.wait_ge(s["glB_ok"], n[c])
                        pe.wait_ge(s["oln_ok"], i * 2 + 0)
                        heads(c, 0, lambda h: hs(glB[c], h), lambda h: inc).then_inc(s["GR_ok"], 1)
                        pe.wait_ge(in_[c], i * 32 + 32)
                        pe.wait_ge(s["vn_ok"], i * 2)
                        heads(c, 1, kT, kT).then_inc(s["KK_ok"], 1)
                        pe.wait_ge(s["S_ok"], i * 2 + 1)
                        heads(c, 2, kT, qT).then_inc(s["KQ_ok"], 1)
                        pe.wait_ge(s["o_ok"], i * 2)
                        for h in range(H):
                            last = nc.tensor.transpose(hs(b[c][3], h), kT(h), ident)
                        last.then_inc(s["Tk_ok"], 1)
                        pe.wait_ge(s["E_ok"], n[c])
                        pe.wait_ge(s["EG_ok"], n[c])
                        for h in range(H):
                            last = nc.tensor.transpose(hs(b[c][0], h), vT(h), ident)
                        last.then_inc(s["Tv_ok"], 1)
                    for c in range(2):
                        pe.wait_ge(s["A_ok"], n[c])
                        for h in range(H):
                            last = nc.tensor.transpose(hs(b[c][1], h), hs(A[c], h), ident)
                        last.then_inc(s["TA_ok"], 1)
                    for l in range(1, NLEV):
                        for c in range(2):
                            pe.wait_ge(s["ATm_ok"], i * (2 * L) + c * L + l)
                            if l == 1:
                                pe.wait_ge(s["X_ok"], i * 4 + 2 * c + 2)
                                pe.wait_ge(s["qkT_ok"], n[c])
                            else:
                                pe.wait_ge(s["lev_ok"], i * (4 * L - 2) + 4 * (l - 2) + 2 * c + 2)
                            heads(c, 2, lambda h: hs(ATm[c][l - 1], h), lambda h: hs(X[c], h)).then_inc(s["Y_mm"], 1)
                        for c in range(2):
                            pe.wait_ge(s["Y_ok"], i * (2 * L) + 2 * (l - 1) + c + 1)
                            if l == 1:
                                pe.wait_ge(s["kd_ok"], n[c])
                                pe.wait_ge(s["AT_ok"], n[c])
                            if l < NLEV - 1:
                                heads(c, 3, lambda h: hs(XT[c], h), lambda h: hs(Y[c], h)).then_inc(s["P2_mm"], 1)
                            heads(c, 1, lambda h: hs(Y[c], h), lambda h: hs(XT[c], h)).then_inc(s["P3_mm"], 1)
                    for c in range(2):
                        pe.wait_ge(s["S_ok"], i * 2 + c + 1)
                        if c == 0:
                            pe.wait_ge(s["vb_ok"], i * 2 + 2)
                        heads(c, 0, lambda h: hs(qkvT[c], h, W), lambda h: hs(S[c], h)).then_inc(s["R_mm"], 1)
                        pe.wait_ge(s["rhs_ok"], n[c])
                        pe.wait_ge(s["lev_ok"], i * (4 * L - 2) + (4 * L - 4) + c + 1)
                        heads(c, 1, lambda h: hs(XT[c], h), lambda h: hs(rhs[c], h)).then_inc(s["vn_mm"], 1)
                        pe.wait_ge(s["vn_ok"], n[c])
                        heads(c, 2, lambda h: hs(kd[c], h), lambda h: hs(vnew[c], h)).then_inc(s["dS_mm"], 1)
                        for h in range(H):
                            nc.tensor.matmul(hs(b[c][3], h), hs(S[c], h), hs(qd[c], h), start=True, stop=False)
                            last = nc.tensor.matmul(hs(b[c][3], h), hs(vnew[c], h), hs(qkT[c], h), start=False, stop=True)
                        last.then_inc(s["O_mm"], 1)
                    for c in range(2):
                        pe.wait_ge(s["osq_ok"], n[c])
                        nc.tensor.matmul(b[c][0][:, :], ones, o_sq[c][:, :], start=True, stop=True).then_inc(s["oss_mm"], 1)

            @block.scalar
            def _(act):
                act.wait_ge(s["g_copied"], 2)
                nc.scalar.activation(eg[:, :], gc[:, :], ACT.Exp).then_inc(s["g_exp"], 1)
                nc.scalar.activation(egl[:, :], gl[:, :], ACT.Exp).then_inc(s["g_exp"], 1)
                act.wait_ge(s["g_dec"], 1)
                nc.scalar.activation(kdec[:, :], kdec[:, :], ACT.Exp).then_inc(s["g_exp"], 1)
                with act.Fori(0, TURNS) as i:
                    n = [i * 2 + 1, i * 2 + 2]
                    for c in range(2):
                        act.wait_ge(s["E_ok"], n[c])
                        act.wait_ge(s["qd_ok"], i * 2)
                        nc.scalar.activation(EG[c][:, :], b[c][0][:, :], ACT.Exp).then_inc(s["EG_ok"], 1)
                        act.wait_ge(s["Emm_ok"], i * 4 + 2 * c + 2)
                        nc.scalar.activation(gN[c][:, :], gN[c][:, :], ACT.Exp, scale=-1.0).then_inc(s["gNe_ok"], 1)
                        nc.scalar.activation(gT[c][:, :], gT[c][:, :], ACT.Exp).then_inc(s["gTe_ok"], 1)
                    for l in range(1, NLEV):
                        for c in range(2):
                            act.wait_ge(s["Y_mm"], i * (2 * L) + 2 * (l - 1) + c + 1)
                            if l > 1:
                                act.wait_ge(s["P3_mm"], i * (2 * L) + 2 * (l - 2) + c + 1)
                            else:
                                act.wait_ge(s["P3_mm"], i * (2 * L))
                            nc.scalar.activation(Y[c][:, :], b[c][2][:, :], ACT.Copy).then_inc(s["Y_ok"], 1)
                    for c in range(2):
                        act.wait_ge(s["vn_mm"], n[c])
                        nc.scalar.activation(vnew[c][:, :], b[c][1][:, :], ACT.Copy).then_inc(s["vn_ok"], 1)
                        act.wait_ge(s["O_mm"], n[c])
                        act.wait_ge(s["on_ok"], i * 2)
                        nc.scalar.activation(o_raw[c][:, :], b[c][3][:, :], ACT.Copy).then_inc(s["o_ok"], 1)
                        act.wait_ge(s["o_ok"], n[c])
                        nc.scalar.activation(o_sq[c][:, :], o_raw[c][:, :], ACT.Square).then_inc(s["osq_ok"], 1)
                    for c in range(2):
                        act.wait_ge(s["oss_mm"], n[c])
                        nc.scalar.activation(rB[c][:, :], b[c][0][:, :], ACT.Ln, bias=t["eps"][:, 0:1],
                                             scale=1.0 / DN_DIM).then_inc(s["oln_ok"], 1)
                        act.wait_ge(s["oln_ok"], n[c])
                        nc.scalar.activation(rB[c][:, :], rB[c][:, :], ACT.Exp, scale=-0.5).then_inc(s["or_ok"], 1)

            @block.gpsimd
            def _(pool):
                nc.gpsimd.memset(S[0][:, :], 0.0).then_inc(s["S_ok"], 1)
                with pool.Fori(0, TURNS) as i:
                    n = [i * 2 + 1, i * 2 + 2]

                    def cols(ap, c):
                        return ap[:, ds(i * (2 * H) + c * H, H)]

                    for c in range(2):
                        pool.wait_ge(s["GR_ok"], i * 2)
                        nc.gpsimd.tensor_copy(quad(glB[c][:, :]), bc(cols(glog, c), P)).then_inc(s["glB_ok"], 1)
                    for c in range(2):
                        pool.wait_ge(s["gNe_ok"], n[c])
                        nc.gpsimd.tensor_tensor(quad(gN[c][:, :]), quad(gN[c][:, :]), bc_mid(low, H), ALU.mult).then_inc(s["gNl_ok"], 1)
                        pool.wait_ge(s["gTe_ok"], n[c])
                        nc.gpsimd.tensor_tensor(quad(gT[c][:, :]), quad(gT[c][:, :]), bc_mid(inc, H), ALU.mult).then_inc(s["gT_ok"], 1)
                        pool.wait_ge(s["gNl_ok"], n[c])
                        nc.gpsimd.tensor_tensor(quad(gN[c][:, :]), quad(gN[c][:, :]), bc(cols(beta, c), P), ALU.mult).then_inc(s["gN_ok"], 1)
                    for c in range(2):
                        pool.wait_ge(s["AT_ok"], n[c])
                        for l in range(1, NLEV):
                            nc.gpsimd.tensor_tensor(quad(ATm[c][l - 1][:, :]), quad(AT[c][:, :]), bc_mid(lev(l, 1), H),
                                                    ALU.mult).then_inc(s["ATm_ok"], 1)
                    for c in range(2):
                        if c == 0:
                            pool.wait_ge(s["g_exp"], 3)
                            pool.wait_ge(s["S_ok"], i * 2 + 1)
                        else:
                            pool.wait_ge(s["S_ok"], i * 2 + 2)
                        nc.gpsimd.tensor_tensor(quad(Sdec[c][:, :]), quad(S[c][:, :]), bc(cols(egl, c), P), ALU.mult).then_inc(s["Sdec_ok"], 1)
                    for c in range(2):
                        pool.wait_ge(s["on_ok"], n[c])
                        pool.wait_ge(stored[c], i * 16)
                        nc.gpsimd.tensor_tensor(o_out[c][:, :], o_out[c][:, :], zT[c][:, :], ALU.mult).then_inc(s["o_done"], 1)
                    for c in range(2):
                        pool.wait_ge(s["o_done"], n[c])
                        pool.dma_start(o_d[:, H:2 * H, ds(i * (2 * P) + c * P, P)], quad(o_out[c][:, :])).then_inc(stored[c], 16)
                for c in range(2):
                    pool.wait_ge(stored[c], 16 * TURNS)

            @block.vector
            def _(dve):
                dve.wait_ge(s["g_sum"], 1)
                nc.vector.tensor_copy(gc[:, :], b[0][0][:, 0:NT * H]).then_inc(s["g_copied"], 1)
                nc.vector.tensor_copy(gl[:, :], b[0][0][:, NT * H:2 * NT * H]).then_inc(s["g_copied"], 1)
                dve.wait_ge(s["g_copied"], 2)
                nc.vector.tensor_tensor(kdec[:, :], gl[:, :], gc[:, :], ALU.subtract).then_inc(s["g_dec"], 1)
                dve.wait_ge(s["g_exp"], 3)
                nc.vector.tensor_tensor(be[:, :], beta, eg[:, :], ALU.mult).then_inc(s["g_dec"], 1)
                dve.wait_ge(s["g_dec"], 2)
                dve.wait_ge(s["gdn_in"], 16)
                with dve.Fori(0, TURNS) as i:
                    n = [i * 2 + 1, i * 2 + 2]

                    def cols(ap, c):
                        return bc(ap[:, ds(i * (2 * H) + c * H, H)], P)

                    for c in range(2):
                        dve.wait_ge(s["GR_ok"], n[c])
                        nc.vector.tensor_tensor(quad(E[c][:, :]), quad(b[c][0][:, :]), cols(gc, c), ALU.subtract).then_inc(s["E_ok"], 1)
                        dve.wait_ge(s["E_ok"], n[c])
                        nc.vector.tensor_scalar(gN[c][:, :], E[c][:, :], 0.0, None, ALU.max).then_inc(s["Emm_ok"], 1)
                        nc.vector.tensor_scalar(gT[c][:, :], E[c][:, :], 0.0, None, ALU.min).then_inc(s["Emm_ok"], 1)
                    for c in range(2):
                        dve.wait_ge(s["KK_ok"], n[c])
                        dve.wait_ge(s["gN_ok"], n[c])
                        nc.vector.tensor_tensor(A[c][:, :], b[c][1][:, :], gN[c][:, :], ALU.mult).then_inc(s["A_ok"], 1)
                    for c in range(2):
                        dve.wait_ge(s["TA_ok"], n[c])
                        nc.vector.tensor_copy(AT[c][:, :], b[c][1][:, :]).then_inc(s["AT_ok"], 1)
                        dve.wait_ge(s["AT_ok"], n[c])
                        nc.vector.tensor_tensor(quad(XT[c][:, :]), quad(AT[c][:, :]), bc_mid(lev(0, 1), H), ALU.mult).then_inc(s["Xm_ok"], 1)
                        nc.vector.tensor_tensor(quad(X[c][:, :]), quad(A[c][:, :]), bc_mid(lev(0, 0), H), ALU.mult).then_inc(s["Xm_ok"], 1)
                        dve.wait_ge(s["Xm_ok"], i * 4 + 2 * c + 2)
                        for y in (XT, X):
                            nc.vector.tensor_tensor(quad(y[c][:, :]), bc_mid(ident, H), quad(y[c][:, :]), ALU.subtract).then_inc(s["X_ok"], 1)
                    for c in range(2):
                        dve.wait_ge(s["KQ_ok"], n[c])
                        dve.wait_ge(s["gT_ok"], n[c])
                        nc.vector.scalar_tensor_tensor(qkT[c][:, :], b[c][2][:, :], SCALE, gT[c][:, :], ALU.mult, ALU.mult).then_inc(s["qkT_ok"], 1)
                        dve.wait_ge(s["EG_ok"], n[c])
                        nc.vector.scalar_tensor_tensor(qd[c][:, :], qkvT[c][:, 0:W], SCALE, EG[c][:, :], ALU.mult, ALU.mult).then_inc(s["qd_ok"], 1)
                        dve.wait_ge(s["Tk_ok"], n[c])
                        nc.vector.tensor_tensor(quad(kd[c][:, :]), quad(b[c][3][:, :]), cols(kdec, c), ALU.mult).then_inc(s["kd_ok"], 1)
                        dve.wait_ge(s["Tv_ok"], n[c])
                        nc.vector.tensor_tensor(quad(vb[c][:, :]), quad(b[c][0][:, :]), cols(beta, c), ALU.mult).then_inc(s["vb_ok"], 1)
                    for l in range(1, NLEV):
                        for c in range(2):
                            if l < NLEV - 1:
                                dve.wait_ge(s["P3_mm"], i * (2 * L) + 2 * (l - 1) + c + 1)
                                dve.wait_ge(s["P2_mm"], i * (2 * L - 2) + 2 * (l - 1) + c + 1)
                                nc.vector.tensor_tensor(X[c][:, :], X[c][:, :], b[c][3][:, :], ALU.subtract).then_inc(s["lev_ok"], 1)
                            else:
                                dve.wait_ge(s["P3_mm"], i * (2 * L) + 2 * (l - 1) + c + 1)
                            nc.vector.tensor_tensor(XT[c][:, :], XT[c][:, :], b[c][1][:, :], ALU.subtract).then_inc(s["lev_ok"], 1)
                    for c in range(2):
                        dve.wait_ge(s["R_mm"], n[c])
                        nc.vector.tensor_tensor(quad(rhs[c][:, :]), quad(b[c][0][:, :]), cols(be, c), ALU.mult).then_inc(s["Rb_ok"], 1)
                        dve.wait_ge(s["Rb_ok"], n[c])
                        nc.vector.tensor_tensor(rhs[c][:, :], vb[c][:, :], rhs[c][:, :], ALU.subtract).then_inc(s["rhs_ok"], 1)
                        dve.wait_ge(s["dS_mm"], n[c])
                        dve.wait_ge(s["Sdec_ok"], n[c])
                        if c == 1:
                            dve.wait_ge(s["O_mm"], i * 2 + 1)
                        else:
                            dve.wait_ge(s["O_mm"], i * 2)
                        nc.vector.tensor_tensor(S[1 - c][:, :], Sdec[c][:, :], b[c][2][:, :], ALU.add).then_inc(s["S_ok"], 1)
                    for c in range(2):
                        dve.wait_ge(s["or_ok"], n[c])
                        dve.wait_ge(stored[c], i * 16)
                        nc.vector.scalar_tensor_tensor(o_out[c][:, :], o_raw[c][:, :], gdn[:, 0:1], rB[c][:, :],
                                                       ALU.mult, ALU.mult).then_inc(s["on_ok"], 1)


def phase_merge(nc, t):
    with Phase(nc, "E") as ph:
        HM = KD // 2
        XW = XA_HEADS * XA_DIM
        XC = XW // P
        MC = MEM // P
        TB = BLK // P
        w_out, wq = ph.sb("w_out", [P, KD, D]), ph.sb("wq", [P, KD, XW])
        wo, w_r = ph.sb("wo", [P, XC, D]), ph.sb("w_r", [P, KD, NR])
        bias_r = ph.sb("bias_r", [P, NR])
        gx, gm, gf = (ph.sb(s, [P, KD]) for s in ("gx", "gm", "gf"))
        oT_in, gates = ph.sb("oT_in", [P, KD, BLK]), ph.sb("gates", [P, 2 * KD, BLK])
        xT, sq, hT = (ph.sb(s, [P, KD, BLK]) for s in ("xT", "sq", "hT"))
        lnr, rB = ph.sb("lnr", [P, BLK]), ph.sb("rB", [P, BLK])
        qT, kT, vm = ph.sb("qT", [P, XC, BLK]), ph.sb("kT", [P, XC, MEM]), ph.sb("vm", [P, MC, XW])
        p = [ph.sb(f"p{i}", [P, TB, MEM]) for i in range(2)]
        pT = [ph.sb(f"pT{i}", [P, MC, BLK]) for i in range(2)]
        aT = ph.sb("aT", [P, XC, BLK])
        mx, nmx, ssum, rsum = (ph.sb(s, [P, XA_HEADS, TB]) for s in ("mx", "nmx", "ssum", "rsum"))
        x2n = [ph.sb(f"x2n{i}", [P, D]) for i in range(2)]
        mss, mr = ph.sb("mss", [P, MC]), ph.sb("mr", [P, MC])
        b = [ph.bank(f"b{i}") for i in range(8)]
        wkv = gates[:, 0:KD, :]
        mem_n = oT_in[:, 0:2 * MC, :].rearrange("p (c a) n -> p c (a n)", c=MC)
        memT = hT[:, :, 0:MEM]
        mem_sq = sq[:, 0:2 * MC, :].rearrange("p (c a) n -> p c (a n)", c=MC)
        const = t["const"]
        ident, ones = const[:, K_ID:K_ID + P], const[:, K_ONE:K_ONE + P]
        names = ("w_in", "mem_in", "wkv_in", "o_in", "g_in", "x_in", "m_sq", "m_ln", "m_r", "m_n", "m_T", "m_Tc",
                 "m_k", "m_kc", "m_v", "m_vc", "ab_mm", "a_g", "b_g", "ab", "x_add", "sq1", "ss1", "ln1", "r1", "h1",
                 "q_mm", "q_ok", "s_mm", "mx_ok", "nmx_ok", "exp_ok", "rs_ok", "p_ok", "pT_mm", "pT_ok", "pv_mm",
                 "aT_ok", "wo_mm", "x_add2", "sq2", "ss2", "ln2", "r2", "h2", "nat_mm", "nat_ok", "lg_mm", "lg_ok")
        s = {n: ph.sem(n) for n in names}
        x2_out = [ph.pool_dma_sem(f"x2_out{i}") for i in range(2)]
        o_d = t["o_d"].rearrange("g p n -> p g n")
        proj = t["proj_d"].rearrange("g p n -> p g n")
        xT_d = t["xT_d"].rearrange("g p n -> p g n")
        x2_d = t["x2_d"].rearrange("(j p) d -> j p d", p=P)
        cols_of = lambda w: w.rearrange("o (k p) n -> p (o k) n", p=P)

        with nc.Block() as block:

            @block.sync
            def _(sp):
                sp.dma_start(mem_n, t["mem"].rearrange("o (c p) d -> p (o c) d", p=P)).then_inc(s["mem_in"], 16)
                sp.dma_start(wkv, cols_of(t["xa_wkv"])).then_inc(s["wkv_in"], 16)
                weights = [(w_out[:, :, :], cols_of(t["w_out"])), (wq[:, :, :], cols_of(t["xa_wq"])),
                           (wo[:, :, :], cols_of(t["xa_wo"])), (w_r[:, :, 0:N_GRP], cols_of(t["w_grp"])),
                           (w_r[:, :, N_GRP:NR], cols_of(t["w_exp"])),
                           (bias_r[:, 0:N_GRP], t["b_grp"].to_broadcast([P, N_GRP])),
                           (bias_r[:, N_GRP:NR], t["b_exp"].to_broadcast([P, NE])),
                           (gx[:, :], t["g_xattn"].rearrange("o (k p) -> p (o k)", p=P)),
                           (gm[:, :], t["g_mem"].rearrange("o (k p) -> p (o k)", p=P)),
                           (gf[:, :], t["g_ffn"].rearrange("o (k p) -> p (o k)", p=P))]
                for dst, src in weights:
                    sp.dma_start(dst, src).then_inc(s["w_in"], 16)
                sp.wait_ge(s["m_n"], MC)
                sp.wait_ge(s["m_v"], 1)
                sp.wait_ge(s["m_T"], KD)
                with sp.Fori(0, NBLK) as i:
                    blk = ds(i * BLK, BLK)
                    sp.wait_ge(s["ab_mm"], i * (2 * KD))
                    sp.dma_start(oT_in[:, :, :], o_d[:, :, blk]).then_inc(s["o_in"], 16)
                    sp.wait_ge(s["x_add"], i * KD)
                    sp.dma_start(gates[:, :, :], proj[:, G_GA:G_GA + 2 * KD, blk]).then_inc(s["g_in"], 16)
                    sp.wait_ge(s["nat_mm"], i * (2 * TB))
                    sp.wait_ge(s["h2"], i * KD)
                    sp.dma_start(xT[:, :, :], xT_d[:, :, blk]).then_inc(s["x_in"], 16)

            @block.tensor
            def _(pe):
                for k in range(KD):
                    pe.wait_ge(s["m_n"], MC)
                    if k >= 2:
                        pe.wait_ge(s["m_Tc"], k - 1)
                    for c in range(MC):
                        last = nc.tensor.transpose(b[k % 2][:, c * P:(c + 1) * P], mem_n[:, c, k * P:(k + 1) * P], ident)
                    last.then_inc(s["m_T"], 1)
                pe.wait_ge(s["m_Tc"], KD)
                pe.wait_ge(s["wkv_in"], 16)
                for c in range(XC):
                    for k in range(KD):
                        last = nc.tensor.matmul(b[2][:, c * MEM:(c + 1) * MEM], wkv[:, k, c * P:(c + 1) * P], memT[:, k, :],
                                                start=(k == 0), stop=(k == KD - 1))
                last.then_inc(s["m_k"], 1)
                for c in range(MC):
                    for k in range(KD):
                        last = nc.tensor.matmul(b[3][:, c * XW:(c + 1) * XW], memT[:, k, c * P:(c + 1) * P], wkv[:, k, XW:2 * XW],
                                                start=(k == 0), stop=(k == KD - 1))
                last.then_inc(s["m_v"], 1)
                pe.wait_ge(s["m_kc"], 1)
                pe.wait_ge(s["m_vc"], 1)
                pe.wait_ge(s["w_in"], 160)
                with pe.Fori(0, NBLK) as i:
                    pe.wait_ge(s["o_in"], i * 16 + 16)
                    pe.wait_ge(s["nat_ok"], i * (2 * TB))
                    for m in range(KD):
                        for br in range(2):
                            if m >= 2:
                                pe.wait_ge(s["b_g" if br else "a_g"], i * KD + (m - 1))
                            for k in range(HM):
                                last = nc.tensor.matmul(b[2 * (m % 2) + br][:, :], w_out[:, br * HM + k, m * P:(m + 1) * P],
                                                        oT_in[:, br * HM + k, :], start=(k == 0), stop=(k == HM - 1))
                            last.then_inc(s["ab_mm"], 1)
                    for k in range(KD):
                        pe.wait_ge(s["sq1"], i * KD + (k + 1))
                        last = nc.tensor.matmul(b[4][:, :], ones, sq[:, k, :], start=(k == 0), stop=(k == KD - 1))
                    last.then_inc(s["ss1"], 1)
                    pe.wait_ge(s["h1"], i * KD + KD)
                    pe.wait_ge(s["lg_ok"], i)
                    for c in range(XC):
                        for k in range(KD):
                            last = nc.tensor.matmul(b[5 + c][:, :], wq[:, k, c * P:(c + 1) * P], hT[:, k, :],
                                                    start=(k == 0), stop=(k == KD - 1))
                        last.then_inc(s["q_mm"], 1)
                    pe.wait_ge(s["q_ok"], i * XC + XC)

                    def scores(h):
                        rows = slice((h % 2) * XA_DIM, (h % 2 + 1) * XA_DIM)
                        if h >= 2:
                            pe.wait_ge(s["exp_ok"], i * (XA_HEADS * TB) + TB * (h - 1))
                        for j in range(TB):
                            last = nc.tensor.matmul(b[2 * (h % 2) + j // 2][:, (j % 2) * MEM:(j % 2 + 1) * MEM],
                                                    qT[rows, h // 2, j * P:(j + 1) * P], kT[rows, h // 2, :], start=True, stop=True)
                        last.then_inc(s["s_mm"], 1)

                    def values(h):
                        rows = slice((h % 2) * XA_DIM, (h % 2 + 1) * XA_DIM)
                        pe.wait_ge(s["p_ok"], i * XA_HEADS + (h + 1))
                        for c in range(MC):
                            if h >= 1:
                                pe.wait_ge(s["pT_ok"], i * (XA_HEADS * MC) + MC * (h - 1) + c + 1)
                            for j in range(TB):
                                last = nc.tensor.transpose(b[5 + c][:, j * P:(j + 1) * P], p[h % 2][:, j, c * P:(c + 1) * P], ident)
                            last.then_inc(s["pT_mm"], 1)
                        if h % 2 == 0:
                            pe.wait_ge(s["aT_ok"], i * XC + h // 2)
                        for c in range(MC):
                            pe.wait_ge(s["pT_ok"], i * (XA_HEADS * MC) + MC * h + c + 1)
                            last = nc.tensor.matmul(b[7][rows, :], vm[:, c, h * XA_DIM:(h + 1) * XA_DIM], pT[h % 2][:, c, :],
                                                    start=(c == 0), stop=(c == MC - 1))
                        last.then_inc(s["pv_mm"], 1)

                    scores(0)
                    scores(1)
                    for h in range(XA_HEADS):
                        values(h)
                        if h + 2 < XA_HEADS:
                            scores(h + 2)
                    pe.wait_ge(s["aT_ok"], i * XC + XC)
                    for m in range(KD):
                        if m >= 4:
                            pe.wait_ge(s["x_add2"], i * KD + (m - 3))
                        for c in range(XC):
                            last = nc.tensor.matmul(b[m % 4][:, :], wo[:, c, m * P:(m + 1) * P], aT[:, c, :],
                                                    start=(c == 0), stop=(c == XC - 1))
                        last.then_inc(s["wo_mm"], 1)
                    for k in range(KD):
                        pe.wait_ge(s["sq2"], i * KD + (k + 1))
                        last = nc.tensor.matmul(b[4][:, :], ones, sq[:, k, :], start=(k == 0), stop=(k == KD - 1))
                    last.then_inc(s["ss2"], 1)
                    for j in range(TB):
                        for half in range(2):
                            n = 2 * j + half
                            if n >= 4:
                                pe.wait_ge(s["nat_ok"], i * (2 * TB) + (n - 3))
                            for m in range(4):
                                last = nc.tensor.transpose(b[n % 4][:, m * P:(m + 1) * P], xT[:, 4 * half + m, j * P:(j + 1) * P], ident)
                            last.then_inc(s["nat_mm"], 1)
                    pe.wait_ge(s["h2"], i * KD + KD)
                    for j in range(TB):
                        for k in range(KD):
                            last = nc.tensor.matmul(b[5][:, j * NR:(j + 1) * NR], hT[:, k, j * P:(j + 1) * P], w_r[:, k, :],
                                                    start=(k == 0), stop=(k == KD - 1))
                    last.then_inc(s["lg_mm"], 1)

            @block.scalar
            def _(act):
                act.wait_ge(s["mem_in"], 16)
                for c in range(MC):
                    nc.scalar.activation(mem_sq[:, c, :], mem_n[:, c, :], ACT.Square, accum_out=mss[:, c:c + 1]).then_inc(s["m_sq"], 1)
                act.wait_ge(s["m_sq"], MC)
                nc.scalar.activation(mr[:, :], mss[:, :], ACT.Ln, bias=t["eps"][:, 0:1], scale=1.0 / D).then_inc(s["m_ln"], 1)
                act.wait_ge(s["m_ln"], 1)
                nc.scalar.activation(mr[:, :], mr[:, :], ACT.Exp, scale=-0.5).then_inc(s["m_r"], 1)
                act.wait_ge(s["m_r"], 1)
                for c in range(MC):
                    nc.scalar.activation(mem_n[:, c, :], mem_n[:, c, :], ACT.Copy, scale=mr[:, c:c + 1]).then_inc(s["m_n"], 1)
                act.wait_ge(s["m_k"], 1)
                nc.scalar.activation(kT[:, :, :], quad(b[2][:, :], MEM), ACT.Copy).then_inc(s["m_kc"], 1)
                act.wait_ge(s["m_v"], 1)
                nc.scalar.activation(vm[:, :, :], quad(b[3][:, :], XW), ACT.Copy).then_inc(s["m_vc"], 1)
                with act.Fori(0, NBLK) as i:
                    for m in range(KD):
                        act.wait_ge(s["x_add"], i * KD + (m + 1))
                        act.wait_ge(s["ss2"], i)
                        nc.scalar.activation(sq[:, m, :], xT[:, m, :], ACT.Square).then_inc(s["sq1"], 1)
                    act.wait_ge(s["ss1"], i + 1)
                    nc.scalar.activation(lnr[:, :], b[4][:, :], ACT.Ln, bias=t["eps"][:, 0:1], scale=1.0 / D).then_inc(s["ln1"], 1)
                    act.wait_ge(s["ln1"], i + 1)
                    act.wait_ge(s["h2"], i * KD)
                    nc.scalar.activation(rB[:, :], lnr[:, :], ACT.Exp, scale=-0.5).then_inc(s["r1"], 1)
                    for c in range(XC):
                        act.wait_ge(s["q_mm"], i * XC + (c + 1))
                        nc.scalar.activation(qT[:, c, :], b[5 + c][:, :], ACT.Copy).then_inc(s["q_ok"], 1)

                    def exps(h):
                        act.wait_ge(s["nmx_ok"], i * XA_HEADS + (h + 1))
                        if h >= 2:
                            act.wait_ge(s["pT_mm"], i * (XA_HEADS * MC) + MC * (h - 1))
                        for j in range(TB):
                            nc.scalar.activation(p[h % 2][:, j, :], b[2 * (h % 2) + j // 2][:, (j % 2) * MEM:(j % 2 + 1) * MEM],
                                                 ACT.Exp, bias=nmx[:, h, j:j + 1], scale=XA_DIM ** -0.5,
                                                 accum_out=ssum[:, h, j:j + 1]).then_inc(s["exp_ok"], 1)

                    def evacs(h):
                        for c in range(MC):
                            act.wait_ge(s["pT_mm"], i * (XA_HEADS * MC) + MC * h + c + 1)
                            if h >= 2:
                                act.wait_ge(s["pv_mm"], i * XA_HEADS + (h - 1))
                            nc.scalar.activation(pT[h % 2][:, c, :], b[5 + c][:, :], ACT.Copy).then_inc(s["pT_ok"], 1)
                        if h % 2 == 1:
                            act.wait_ge(s["pv_mm"], i * XA_HEADS + (h + 1))
                            nc.scalar.activation(aT[:, h // 2, :], b[7][:, :], ACT.Copy).then_inc(s["aT_ok"], 1)

                    exps(0)
                    for h in range(XA_HEADS):
                        if h + 1 < XA_HEADS:
                            exps(h + 1)
                        evacs(h)
                    for m in range(KD):
                        act.wait_ge(s["x_add2"], i * KD + (m + 1))
                        nc.scalar.activation(sq[:, m, :], xT[:, m, :], ACT.Square).then_inc(s["sq2"], 1)
                    act.wait_ge(s["ss2"], i + 1)
                    nc.scalar.activation(lnr[:, :], b[4][:, :], ACT.Ln, bias=t["eps"][:, 0:1], scale=1.0 / D).then_inc(s["ln2"], 1)
                    act.wait_ge(s["ln2"], i + 1)
                    nc.scalar.activation(rB[:, :], lnr[:, :], ACT.Exp, scale=-0.5).then_inc(s["r2"], 1)

            @block.gpsimd
            def _(pool):
                with pool.Fori(0, NBLK) as i:
                    pool.wait_ge(s["x_in"], i * 16 + 16)
                    for m in range(KD):
                        pool.wait_ge(s["a_g"], i * KD + (m + 1))
                        pool.wait_ge(s["b_g"], i * KD + (m + 1))
                        nc.gpsimd.tensor_tensor(gates[:, m, :], gates[:, m, :], gates[:, KD + m, :], ALU.add).then_inc(s["ab"], 1)
                        pool.wait_ge(s["ab"], i * KD + (m + 1))
                        nc.gpsimd.tensor_tensor(xT[:, m, :], xT[:, m, :], gates[:, m, :], ALU.add).then_inc(s["x_add"], 1)
                    for j in range(TB):
                        pool.wait_ge(s["nat_ok"], i * (2 * TB) + 2 * (j + 1))
                        pool.dma_start(x2_d[ds(i * TB + j, 1), :, :], x2n[j % 2][:, :]).then_inc(x2_out[j % 2], 16)
                for j in range(2):
                    pool.wait_ge(x2_out[j], 16 * NT // 2)

            @block.vector
            def _(dve):
                for k in range(KD):
                    dve.wait_ge(s["m_T"], k + 1)
                    dve.wait_ge(s["w_in"], 160)
                    nc.vector.tensor_scalar(memT[:, k, :], b[k % 2][:, 0:MEM], gm[:, k:k + 1], None, ALU.mult).then_inc(s["m_Tc"], 1)
                with dve.Fori(0, NBLK) as i:
                    dve.wait_ge(s["g_in"], i * 16 + 16)
                    for m in range(KD):
                        dve.wait_ge(s["ab_mm"], i * (2 * KD) + 2 * (m + 1))
                        nc.vector.tensor_tensor(gates[:, m, :], b[2 * (m % 2)][:, :], gates[:, m, :], ALU.mult).then_inc(s["a_g"], 1)
                        nc.vector.tensor_tensor(gates[:, KD + m, :], b[2 * (m % 2) + 1][:, :], gates[:, KD + m, :],
                                                ALU.mult).then_inc(s["b_g"], 1)
                    dve.wait_ge(s["r1"], i + 1)
                    dve.wait_ge(s["lg_mm"], i)
                    for m in range(KD):
                        nc.vector.scalar_tensor_tensor(hT[:, m, :], xT[:, m, :], gx[:, m:m + 1], rB[:, :],
                                                       ALU.mult, ALU.mult).then_inc(s["h1"], 1)

                    def peak(h):
                        dve.wait_ge(s["s_mm"], i * XA_HEADS + (h + 1))
                        if h == 0:
                            dve.wait_ge(s["exp_ok"], i * (XA_HEADS * TB))
                        for a in range(2):
                            nc.vector.tensor_reduce(mx[:, h, 2 * a:2 * a + 2], quad(b[2 * (h % 2) + a][:, :], MEM), axis=AX.X,
                                                    op=ALU.max).then_inc(s["mx_ok"], 1)
                        dve.wait_ge(s["mx_ok"], i * (2 * XA_HEADS) + 2 * (h + 1))
                        nc.vector.tensor_scalar(nmx[:, h, :], mx[:, h, :], -XA_DIM ** -0.5, None, ALU.mult).then_inc(s["nmx_ok"], 1)

                    def norm(h):
                        dve.wait_ge(s["exp_ok"], i * (XA_HEADS * TB) + TB * (h + 1))
                        nc.vector.reciprocal(rsum[:, h, :], ssum[:, h, :]).then_inc(s["rs_ok"], 1)
                        dve.wait_ge(s["rs_ok"], i * XA_HEADS + (h + 1))
                        nc.vector.tensor_tensor(p[h % 2][:, :, :], p[h % 2][:, :, :], bc(rsum[:, h, :], MEM), ALU.mult).then_inc(s["p_ok"], 1)

                    peak(0)
                    for h in range(XA_HEADS):
                        if h + 1 < XA_HEADS:
                            peak(h + 1)
                        norm(h)
                    for m in range(KD):
                        dve.wait_ge(s["wo_mm"], i * KD + (m + 1))
                        nc.vector.tensor_tensor(xT[:, m, :], xT[:, m, :], b[m % 4][:, :], ALU.add).then_inc(s["x_add2"], 1)
                    for j in range(TB):
                        if j < 2:
                            dve.wait_ge(x2_out[j % 2], i * 32)
                        else:
                            dve.wait_ge(x2_out[j % 2], i * 32 + 16)
                        for half in range(2):
                            n = 2 * j + half
                            dve.wait_ge(s["nat_mm"], i * (2 * TB) + (n + 1))
                            nc.vector.tensor_copy(x2n[j % 2][:, half * BLK:(half + 1) * BLK], b[n % 4][:, :]).then_inc(s["nat_ok"], 1)
                    dve.wait_ge(s["r2"], i + 1)
                    dve.wait_ge(s["q_mm"], i * XC + XC)
                    dve.wait_ge(s["x_add2"], i * KD + KD)
                    for m in range(KD):
                        nc.vector.scalar_tensor_tensor(hT[:, m, :], xT[:, m, :], gf[:, m:m + 1], rB[:, :],
                                                       ALU.mult, ALU.mult).then_inc(s["h2"], 1)
                    dve.wait_ge(s["lg_mm"], i + 1)
                    nc.vector.tensor_tensor(t["logits"][:, ds(i * TB, TB), :], quad(b[5][:, 0:TB * NR], NR), bc_mid(bias_r[:, :], TB),
                                            ALU.add).then_inc(s["lg_ok"], 1)
                dve.wait_ge(s["lg_ok"], NBLK)


W_SLOTS = 3
SLOT_BLOCKS = MAX_MOE + 2


def load_expert(sp, t, e, slot):
    for name, src in (("wg", "we_gate"), ("wu", "we_up"), ("wd", "we_down")):
        rows = t[src][0].rearrange("e (k p) n -> e p k n", p=P)[ds(e, 1), :, :, :]
        sp.dma_start(t[name][slot][:, :, :], rows.rearrange("e p k n -> p (e k) n")).then_inc(t[name + "_in"][slot], 16)


def phase_route(nc, t):
    with Phase(nc, "F") as ph:
        NEG = -3.0e38
        lg = t["logits"]
        g8, gv, gi = ph.sb("g8", [P, NT, 8]), ph.sb("gv", [P, NT, 8]), ph.sb("gi", [P, NT, 8], U32)
        gif = ph.sb("gif", [P, NT])
        ohg, e4 = ph.sb("ohg", [P, NT, N_GRP]), ph.sb("e4", [P, NT, N_GRP])
        esum, pg = ph.sb("esum", [P, NT]), ph.sb("pg", [P, NT])
        le = ph.sb("le", [P, NT, NE])
        ev, ei = ph.sb("ev", [P, NT, 8]), ph.sb("ei", [P, NT, 8], U32)
        eif = ph.sb("eif", [P, NT, TOP_K])
        oh = [ph.sb(f"oh{j}", [P, NT, NE]) for j in range(TOP_K)]
        both, pos, tmp = ph.sb("both", [P, NT, NE]), ph.sb("pos", [P, NT, NE]), ph.sb("tmp", [P, NT, NE])
        tot, run = ph.sb("tot", [P, NT, NE]), ph.sb("run", [P, NT + 1, NE])
        cmp = ph.sb("cmp", [P, NE, NT])
        blocks, ends, base = ph.sb("blocks", [P, NE]), ph.sb("ends", [P, NE]), ph.sb("base", [P, NE])
        dst = ph.sb("dst", [P, NT, TOP_K])
        e1, w1 = ph.sb("e1", [P, NT]), ph.sb("w1", [P, NT])
        rows_f, over = ph.sb("rows_f", [P, SLOT_BLOCKS]), ph.sb("over", [P, SLOT_BLOCKS])
        slots = ph.sb("slots", [SLOT_BLOCKS, P])
        pc = [ph.bank(f"c{i}") for i in range(3)]
        const = t["const"]
        ident, ones, exc = (const[:, k:k + P] for k in (K_ID, K_ONE, K_EXC))
        iota = const[:, K_IOTA:K_IOTA + 32]
        step, mm, act_done, dst_ok = (ph.sem(s) for s in ("step", "mm", "act_done", "dst_ok"))
        cleared, scattered, slots_in = (ph.pool_dma_sem(s) for s in ("cleared", "scattered", "slots_in"))

        with nc.Block() as block:
            mark = {}

            @block.vector
            def _(dve):
                count = [0]

                def link(ins):
                    count[0] += 1
                    ins.then_inc(step, 1)
                    dve.wait_ge(step, count[0])

                v = nc.vector
                link(v.memset(g8[:, :, :], NEG))
                link(v.tensor_copy(g8[:, :, 0:N_GRP], lg[:, :, 0:N_GRP]))
                for i in range(NT):
                    link(v.max(gv[:, i, :], g8[:, i, :]))
                    link(v.max_index(gi[:, i, :], gv[:, i, :], g8[:, i, :]))
                link(v.tensor_copy(gif[:, :], gi[:, :, 0]))
                link(v.tensor_tensor(ohg[:, :, :], bc_mid(iota[:, 0:N_GRP], NT), bc(gif[:, :], N_GRP), ALU.is_equal))
                link(v.tensor_tensor(e4[:, :, :], lg[:, :, 0:N_GRP], bc(gv[:, :, 0], N_GRP), ALU.subtract))
                mark["e4"] = count[0]
                four = le[:, :, :].rearrange("p t (g e) -> p (t g) e", g=N_GRP)
                flat = ohg[:, :, :].rearrange("p t g -> p (t g)")
                for g in range(N_GRP):
                    link(v.tensor_tensor(le[:, :, g * PER_GRP:(g + 1) * PER_GRP], lg[:, :, N_GRP + g * PER_GRP:N_GRP + (g + 1) * PER_GRP],
                                         bc(ohg[:, :, g], PER_GRP), ALU.mult))
                link(v.tensor_scalar(ohg[:, :, :], ohg[:, :, :], -1.0, -NEG / 2, ALU.add, ALU.mult))
                link(v.tensor_tensor(four, four, bc(flat, PER_GRP), ALU.add))
                for i in range(NT):
                    link(v.max(ev[:, i, :], le[:, i, :]))
                    link(v.max_index(ei[:, i, :], ev[:, i, :], le[:, i, :]))
                link(v.tensor_copy(eif[:, :, :], ei[:, :, 0:TOP_K]))
                for j in range(TOP_K):
                    link(v.tensor_tensor(oh[j][:, :, :], bc_mid(iota, NT), bc(eif[:, :, j], NE), ALU.is_equal))
                link(v.tensor_tensor(both[:, :, :], oh[0][:, :, :], oh[1][:, :, :], ALU.add))
                link(v.tensor_tensor(e1[:, :], ev[:, :, 1], ev[:, :, 0], ALU.subtract))
                mark["both"] = count[0]
                dve.wait_ge(mm, 1)
                link(v.tensor_copy(pos[:, :, :], quad(pc[0][:, :], NE)))
                link(v.tensor_copy(tot[:, :, :], quad(pc[1][:, :], NE)))
                link(v.memset(run[:, 0, :], 0.0))
                for i in range(NT):
                    link(v.tensor_tensor(run[:, i + 1, :], run[:, i, :], tot[:, i, :], ALU.add))
                link(v.tensor_scalar(tmp[:, 0, 0:NT], iota[:, 0:NT], float(P), None, ALU.mult))
                link(v.tensor_tensor(cmp[:, :, :], bc(run[:, NT, :], NT), bc_mid(tmp[:, 0, 0:NT], NE), ALU.is_gt))
                link(v.tensor_reduce(blocks[:, :], cmp[:, :, :], axis=AX.X, op=ALU.add))
                link(v.tensor_scalar(blocks[:, :], blocks[:, :], 1.0, None, ALU.max))
                link(v.tensor_tensor_scan(ends[:, :], blocks[:, :], blocks[:, :], 0.0, ALU.add, ALU.bypass))
                link(v.tensor_tensor(base[:, :], ends[:, :], blocks[:, :], ALU.subtract))
                link(v.tensor_copy(t["n_blocks"][:, 0:NE], blocks[:, :]))
                link(v.tensor_copy(t["n_blocks"][:, NE:2 * NE], base[:, :]))
                link(v.tensor_copy(t["n_blocks"][:, 2 * NE:2 * NE + 1], ends[:, NE - 1:NE]))
                link(v.tensor_scalar(base[:, :], base[:, :], float(P), None, ALU.mult))
                link(v.tensor_tensor(pos[:, :, :], pos[:, :, :], run[:, 0:NT, :], ALU.add))
                link(v.tensor_tensor(pos[:, :, :], pos[:, :, :], bc_mid(base[:, :], NT), ALU.add))
                for j in range(TOP_K):
                    link(v.tensor_tensor(tmp[:, :, :], pos[:, :, :], oh[j][:, :, :], ALU.mult))
                    link(v.tensor_reduce(dst[:, :, j:j + 1], tmp[:, :, :], axis=AX.X, op=ALU.add))
                v.tensor_copy(t["dest"][:, :, :], dst[:, :, :]).then_inc(dst_ok, 1)
                dve.wait_ge(act_done, 2)
                link(v.tensor_reduce(esum[:, :].unsqueeze(2), e4[:, :, :], axis=AX.X, op=ALU.add))
                link(v.reciprocal(pg[:, :], esum[:, :]))
                link(v.tensor_scalar(w1[:, :], e1[:, :], 1.0, None, ALU.add))
                link(v.reciprocal(w1[:, :], w1[:, :]))
                link(v.tensor_tensor(w1[:, :], w1[:, :], pg[:, :], ALU.mult))
                link(v.tensor_copy(t["wts"][:, :, 0], w1[:, :]))
                link(v.tensor_tensor(t["wts"][:, :, 1], w1[:, :], e1[:, :], ALU.mult))
                dve.wait_ge(mm, 2)
                link(v.tensor_copy(rows_f[:, :], pc[2][:, 0:SLOT_BLOCKS]))
                link(v.tensor_copy(t["slot_row"][:, :], rows_f[:, :]))
                for j in range(TOP_K):
                    link(v.tensor_scalar(over[:, :], rows_f[:, :], float(SEQ), float(SEQ), ALU.is_ge, ALU.mult))
                    link(v.tensor_tensor(rows_f[:, :], rows_f[:, :], over[:, :], ALU.subtract))
                link(v.tensor_copy(t["slot_tok"][:, :], rows_f[:, :]))

            @block.sync
            def _(sp):
                load_expert(sp, t, 0, 0)

            @block.scalar
            def _(act):
                act.wait_ge(step, mark["e4"])
                nc.scalar.activation(e4[:, :, :], e4[:, :, :], ACT.Exp).then_inc(act_done, 1)
                act.wait_ge(step, mark["both"])
                nc.scalar.activation(e1[:, :], e1[:, :], ACT.Exp).then_inc(act_done, 1)

            @block.tensor
            def _(pe):
                pe.wait_ge(step, mark["both"])
                flat = both[:, :, :].rearrange("p t e -> p (t e)")
                nc.tensor.matmul(pc[0][:, :], exc, flat, start=True, stop=True)
                nc.tensor.matmul(pc[1][:, :], ones, flat, start=True, stop=True).then_inc(mm, 1)
                pe.wait_ge(slots_in, 16)
                nc.tensor.transpose(pc[2][:, 0:SLOT_BLOCKS], slots[:, :], ident[0:SLOT_BLOCKS, 0:SLOT_BLOCKS]).then_inc(mm, 1)

            @block.gpsimd
            def _(pool):
                pool.dma_start(t["slot_d"].rearrange("(b p) o -> b (p o)", p=P), const[0:SLOT_BLOCKS, K_PAD:K_PAD + P]).then_inc(cleared, 16)
                pool.wait_ge(cleared, 16)
                pool.wait_ge(dst_ok, 1)
                for i in range(NT):
                    for j in range(TOP_K):
                        pool.indirect_dma_start(t["slot_d"], bass.IndirectOffsetOnAxis(ap=t["dest"][:, i, j:j + 1], axis=0),
                                                const[:, K_TOK + j * NT + i:K_TOK + j * NT + i + 1], None).then_inc(scattered, 16)
                pool.wait_ge(scattered, 16 * NT * TOP_K)
                pool.dma_start(slots[:, :], t["slot_d"].rearrange("(b p) o -> b (p o)", p=P)).then_inc(slots_in, 16)
                pool.wait_ge(slots_in, 16)


def phase_experts(nc, t):
    with Phase(nc, "G") as ph:
        KE = DE // P
        wg, wu, wd = t["wg"], t["wu"], t["wd"]
        TURNS, REST = divmod(NE, W_SLOTS)
        tok, row = ph.sb("tok", [P, 1], I32), ph.sb("row", [P, 1], I32)
        xg, xn = ph.sb("xg", [P, D]), ph.sb("xn", [P, D])
        xsq = ph.sb("xsq", [P, D])
        ss, lnr, r = (ph.sb(s, [P, 1]) for s in ("ss", "lnr", "r"))
        hT = ph.sb("hT", [P, KD, P])
        sg, a, aT = ph.sb("sg", [P, DE]), ph.sb("a", [P, DE]), ph.sb("aT", [P, KE, P])
        y = ph.sb("y", [P, D])
        gf = ph.sb("gf", [P, KD])
        bx = [ph.bank(f"x{i}") for i in range(2)]
        bg, bu, ba = ph.bank("g"), ph.bank("u"), ph.bank("a")
        by = [ph.bank(f"y{i}") for i in range(2)]
        w_used = [ph.sem(f"w_used{i}") for i in range(W_SLOTS)]
        names = ("gf_in", "tok_ok", "row_ok", "indices_set", "expert_begun", "sq_ok", "ln_ok", "r_ok", "xn_ok", "xT_mm", "hT_ok", "g_mm", "u_mm", "sg_ok", "a_ok",
                 "aT_mm", "aT_ok", "y_mm", "y0_ok", "y1_ok")
        s = {n: ph.sem(n) for n in names} | {n: ph.pool_dma_sem(n) for n in ("xg_in", "y_out")}
        ident = t["const"][:, K_ID:K_ID + P]
        x_rows = t["x2_d"]
        nb = t["n_blocks"]
        def all_blocks(eng):
            return eng.value_load(nb[0:1, 2 * NE:2 * NE + 1], min_val=NE, max_val=MAX_MOE)

        with nc.Block() as block:

            @block.sync
            def _(sp):
                sp.dma_start(gf[:, :], t["g_ffn"].rearrange("o (k p) -> p (o k)", p=P)).then_inc(s["gf_in"], 16)
                for e in range(1, W_SLOTS):
                    load_expert(sp, t, e, e)
                with sp.Fori(1, TURNS) as i:
                    for q in range(W_SLOTS):
                        sp.wait_ge(w_used[q], i)
                        load_expert(sp, t, i * W_SLOTS + q, q)
                for q in range(REST):
                    sp.wait_ge(w_used[q], TURNS)
                    load_expert(sp, t, TURNS * W_SLOTS + q, q)

            @block.gpsimd
            def _(pool):
                n = all_blocks(pool)

                def gather(i):
                    nc.gpsimd.tensor_copy(tok[:, :], t["slot_tok"][:, ds(i, 1)]).then_inc(s["tok_ok"], 1)
                    pool.wait_ge(s["tok_ok"], i + 1)
                    pool.sem_inc(s["indices_set"], 1)
                    pool.indirect_dma_start(xg[:, :], None, x_rows, bass.IndirectOffsetOnAxis(ap=tok[:, 0:1], axis=0)).then_inc(s["xg_in"], 16)

                gather(0)
                pool.wait_ge(s["xn_ok"], 1)
                gather(1)
                with pool.Fori(0, n) as i:
                    pool.wait_ge(s["xn_ok"], i + 2)
                    gather(i + 2)
                    pool.wait_ge(s["y_out"], i * 16)
                    nc.gpsimd.tensor_copy(row[:, :], t["slot_row"][:, ds(i, 1)]).then_inc(s["row_ok"], 1)
                    pool.wait_ge(s["row_ok"], i + 1)
                    pool.wait_ge(s["y0_ok"], i + 1)
                    pool.wait_ge(s["y1_ok"], i + 1)
                    pool.sem_inc(s["indices_set"], 1)
                    pool.indirect_dma_start(t["y_d"], bass.IndirectOffsetOnAxis(ap=row[:, 0:1], axis=0), y[:, :], None).then_inc(s["y_out"], 16)
                pool.wait_ge(s["y_out"], n * 16)
                pool.wait_ge(s["xg_in"], n * 16 + 32)

            @block.scalar
            def _(act):
                n = all_blocks(act)

                def norm(i):
                    act.wait_ge(s["xg_in"], i * 16 + 16)
                    nc.scalar.activation(xsq[:, :], xg[:, :], ACT.Square, accum_out=ss[:, :]).then_inc(s["sq_ok"], 1)
                    act.wait_ge(s["sq_ok"], i + 1)
                    nc.scalar.activation(lnr[:, :], ss[:, :], ACT.Ln, bias=t["eps"][:, 0:1], scale=1.0 / D).then_inc(s["ln_ok"], 1)
                    act.wait_ge(s["ln_ok"], i + 1)
                    nc.scalar.activation(r[:, :], lnr[:, :], ACT.Exp, scale=-0.5).then_inc(s["r_ok"], 1)
                    act.wait_ge(s["r_ok"], i + 1)
                    act.wait_ge(s["xT_mm"], i)
                    nc.scalar.activation(xn[:, :], xg[:, :], ACT.Copy, scale=r[:, 0:1]).then_inc(s["xn_ok"], 1)

                norm(0)
                with act.Fori(0, n) as i:
                    act.wait_ge(s["g_mm"], i + 1)
                    act.wait_ge(s["a_ok"], i)
                    nc.scalar.activation(sg[:, :], bg[:, :], ACT.Silu).then_inc(s["sg_ok"], 1)
                    norm(i + 1)
                    act.wait_ge(s["y_mm"], i + 1)
                    act.wait_ge(s["y_out"], i * 16)
                    nc.scalar.activation(y[:, 0:BLK], by[0][:, :], ACT.Copy).then_inc(s["y0_ok"], 1)

            @block.vector
            def _(dve):
                n = all_blocks(dve)
                dve.wait_ge(s["gf_in"], 16)

                def scaled(i):
                    for c in range(2):
                        dve.wait_ge(s["xT_mm"], i + 1)
                        nc.vector.tensor_tensor(hT[:, 4 * c:4 * c + 4, :], quad(bx[c][:, :]), bc(gf[:, 4 * c:4 * c + 4], P),
                                                ALU.mult).then_inc(s["hT_ok"], 1)

                scaled(0)
                with dve.Fori(0, n) as i:
                    dve.wait_ge(s["sg_ok"], i + 1)
                    dve.wait_ge(s["u_mm"], i + 1)
                    dve.wait_ge(s["aT_mm"], i)
                    nc.vector.tensor_tensor(a[:, :], sg[:, :], bu[:, :], ALU.mult).then_inc(s["a_ok"], 1)
                    dve.wait_ge(s["aT_mm"], i + 1)
                    dve.wait_ge(s["y_mm"], i)
                    nc.vector.tensor_copy(aT[:, :, :], quad(ba[:, :])).then_inc(s["aT_ok"], 1)
                    scaled(i + 1)
                    dve.wait_ge(s["y_mm"], i + 1)
                    dve.wait_ge(s["y_out"], i * 16)
                    nc.vector.tensor_copy(y[:, BLK:D], by[1][:, :]).then_inc(s["y1_ok"], 1)

            @block.tensor
            def _(pe):
                def rows_T(n):
                    pe.wait_ge(s["xn_ok"], n + 1)
                    pe.wait_ge(s["hT_ok"], n * 2)
                    for k in range(KD):
                        last = nc.tensor.transpose(bx[k // 4][:, (k % 4) * P:(k % 4 + 1) * P], xn[:, k * P:(k + 1) * P], ident)
                    last.then_inc(s["xT_mm"], 1)

                def expert(e, q, turn):
                    count = pe.value_load(nb[0:1, ds(e, 1)], min_val=1, max_val=SEQ // P)
                    first = pe.value_load(nb[0:1, ds(e + NE, 1)], min_val=0, max_val=MAX_MOE)
                    for name in ("wg_in", "wu_in", "wd_in"):
                        pe.wait_ge(t[name][q], turn * 16 + 16)
                    pe.sem_inc(s["expert_begun"], 1)
                    with pe.Fori(0, count) as j:
                        n = first + j
                        pe.wait_ge(s["hT_ok"], n * 2 + 2)
                        pe.wait_ge(s["sg_ok"], n)
                        for k in range(KD):
                            last = nc.tensor.matmul(bg[:, :], hT[:, k, :], wg[q][:, k, :], start=(k == 0), stop=(k == KD - 1))
                        last.then_inc(s["g_mm"], 1)
                        pe.wait_ge(s["a_ok"], n)
                        for k in range(KD):
                            last = nc.tensor.matmul(bu[:, :], hT[:, k, :], wu[q][:, k, :], start=(k == 0), stop=(k == KD - 1))
                        last.then_inc(s["u_mm"], 1)
                        rows_T(n + 1)
                        pe.wait_ge(s["a_ok"], n + 1)
                        pe.wait_ge(s["aT_ok"], n)
                        for k in range(KE):
                            last = nc.tensor.transpose(ba[:, k * P:(k + 1) * P], a[:, k * P:(k + 1) * P], ident)
                        last.then_inc(s["aT_mm"], 1)
                        pe.wait_ge(s["aT_ok"], n + 1)
                        pe.wait_ge(s["y0_ok"], n)
                        pe.wait_ge(s["y1_ok"], n)
                        for c in range(2):
                            for k in range(KE):
                                last = nc.tensor.matmul(by[c][:, :], aT[:, k, :], wd[q][:, k, c * BLK:(c + 1) * BLK],
                                                        start=(k == 0), stop=(k == KE - 1))
                        last.then_inc(s["y_mm"], 1)
                    pe.wait_ge(s["y_mm"], first + count)
                    pe.sem_inc(w_used[q], 1)

                rows_T(0)
                with pe.Fori(0, TURNS) as i:
                    for q in range(W_SLOTS):
                        expert(i * W_SLOTS + q, q, i)
                for q in range(REST):
                    expert(TURNS * W_SLOTS + q, q, TURNS)


def phase_combine(nc, t):
    with Phase(nc, "H") as ph:
        def two(name, shape, dt=F32):
            return [ph.sb(f"{name}{c}", shape, dt) for c in range(2)]

        x, o = two("x", [P, D]), two("o", [P, D])
        y = two("y", [P, TOP_K, D])
        ss, r = two("ss", [P, 1]), two("r", [P, 1])
        g = ph.sb("g", [P, D])
        sems = lambda n: [ph.sem(f"{n}{c}") for c in range(2)]
        out_done = [ph.pool_dma_sem(f"out_done{c}") for c in range(2)]
        x_in, y_in, add_ok, sq_ok, ln_ok, r_ok, n_ok = (
            sems(n) for n in ("x_in", "y_in", "add_ok", "sq_ok", "ln_ok", "r_ok", "n_ok"))
        g_in = ph.sem("g_in")
        wts_flat = t["wts"][:, :, :].rearrange("p t j -> p (t j)")
        x_d = t["x2_d"].rearrange("(j p) d -> j p d", p=P)
        y_d = t["y_d"][0:TOP_K * SEQ, :].rearrange("(k j p) d -> j p k d", p=P, k=TOP_K)
        out_d = t["out"].rearrange("b (j p) d -> (b j) p d", p=P)

        with nc.Block() as block:

            @block.sync
            def _(sp):
                sp.dma_start(g[:, :], t["g_final"].rearrange("(o d) -> o d", o=1).to_broadcast([P, D])).then_inc(g_in, 16)
                with sp.Fori(0, NT // 2) as i:
                    for c in range(2):
                        sp.wait_ge(n_ok[c], i)
                        sp.dma_start(x[c][:, :], x_d[ds(i * 2 + c, 1), :, :]).then_inc(x_in[c], 16)
                        sp.dma_start(y[c][:, :, :], y_d[ds(i * 2 + c, 1), :, :, :].rearrange("j p k d -> p (j k) d")).then_inc(y_in[c], 16)

            @block.vector
            def _(dve):
                dve.wait_ge(g_in, 16)
                with dve.Fori(0, NT // 2) as i:
                    for c in range(2):
                        dve.wait_ge(y_in[c], i * 16 + 16)
                        dve.wait_ge(x_in[c], i * 16 + 16)
                        for j in range(TOP_K):
                            if j:
                                dve.wait_ge(add_ok[c], i * TOP_K + j)
                            nc.vector.scalar_tensor_tensor(x[c][:, :], y[c][:, j, :], wts_flat[:, ds(i * (2 * TOP_K) + (c * TOP_K + j), 1)],
                                                           x[c][:, :], ALU.mult, ALU.add).then_inc(add_ok[c], 1)
                    for c in range(2):
                        dve.wait_ge(r_ok[c], i + 1)
                        dve.wait_ge(out_done[c], i * 16)
                        nc.vector.scalar_tensor_tensor(o[c][:, :], x[c][:, :], r[c][:, 0:1], g[:, :], ALU.mult, ALU.mult).then_inc(n_ok[c], 1)

            @block.scalar
            def _(act):
                with act.Fori(0, NT // 2) as i:
                    for c in range(2):
                        act.wait_ge(add_ok[c], i * TOP_K + TOP_K)
                        act.wait_ge(out_done[c], i * 16)
                        nc.scalar.activation(o[c][:, :], x[c][:, :], ACT.Square, accum_out=ss[c][:, :]).then_inc(sq_ok[c], 1)
                        act.wait_ge(sq_ok[c], i + 1)
                        nc.scalar.activation(ss[c][:, :], ss[c][:, :], ACT.Ln, bias=t["eps"][:, 0:1], scale=1.0 / D).then_inc(ln_ok[c], 1)
                        act.wait_ge(ln_ok[c], i + 1)
                        nc.scalar.activation(r[c][:, :], ss[c][:, :], ACT.Exp, scale=-0.5).then_inc(r_ok[c], 1)

            @block.gpsimd
            def _(pool):
                with pool.Fori(0, NT // 2) as i:
                    for c in range(2):
                        pool.wait_ge(n_ok[c], i + 1)
                        pool.dma_start(out_d[ds(i * 2 + c, 1), :, :], o[c][:, :]).then_inc(out_done[c], 16)
                for c in range(2):
                    pool.wait_ge(out_done[c], 16 * NT // 2)


def build(nc, tensors):
    t = dict(tensors)
    for name, shape in (("xT_d", (KD, P, SEQ)), ("proj_d", (NGRP, P, SEQ)), ("o_d", (KD, P, SEQ)),
                        ("x2_d", (SEQ, D)), ("slot_d", (SLOT_BLOCKS * P, 1)), ("y_d", (TOP_K * SEQ + P, D))):
        t[name] = nc.dram_tensor(name, shape, F32, kind="Internal").ap()
    with Phase(nc, "all") as ph, nc.allow_non_contiguous_dma(reason="small vectors, a feature on each partition"):
        t["const"] = ph.sb("const", [P, NCONST])
        t["eps"] = ph.sb("eps", [P, 1])
        t["beta"], t["glog"] = (ph.sb(n, [P, NT, DN_HEADS]) for n in ("beta", "glog"))
        t["logits"] = ph.sb("logits", [P, NT, NR])
        t["dest"], t["wts"] = ph.sb("dest", [P, NT, TOP_K], I32), ph.sb("wts", [P, NT, TOP_K])
        t["n_blocks"] = ph.sb("n_blocks", [P, 2 * NE + 1], I32)
        t["slot_tok"], t["slot_row"] = (ph.sb(n, [P, SLOT_BLOCKS], I32) for n in ("slot_tok", "slot_row"))
        with Phase(nc, "h") as hp:
            h_hi, h_lo = (hp.sb(n, [P, KD, SEQ], F32R) for n in ("h_hi", "h_lo"))
            phase_norm_x(nc, t, h_hi, h_lo)
            phase_project(nc, t, h_hi, h_lo)
        phase_stick(nc, t)
        phase_delta(nc, t)
        phase_merge(nc, t)
        with Phase(nc, "w") as wp:
            t["wg"], t["wu"] = ([wp.sb(f"{n}{i}", [P, KD, DE]) for i in range(W_SLOTS)] for n in ("wg", "wu"))
            t["wd"] = [wp.sb(f"wd{i}", [P, DE // P, D]) for i in range(W_SLOTS)]
            for n in ("wg_in", "wu_in", "wd_in"):
                t[n] = [wp.sem(f"{n}{i}") for i in range(W_SLOTS)]
            phase_route(nc, t)
            phase_experts(nc, t)
        phase_combine(nc, t)


_INS = ["x", "mem", "g_mix", "w_in", "dn_conv_w", "dn_a_log", "dn_dt_bias", "dn_norm_g", "w_out", "g_xattn", "g_mem",
        "xa_wq", "xa_wkv", "xa_wo", "g_ffn", "w_grp", "b_grp", "w_exp", "b_exp", "we_gate", "we_up", "we_down",
        "g_final"]


def constants():
    import numpy as np
    c = np.zeros((P, NCONST), np.float32)
    p, f = np.arange(P)[:, None], np.arange(P)[None, :]
    c[:, K_ID:K_ID + P] = p == f
    c[:, K_ONE:K_ONE + P] = 1
    c[:, K_INC:K_INC + P] = p <= f
    c[:, K_EXC:K_EXC + P] = p < f
    c[:, K_LOW:K_LOW + P] = p > f
    c[:, K_NEG:K_NEG + P] = MASKED * (f >= p)
    c[:, K_IOTA:K_IOTA + 32] = np.arange(32)
    c[:, K_TOK:K_TOK + TOP_K * NT] = p + P * np.arange(TOP_K * NT)
    c[:, K_PAD:K_PAD + P] = TOP_K * SEQ + f
    for lev in range(NLEV):
        s = 1 << lev
        m = (p // (2 * s) == f // (2 * s)) & ((p // s) % 2 == 1) & ((f // s) % 2 == 0)
        c[:, K_LEV + 2 * lev * P:K_LEV + (2 * lev + 1) * P] = m
        c[:, K_LEV + (2 * lev + 1) * P:K_LEV + (2 * lev + 2) * P] = m.T
    return c


def kernel(**inputs):
    import numpy as _np
    import concourse.bacc as _bacc
    from concourse import mybir as _mybir
    from concourse.bass_utils import run_bass_kernel_spmd as _run

    nc = _bacc.Bacc("TRN2", target_bir_lowering=False, num_devices=1)
    arrays, tensors = {"const_dram": constants()}, {}
    for name in _INS:
        a = _np.ascontiguousarray(inputs[name])
        arrays[f"in_{name}_dram"] = a
        tensors[name] = nc.dram_tensor(f"in_{name}_dram", a.shape, _mybir.dt.from_np(a.dtype), kind="ExternalInput").ap()
    tensors["const_d"] = nc.dram_tensor("const_dram", (P, NCONST), _mybir.dt.float32, kind="ExternalInput").ap()
    tensors["out"] = nc.dram_tensor("out_dram", (1, SEQ, D), _mybir.dt.float32, kind="ExternalOutput").ap()
    build(nc, tensors)
    r = _run(nc, [arrays], core_ids=[0])
    return r.results[0]["out_dram"]
```

```python
import concourse.bass as bass
from concourse import mybir
from contextlib import ExitStack

F32 = mybir.dt.float32
F32R = mybir.dt.float32r
I32 = mybir.dt.int32
U32 = mybir.dt.uint32
ALU = mybir.AluOpType
ACT = mybir.ActivationFunctionType
AX = mybir.AxisListType
ds = bass.ds

P = 128
SEQ, D, MEM = 2048, 1024, 256
KD = D // P
BLK = 512
NBLK = SEQ // BLK
NT = SEQ // P
EPS = 1e-6
SB_HEADS, SB_DIM = 8, 64
DN_HEADS, DN_DIM, DN_CONV = 4, 128, 4
XA_HEADS, XA_DIM = 4, 64
N_GRP, PER_GRP, DE = 4, 8, 512
NE = N_GRP * PER_GRP
NR = N_GRP + NE
TOP_K = 2
MAX_MOE = SEQ * TOP_K // P + NE
NLEV = 7

G_DNQ, G_DNK, G_DNV, G_SBQ, G_SBK, G_SBV, G_Z, G_GA, G_GB, NGRP = 0, 4, 8, 12, 16, 20, 24, 28, 36, 44
C_DN = 3 * SB_HEADS * SB_DIM
C_BA = C_DN + 3 * DN_HEADS * DN_DIM
C_Z = C_BA + 2 * DN_HEADS
IN_W = C_Z + DN_HEADS * DN_DIM + 2 * D

K_ID, K_ONE, K_INC, K_EXC, K_LOW, K_NEG, K_IOTA, K_TOK, K_PAD, K_LEV = 0, 128, 256, 384, 512, 640, 768, 800, 832, 960
NCONST = K_LEV + 2 * NLEV * P
MASKED = -1.0e5


class Phase:

    def __init__(self, nc, name):
        self.nc, self.name, self.stack, self.sems = nc, name, ExitStack(), []

    def __enter__(self):
        return self

    def __exit__(self, *a):
        if self.sems and not a[0]:
            with self.nc.Block() as block:

                @block.gpsimd
                def _(pool):
                    ids = sorted(sem.num for sem in self.sems)
                    first = ids[0]
                    for at, after in zip(ids, ids[1:] + [None]):
                        if after != at + 1:
                            pool.sem_clear(range(first, at + 1))
                            first = after

        self.stack.close()

    def sb(self, name, shape, dt=F32):
        return self.stack.enter_context(self.nc.sbuf_tensor(f"{self.name}_{name}", shape, dt))

    def bank(self, name):
        return self.stack.enter_context(self.nc.psum_tensor(f"{self.name}_bank_{name}", [P, BLK], F32))

    def sem(self, name):
        sem = self.stack.enter_context(self.nc.semaphore(f"{self.name}_{name}"))
        self.sems.append(sem)
        return sem

    def pool_dma_sem(self, name):
        return self.nc.alloc_semaphore(f"{self.name}_{name}")


def bc(ap, n):
    return ap.unsqueeze(2).to_broadcast([ap.shape[0], ap.shape[1], n])


def bc_mid(ap, n):
    return ap.unsqueeze(1).to_broadcast([ap.shape[0], n, ap.shape[1]])


def quad(ap, n=P):
    return ap.rearrange("p (h f) -> p h f", f=n)


def phase_norm_x(nc, t, h_hi, h_lo):
    with Phase(nc, "A") as ph:
        TB = BLK // P
        x_in = [ph.sb(f"x{i}", [P, D]) for i in range(TB)]
        xT = [ph.sb(f"xT{i}", [P, KD, BLK]) for i in range(2)]
        sq = [ph.sb(f"sq{i}", [P, BLK]) for i in range(2)]
        h = [ph.sb(f"h{i}", [P, BLK]) for i in range(2)]
        lnr, rB, g = ph.sb("lnr", [P, BLK]), ph.sb("rB", [P, BLK]), ph.sb("g", [P, KD])
        pT = [ph.bank(f"pT{i}") for i in range(4)]
        pS = [ph.bank(f"pS{i}") for i in range(2)]
        const_in, g_in = ph.sem("const_in"), ph.sem("g_in")
        x_loaded = [ph.sem(f"x_loaded{i}") for i in range(TB)]
        xT_stored = [ph.pool_dma_sem(f"xT_stored{i}") for i in range(2)]
        trans, copied, squared, summed, ln_done, r_done, h_done, hi_done, lo_done = (
            ph.sem(s) for s in ("trans", "copied", "squared", "summed", "ln_done", "r_done", "h_done", "hi_done", "lo_done"))
        ident, ones = t["const"][:, K_ID:K_ID + P], t["const"][:, K_ONE:K_ONE + P]
        x_d = t["x"].rearrange("b (j p) d -> (b j) p d", p=P)
        xT_d = t["xT_d"].rearrange("k p (c n) -> c p k n", n=BLK)

        with nc.Block() as block:

            @block.sync
            def _(sp):
                sp.dma_start(x_in[0][:, :], x_d[0]).then_inc(x_loaded[0], 16)
                sp.dma_start(t["const"][:, :], t["const_d"]).then_inc(const_in, 16)
                for j in range(1, NT):
                    if j >= TB:
                        sp.wait_ge(trans, 2 * (j - TB + 1))
                    sp.dma_start(x_in[j % TB][:, :], x_d[j]).then_inc(x_loaded[j % TB], 16)
                    if j == 1:
                        sp.dma_start(g[:, :], t["g_mix"].rearrange("o (k p) -> p (o k)", p=P)).then_inc(g_in, 16)

            @block.tensor
            def _(pe):
                pe.wait_ge(const_in, 16)

                def transposes(b):
                    for j in range(TB * b, TB * b + TB):
                        pe.wait_ge(x_loaded[j % TB], 16 * (j // TB + 1))
                        for half in range(2):
                            n = 2 * j + half
                            if n >= 4:
                                pe.wait_ge(copied, n - 3)
                            for m in range(4):
                                k = 4 * half + m
                                last = nc.tensor.transpose(pT[n % 4][:, m * P:(m + 1) * P], x_in[j % TB][:, k * P:(k + 1) * P], ident)
                            last.then_inc(trans, 1)

                transposes(0)
                for b in range(NBLK):
                    if b + 1 < NBLK:
                        transposes(b + 1)
                    if b >= 2:
                        pe.wait_ge(ln_done, b - 1)
                    for k in range(KD):
                        pe.wait_ge(squared, KD * b + k + 1)
                        last = nc.tensor.matmul(pS[b % 2][:, :], ones, sq[k % 2][:, :], start=(k == 0), stop=(k == KD - 1))
                        last.then_inc(summed, 1)

            @block.scalar
            def _(act):
                for b in range(NBLK):
                    for k in range(KD):
                        n = KD * b + k
                        act.wait_ge(copied, KD * (b + 1))
                        if n >= 2:
                            act.wait_ge(summed, n - 1)
                        nc.scalar.activation(sq[k % 2][:, :], xT[b % 2][:, k, :], ACT.Square).then_inc(squared, 1)
                    act.wait_ge(summed, KD * (b + 1))
                    nc.scalar.activation(lnr[:, :], pS[b % 2][:, :], ACT.Ln, bias=t["eps"][:, 0:1],
                                         scale=1.0 / D).then_inc(ln_done, 1)
                    act.wait_ge(ln_done, b + 1)
                    act.wait_ge(h_done, KD * b)
                    nc.scalar.activation(rB[:, :], lnr[:, :], ACT.Exp, scale=-0.5).then_inc(r_done, 1)
                    for k in range(KD):
                        n = KD * b + k
                        act.wait_ge(h_done, n + 1)
                        nc.scalar.activation(h_hi[:, k, b * BLK:(b + 1) * BLK], h[n % 2][:, :], ACT.Copy).then_inc(hi_done, 1)

            @block.gpsimd
            def _(pool):
                for n in range(KD * NBLK):
                    b, k = divmod(n, KD)
                    part = slice(b * BLK, (b + 1) * BLK)
                    if k == 0:
                        pool.wait_ge(copied, KD * (b + 1))
                        pool.dma_start(xT_d[b], xT[b % 2][:, :, :]).then_inc(xT_stored[b % 2], 16)
                    pool.wait_ge(hi_done, n + 1)
                    nc.gpsimd.tensor_tensor(h_lo[:, k, part], h[n % 2][:, :], h_hi[:, k, part].bitcast(F32),
                                            ALU.subtract).then_inc(lo_done, 1)
                for i in range(2):
                    pool.wait_ge(xT_stored[i], 16 * NBLK // 2)

            @block.vector
            def _(dve):
                nc.vector.memset(t["eps"][:, :], EPS)

                def copies(b):
                    if b >= 2:
                        dve.wait_ge(xT_stored[b % 2], 16 * (b // 2))
                        dve.wait_ge(squared, KD * (b - 1))
                        dve.wait_ge(h_done, KD * (b - 1))
                    for j in range(TB):
                        for half in range(2):
                            n = 2 * (TB * b + j) + half
                            dve.wait_ge(trans, n + 1)
                            nc.vector.tensor_copy(xT[b % 2][:, 4 * half:4 * half + 4, j * P:(j + 1) * P],
                                                  quad(pT[n % 4][:, :])).then_inc(copied, 1)

                copies(0)
                dve.wait_ge(g_in, 16)
                for b in range(NBLK):
                    if b + 1 < NBLK:
                        copies(b + 1)
                    dve.wait_ge(r_done, b + 1)
                    for k in range(KD):
                        n = KD * b + k
                        if n >= 2:
                            dve.wait_ge(lo_done, n - 1)
                        nc.vector.scalar_tensor_tensor(h[n % 2][:, :], xT[b % 2][:, k, :], g[:, k:k + 1],
                                                       rB[:, :], ALU.mult, ALU.mult).then_inc(h_done, 1)


def phase_project(nc, t, h_hi, h_lo):
    with Phase(nc, "B") as ph:
        w = ph.sb("w", [P, KD, P])
        w_hi, w_lo = ([ph.sb(f"{n}{i}", [P, KD, P], F32R) for i in range(2)] for n in ("w_hi", "w_lo"))
        w_ba = ph.sb("w_ba", [P, KD, 2 * DN_HEADS])
        ba_hi, ba_lo = (ph.sb(n, [P, KD, 2 * DN_HEADS], F32R) for n in ("ba_hi", "ba_lo"))
        stage = [ph.sb(f"stage{i}", [P, SEQ]) for i in range(2)]
        PAD = DN_CONV
        raw = ph.sb("raw", [P, PAD + SEQ])
        conv = [ph.sb(f"conv{i}", [P, SEQ]) for i in range(2)]
        cw = ph.sb("cw", [P, 12, DN_CONV])
        alog = ph.sb("alog", [P, DN_HEADS])
        dtb = ph.sb("dtb", [P, DN_HEADS])
        cw_flat = cw[:, :, :].rearrange("p g j -> p (g j)")
        expA = ph.sb("expA", [P, DN_HEADS])
        a_in, a_pos, a_abs, e_abs, ln_e = (
            ph.sb(s, [P, NT, DN_HEADS]) for s in ("a_in", "a_pos", "a_abs", "e_abs", "ln_e"))
        acc = [[ph.bank(f"acc{i}{j}") for j in range(NBLK)] for i in range(2)]
        def per_slot(name):
            return [ph.sem(f"{name}{i}") for i in range(2)]

        mm_done, evac_done, staged, stored = (per_slot(s) for s in ("mm_done", "evac_done", "staged", "stored"))
        split_begun, w_loaded, w_hi_done, w_split, ba_split = (ph.sem(s) for s in ("split_begun", "w_loaded", "w_hi_done", "w_split", "ba_split"))
        conv_step, conv_done, silu_done, sq_done, ssq_done, ln_done, r_done = (
            per_slot(s) for s in ("conv_step", "conv_done", "silu_done", "sq_done", "ssq_done", "ln_done", "r_done"))
        padded, misc_in, ba_done, ba_act, ba_dve = (
            ph.sem(s) for s in ("padded", "misc_in", "ba_done", "ba_act", "ba_dve"))
        ones = t["const"][:, K_ONE:K_ONE + P]
        w_d = t["w_in"].rearrange("o (k p) n -> p (o k) n", p=P)
        proj_d = t["proj_d"]
        QK, V, SBG, Z, GT = "qk", "v", "copy", ACT.Silu, ACT.Sigmoid
        runs = [(QK, C_DN, 4), (V, C_DN + 8 * P, 2), (SBG, 0, 6), (Z, C_Z, 2), (GT, C_Z + 4 * P, 8)]
        before = [sum(r[2] for r in runs[:i]) for i in range(len(runs))]
        RUNS = [(*r, b) for r, b in zip(runs, before)]

        with nc.Block() as block:

            @block.sync
            def _(sp):
                sp.dma_start(w_ba[:, :, :], w_d[:, :, C_BA:C_Z]).then_inc(misc_in, 16)
                for g in range(12):
                    sp.dma_start(cw[:, g, :], t["dn_conv_w"][0, :, g * P:(g + 1) * P].rearrange("j p -> p j")).then_inc(misc_in, 16)
                sp.dma_start(alog[:, :], t["dn_a_log"].to_broadcast([P, DN_HEADS])).then_inc(misc_in, 16)
                sp.dma_start(dtb[:, :], t["dn_dt_bias"].to_broadcast([P, DN_HEADS])).then_inc(misc_in, 16)

                def store(turn, s):
                    sp.wait_ge(staged[s], turn * NBLK + NBLK)
                    sp.dma_start(proj_d[ds(turn * 2 + s, 1), :, :], stage[s][:, :]).then_inc(stored[s], 16)

                for kind, col, turns, at in RUNS:
                    first = 1 if at == 0 else 0
                    if first:
                        for s in range(2):
                            sp.wait_ge(w_split, s)
                            sp.dma_start(w[:, :, :], w_d[:, :, col + s * P:col + (s + 1) * P]).then_inc(w_loaded, 16)
                    with sp.Fori(first, turns) as i:
                        for s in range(2):
                            sp.wait_ge(w_split, i * 2 + (2 * at + s))
                            sp.dma_start(w[:, :, :], w_d[:, :, ds(i * (2 * P) + (col + s * P), P)]).then_inc(w_loaded, 16)
                        for s in range(2):
                            store(i + (at - 1), s)
                for s in range(2):
                    store(NGRP // 2 - 1, s)
                for s in range(2):
                    sp.wait_ge(stored[s], 16 * NGRP // 2)

            @block.gpsimd
            def _(pool):
                pool.wait_ge(misc_in, 240)
                nc.gpsimd.tensor_copy(ba_hi[:, :, :], w_ba[:, :, :]).then_inc(ba_split, 1)
                pool.wait_ge(ba_split, 1)
                nc.gpsimd.tensor_tensor(ba_lo[:, :, :], w_ba[:, :, :], ba_hi[:, :, :].bitcast(F32), ALU.subtract).then_inc(ba_split, 1)
                with pool.Fori(0, NGRP // 2) as i:
                    for s in range(2):
                        pool.wait_ge(w_loaded, i * 32 + 16 * (s + 1))
                        pool.wait_ge(mm_done[s], i)
                        pool.sem_inc(split_begun, 1)
                        nc.gpsimd.tensor_copy(w_hi[s][:, :, :], w[:, :, :]).then_inc(w_hi_done, 1)
                        pool.wait_ge(w_hi_done, i * 2 + (s + 1))
                        nc.gpsimd.tensor_tensor(w_lo[s][:, :, :], w[:, :, :], w_hi[s][:, :, :].bitcast(F32),
                                                ALU.subtract).then_inc(w_split, 1)

            @block.tensor
            def _(pe):
                pe.wait_ge(ba_split, 2)
                for j in range(NT):
                    for k in range(KD):
                        for n, (x, y) in enumerate(((h_hi, ba_hi), (h_hi, ba_lo), (h_lo, ba_hi))):
                            last = nc.tensor.matmul(acc[1][3][:, j * 8:(j + 1) * 8], x[:, k, j * P:(j + 1) * P], y[:, k, :],
                                                    start=(k == 0 and n == 0), stop=(k == KD - 1 and n == 2))
                last.then_inc(ba_done, 1)
                pe.wait_ge(ba_dve, 1)
                for kind, col, turns, at in RUNS:
                    with pe.Fori(0, turns) as i:
                        for s in range(2):
                            pe.wait_ge(w_split, i * 2 + (2 * at + s + 1))
                            pe.wait_ge((evac_done if kind in (QK, V) else staged)[s], i * NBLK + NBLK * at)
                            if kind == QK:
                                pe.wait_ge(ln_done[s], i * NBLK)
                            elif kind == V:
                                pe.wait_ge(ln_done[s], NBLK * at)
                            for k in range(KD):
                                for n, (x, y) in enumerate(((w_hi, h_hi), (w_hi, h_lo), (w_lo, h_hi))):
                                    for j in range(NBLK):
                                        last = nc.tensor.matmul(acc[s][j][:, :], x[s][:, k, :], y[:, k, j * BLK:(j + 1) * BLK],
                                                                start=(k == 0 and n == 0), stop=(k == KD - 1 and n == 2))
                            last.then_inc(mm_done[s], 1)
                        if kind == QK:
                            for s in range(2):
                                pe.wait_ge(evac_done[s], i * NBLK + NBLK)
                                for j in range(NBLK):
                                    pe.wait_ge(sq_done[s], i * NBLK + (j + 1))
                                    nc.tensor.matmul(acc[s][j][:, :], ones, stage[s][:, j * BLK:(j + 1) * BLK],
                                                     start=True, stop=True).then_inc(ssq_done[s], 1)

            @block.scalar
            def _(act):
                b_cols = quad(acc[1][3][:, 0:NT * 8], 8)[:, :, 0:DN_HEADS]
                act.wait_ge(ba_done, 1)
                nc.scalar.activation(t["beta"][:, :, :], b_cols, ACT.Sigmoid).then_inc(ba_act, 1)
                act.wait_ge(misc_in, 240)
                nc.scalar.activation(expA[:, :], alog[:, :], ACT.Exp).then_inc(ba_act, 1)
                act.wait_ge(ba_dve, 3)
                nc.scalar.activation(e_abs[:, :, :], a_abs[:, :, :], ACT.Exp, scale=-1.0).then_inc(ba_act, 1)
                act.wait_ge(ba_act, 3)
                nc.scalar.activation(ln_e[:, :, :], e_abs[:, :, :], ACT.Ln, bias=1.0).then_inc(ba_act, 1)
                act.wait_ge(padded, 1)
                for kind, col, turns, at in RUNS:
                    with act.Fori(0, turns) as i:
                        for s in range(2):
                            act.wait_ge(mm_done[s], i + (at + 1))
                            if kind in (QK, V):
                                act.wait_ge(conv_done[1 - s], i + (at + s))
                                for j in range(NBLK):
                                    nc.scalar.activation(raw[:, PAD + j * BLK:PAD + (j + 1) * BLK], acc[s][j][:, :],
                                                         ACT.Copy).then_inc(evac_done[s], 1)
                                act.wait_ge(conv_done[s], i + (at + 1))
                                act.wait_ge(stored[s], i * 16 + 16 * at)
                                for j in range(NBLK):
                                    part = slice(j * BLK, (j + 1) * BLK)
                                    if kind == V:
                                        nc.scalar.activation(stage[s][:, part], conv[s][:, part],
                                                             ACT.Silu).then_inc(staged[s], 1)
                                    else:
                                        nc.scalar.activation(conv[s][:, part], conv[s][:, part],
                                                             ACT.Silu).then_inc(silu_done[s], 1)
                                        act.wait_ge(silu_done[s], i * NBLK + (j + 1))
                                        nc.scalar.activation(stage[s][:, part], conv[s][:, part],
                                                             ACT.Square).then_inc(sq_done[s], 1)
                            else:
                                act.wait_ge(stored[s], i * 16 + 16 * at)
                                for j in range(NBLK):
                                    nc.scalar.activation(stage[s][:, j * BLK:(j + 1) * BLK], acc[s][j][:, :],
                                                         ACT.Copy if kind == SBG else kind).then_inc(staged[s], 1)
                        if kind == QK:
                            for s in range(2):
                                for j in range(NBLK):
                                    part = slice(j * BLK, (j + 1) * BLK)
                                    act.wait_ge(ssq_done[s], i * NBLK + (j + 1))
                                    nc.scalar.activation(stage[s][:, part], acc[s][j][:, :], ACT.Ln,
                                                         bias=t["eps"][:, 0:1]).then_inc(ln_done[s], 1)
                                for j in range(NBLK):
                                    part = slice(j * BLK, (j + 1) * BLK)
                                    act.wait_ge(ln_done[s], i * NBLK + (j + 1))
                                    nc.scalar.activation(stage[s][:, part], stage[s][:, part], ACT.Exp,
                                                         scale=-0.5).then_inc(r_done[s], 1)

            @block.vector
            def _(dve):
                nc.vector.memset(raw[:, 0:PAD], 0.0).then_inc(padded, 1)
                a_cols = quad(acc[1][3][:, 0:NT * 8], 8)[:, :, DN_HEADS:2 * DN_HEADS]
                dve.wait_ge(misc_in, 240)
                dve.wait_ge(ba_done, 1)
                dve.wait_ge(ba_act, 1)
                nc.vector.tensor_tensor(a_in[:, :, :], a_cols, bc_mid(dtb[:, :], NT), ALU.add).then_inc(ba_dve, 1)
                dve.wait_ge(ba_dve, 1)
                nc.vector.tensor_scalar(a_pos[:, :, :], a_in[:, :, :], 0.0, None, ALU.max).then_inc(ba_dve, 1)
                nc.vector.scalar_tensor_tensor(a_abs[:, :, :], a_in[:, :, :], -1.0, a_in[:, :, :], ALU.mult, ALU.max).then_inc(ba_dve, 1)
                dve.wait_ge(ba_act, 4)
                dve.wait_ge(ba_dve, 3)
                nc.vector.tensor_tensor(a_in[:, :, :], a_pos[:, :, :], ln_e[:, :, :], ALU.add).then_inc(ba_dve, 1)
                dve.wait_ge(ba_dve, 4)
                nc.vector.scalar_tensor_tensor(t["glog"][:, :, :], a_in[:, :, :], -1.0, bc_mid(expA[:, :], NT),
                                               ALU.mult, ALU.mult).then_inc(ba_dve, 1)
                for kind, col, turns, at in RUNS[0:2]:
                    with dve.Fori(0, turns) as i:
                        for s in range(2):
                            dve.wait_ge(evac_done[s], i * NBLK + NBLK * (at + 1))
                            dve.wait_ge(staged[s], i * NBLK + NBLK * at)
                            for j in range(DN_CONV):
                                src = raw[:, PAD - DN_CONV + 1 + j:PAD - DN_CONV + 1 + j + SEQ]
                                wj = cw_flat[:, ds(i * (2 * DN_CONV) + ((2 * at + s) * DN_CONV + j), 1)]
                                if j == 0:
                                    ins = nc.vector.tensor_scalar(conv[s][:, :], src, wj, None, ALU.mult)
                                else:
                                    dve.wait_ge(conv_step[s], i * 3 + (3 * at + j))
                                    ins = nc.vector.scalar_tensor_tensor(conv[s][:, :], src, wj, conv[s][:, :],
                                                                         ALU.mult, ALU.add)
                                ins.then_inc(conv_done[s] if j == DN_CONV - 1 else conv_step[s], 1)
                        if kind == QK:
                            for s in range(2):
                                for j in range(NBLK):
                                    part = slice(j * BLK, (j + 1) * BLK)
                                    dve.wait_ge(r_done[s], i * NBLK + (j + 1))
                                    nc.vector.tensor_tensor(stage[s][:, part], conv[s][:, part], stage[s][:, part],
                                                            ALU.mult).then_inc(staged[s], 1)


def phase_mix(nc, t):
    with Phase(nc, "C") as ph:
        qf, kf, vf = (ph.sb(s, [P, SEQ]) for s in ("qf", "kf", "vf"))
        q2, k2_hi, k2_lo = (ph.sb(s, [P, SEQ], F32R) for s in ("q2", "k2_hi", "k2_lo"))
        vn = ph.sb("vn", [P, NT, SB_DIM])
        oT = ph.sb("oT", [SB_DIM, SEQ])
        NZB, NRING = 2, 4
        keep = [ph.sb(f"keep{i}", [P, BLK]) for i in range(NRING)]
        sig = [ph.sb(f"sig{i}", [P, BLK]) for i in range(NRING)]
        prod = [ph.sb(f"prod{i}", [P, SEQ + 4]) for i in range(2)]
        att = [ph.sb(f"att{i}", [P, BLK]) for i in range(NRING)]
        attT = [ph.sb(f"attT{i}", [P, BLK]) for i in range(2)]
        bz = [ph.bank(f"z{i}") for i in range(NZB)]
        bt, bo = ph.bank("t"), ph.bank("o")
        (q_in, k_in, v_in, hi_done, split, turn, v_trans, v_copied, z_done, keep_done, sig_done, scan_done, att_done, trans_done,
         attT_done, av_done, o_copied, one_set) = (
            ph.sem(s) for s in ("q_in", "k_in", "v_in", "hi_done", "split", "turn", "v_trans", "v_copied", "z_done", "keep_done", "sig_done",
                                "scan_done", "att_done", "trans_done", "attT_done", "av_done", "o_copied",
                                "one_set"))
        o_store, o_stored = ph.pool_dma_sem("o_store"), ph.pool_dma_sem("o_stored")
        neg = t["const"][:, K_NEG:K_NEG + P]
        proj, o_d = t["proj_d"], t["o_d"]
        o_heads = o_d.rearrange("g (a p) n -> (g a) p n", p=SB_DIM)
        END = SEQ
        HALF = SB_DIM
        low_rows, high_rows = slice(0, HALF), slice(HALF, P)

        steps = []
        for i in range(NT):
            n = (i + 1) * P
            starts = list(range(0, n, BLK))[::-1]
            steps += [(i, k0, min(BLK, n - k0), k0 == starts[0], k0 == 0) for k0 in starts]
        NS = len(steps)
        AHEAD = 2
        NOQ = NT // 4
        NVT = NT * SB_DIM // BLK
        SPREAD = NS // 2

        H, W = DN_HEADS, DN_HEADS * P
        SCALE = DN_DIM ** -0.5
        L = NLEV - 1

        def tile(name):
            return ph.sb("d_" + name, [P, W])

        qkvT = ph.sb("d_qkvT", [P, 3 * W])
        zT, glB, E, gN, gT, EG, A, AT, X, XT, Y = (tile(n) for n in ("zT", "glB", "E", "gN", "gT", "EG", "A", "AT", "X", "XT", "Y"))
        ATm = [tile(f"ATm{l}") for l in range(1, NLEV)]
        qkT, qd, kd, vb, rhs, vnew, Sdec, o_raw, o_sq, rB, o_out = (
            tile(n) for n in ("qkT", "qd", "kd", "vb", "rhs", "vnew", "Sdec", "o_raw", "o_sq", "rB", "o_out"))
        S = [tile("S0"), tile("S1")]
        gc, gl, eg, egl, kdec, be = (ph.sb(s, [P, NT * H]) for s in ("gc", "gl", "eg", "egl", "kdec", "be"))
        gdn = ph.sb("gdn", [P, 1])
        b = [ph.bank(f"b{j}") for j in range(4)]
        const = t["const"]
        ident, ones = const[:, K_ID:K_ID + P], const[:, K_ONE:K_ONE + P]
        inc, low = const[:, K_INC:K_INC + P], const[:, K_LOW:K_LOW + P]

        def lev(l, transposed):
            at = K_LEV + (2 * l + transposed) * P
            return const[:, at:at + P]

        glog, beta = (t[s][:, :, :].rearrange("p t h -> p (t h)") for s in ("glog", "beta"))
        proj_g = t["proj_d"].rearrange("g p n -> p g n")
        o_g = t["o_d"].rearrange("g p n -> p g n")
        names = ("in", "z_in", "gdn_in", "g_sum", "g_copied", "g_exp", "g_dec", "glB_ok", "GR_ok", "E_ok", "EG_ok", "Emm_ok", "gNe_ok",
                 "gTe_ok", "gNl_ok", "gN_ok", "gT_ok", "KK_ok", "KQ_ok", "Tk_ok", "Tv_ok", "A_ok", "qkT_ok", "qd_ok", "kd_ok",
                 "vb_ok", "TA_ok", "AT_ok", "ATm_ok", "Xm_ok", "X_ok", "Y_mm", "Y_ok", "P2_mm", "P3_mm", "lev_ok",
                 "R_mm", "Rb_ok", "rhs_ok", "vn_mm", "vn_ok", "Sdec_ok", "dS_mm", "S_ok", "O_mm", "o_ok", "osq_ok",
                 "oss_mm", "oln_ok", "or_ok", "on_ok", "o_done")
        s = {n: ph.sem("d_" + n) for n in names}

        Y_AT = {5 + 2 * (l - 1): l for l in range(1, NLEV)}
        P_AT = {6 + 2 * (l - 1): l for l in range(1, NLEV)}
        R_AT, A_AT, TA_AT, VN_AT, DS_AT, OSS_AT = 2, 2, 4, 17, 18, 19
        assert OSS_AT < SPREAD

        def hs(tile, h, at=0):
            return tile[:, at + h * P:at + (h + 1) * P]

        with nc.Block() as block:

            @block.sync
            def _(sp):
                sp.dma_start(gdn[:, :], t["dn_norm_g"].rearrange("o p -> p o")).then_inc(s["gdn_in"], 16)
                with sp.Fori(0, SB_HEADS // 2) as pair:
                    for h in range(2):
                        rows = slice(h * HALF, (h + 1) * HALF)
                        head = pair * 2 + h
                        sp.wait_ge(split, head * 3)
                        for half in (low_rows, high_rows):
                            sp.dma_start(qf[half, :], proj[ds(pair + G_SBQ, 1), rows, :]).then_inc(q_in, 16)
                            sp.dma_start(kf[half, :], proj[ds(pair + G_SBK, 1), rows, :]).then_inc(k_in, 16)
                        sp.wait_ge(v_trans, head * NVT)
                        sp.dma_start(vf[low_rows, :], proj[ds(pair + G_SBV, 1), rows, :]).then_inc(v_in, 16)
                        for c in range(2):
                            chunk = head * 2 + c
                            sp.wait_ge(s["R_mm"], chunk)
                            sp.wait_ge(s["qd_ok"], chunk)
                            cols = ds(pair * (4 * P) + (2 * h + c) * P, P)
                            sp.dma_start(quad(qkvT[:, :]), proj_g[:, G_DNQ:G_DNQ + 12, cols]).then_inc(s["in"], 16)
                            sp.wait_ge(s["o_done"], chunk)
                            sp.dma_start(quad(zT[:, :]), proj_g[:, G_Z:G_Z + H, cols]).then_inc(s["z_in"], 16)

            @block.tensor
            def _(pe):
                nc.tensor.matmul(b[0][:, 0:NT * H], inc, glog, start=True, stop=True)
                nc.tensor.matmul(b[0][:, NT * H:2 * NT * H], ones, glog, start=True, stop=True).then_inc(s["g_sum"], 1)
                pe.wait_ge(s["g_copied"], 2)
                with pe.Fori(0, SB_HEADS) as head:

                    def heads(j, lhs, rhs_of):
                        for h in range(H):
                            last = nc.tensor.matmul(b[j][:, h * P:(h + 1) * P], lhs(h), rhs_of(h), start=True, stop=True)
                        return last

                    def turned(j, src):
                        for h in range(H):
                            last = nc.tensor.transpose(hs(b[j], h), src(h), ident)
                        return last

                    kT = lambda h: hs(qkvT, h, W)

                    def delta(at, c):
                        before, now = head * 2 + c, head * 2 + (c + 1)
                        if at == 0:
                            pe.wait_ge(s["in"], head * 32 + 16 * (c + 1))
                            pe.wait_ge(s["vn_ok"], before)
                            heads(1, kT, kT).then_inc(s["KK_ok"], 1)
                            pe.wait_ge(s["S_ok"], before + 1)
                            heads(2, kT, lambda h: hs(qkvT, h)).then_inc(s["KQ_ok"], 1)
                            pe.wait_ge(s["o_ok"], before)
                            turned(3, kT).then_inc(s["Tk_ok"], 1)
                            pe.wait_ge(s["glB_ok"], now)
                            pe.wait_ge(s["oln_ok"], before)
                            heads(0, lambda h: hs(glB, h), lambda h: inc).then_inc(s["GR_ok"], 1)
                        elif at == 1:
                            pe.wait_ge(s["E_ok"], now)
                            pe.wait_ge(s["EG_ok"], now)
                            turned(0, lambda h: hs(qkvT, h, 2 * W)).then_inc(s["Tv_ok"], 1)
                        elif at == R_AT:
                            pe.wait_ge(s["vb_ok"], now)
                            heads(0, kT, lambda h: hs(S[c], h)).then_inc(s["R_mm"], 1)
                        elif at == TA_AT:
                            pe.wait_ge(s["A_ok"], now)
                            turned(1, lambda h: hs(A, h)).then_inc(s["TA_ok"], 1)
                        elif at in Y_AT:
                            l = Y_AT[at]
                            pe.wait_ge(s["ATm_ok"], head * (2 * L) + c * L + l)
                            if l == 1:
                                pe.wait_ge(s["X_ok"], head * 4 + 2 * c + 2)
                                pe.wait_ge(s["qkT_ok"], now)
                            else:
                                pe.wait_ge(s["lev_ok"], head * (4 * L - 2) + (2 * L - 1) * c + 2 * (l - 1))
                            heads(2, lambda h: hs(ATm[l - 1], h), lambda h: hs(X, h)).then_inc(s["Y_mm"], 1)
                        elif at in P_AT:
                            l = P_AT[at]
                            pe.wait_ge(s["Y_ok"], head * (2 * L) + c * L + l)
                            if l == 1:
                                pe.wait_ge(s["kd_ok"], now)
                                pe.wait_ge(s["AT_ok"], now)
                            if l < NLEV - 1:
                                heads(3, lambda h: hs(XT, h), lambda h: hs(Y, h)).then_inc(s["P2_mm"], 1)
                            heads(1, lambda h: hs(Y, h), lambda h: hs(XT, h)).then_inc(s["P3_mm"], 1)
                        elif at == VN_AT:
                            pe.wait_ge(s["rhs_ok"], now)
                            pe.wait_ge(s["lev_ok"], head * (4 * L - 2) + (2 * L - 1) * (c + 1))
                            heads(1, lambda h: hs(XT, h), lambda h: hs(rhs, h)).then_inc(s["vn_mm"], 1)
                        elif at == DS_AT:
                            pe.wait_ge(s["vn_ok"], now)
                            heads(2, lambda h: hs(kd, h), lambda h: hs(vnew, h)).then_inc(s["dS_mm"], 1)
                            for h in range(H):
                                nc.tensor.matmul(hs(b[3], h), hs(S[c], h), hs(qd, h), start=True, stop=False)
                                last = nc.tensor.matmul(hs(b[3], h), hs(vnew, h), hs(qkT, h), start=False, stop=True)
                            last.then_inc(s["O_mm"], 1)
                        elif at == OSS_AT:
                            pe.wait_ge(s["osq_ok"], now)
                            pe.wait_ge(s["Rb_ok"], now)
                            nc.tensor.matmul(b[0][:, :], ones, o_sq[:, :], start=True, stop=True).then_inc(s["oss_mm"], 1)

                    def scores(n):
                        i, k0, w, first, last = steps[n]
                        if n >= NZB:
                            pe.wait_ge(sig_done, head * NS + (n + 1 - NZB))
                            pe.wait_ge(keep_done, head * NS + (n + 1 - NZB))
                        tile_q = q2[:, i * P:(i + 1) * P]
                        nc.tensor.matmul(bz[n % NZB][:, 0:w], tile_q, k2_hi[:, k0:k0 + w], start=True, stop=False)
                        ins = nc.tensor.matmul(bz[n % NZB][:, 0:w], tile_q, k2_lo[:, k0:k0 + w], start=False, stop=not first)
                        if first:
                            ins = nc.tensor.matmul(bz[n % NZB][:, w - P:w], ident, neg, start=False, stop=True)
                        ins.then_inc(z_done, 1)

                    def transposes(n):
                        w = steps[n][2]
                        pe.wait_ge(att_done, head * NS + (n + 1))
                        if n >= 1:
                            pe.wait_ge(attT_done, head * NS + n)
                        else:
                            pe.wait_ge(v_copied, head * NVT + NVT)
                        for m in range(w // P):
                            ins = nc.tensor.transpose(bt[:, m * P:(m + 1) * P], att[n % NRING][:, m * P:(m + 1) * P], ident)
                        ins.then_inc(trans_done, 1)

                    def values(n):
                        i, k0, w, first, last = steps[n]
                        pe.wait_ge(attT_done, head * NS + (n + 1))
                        if first and i % 4 == 0:
                            pe.wait_ge(o_copied, head * NOQ + i // 4)
                        for m in range(w // P):
                            ins = nc.tensor.matmul(bo[low_rows, (i % 4) * P:(i % 4 + 1) * P], vn[:, k0 // P + m, :],
                                                   attT[n % 2][:, m * P:(m + 1) * P],
                                                   start=first and m == 0, stop=last and m == w // P - 1)
                        ins.then_inc(av_done, 1)

                    pe.wait_ge(split, head * 3 + 3)
                    pe.wait_ge(sig_done, head * NS)
                    for n in range(AHEAD):
                        scores(n)
                    pe.wait_ge(v_in, head * 16 + 16)
                    for j in range(NVT):
                        if j == 0:
                            pe.wait_ge(attT_done, head * NS)
                        else:
                            pe.wait_ge(v_copied, head * NVT + j)
                        pe.sem_inc(turn, 1)
                        for m in range(NT // NVT):
                            at = j * (NT // NVT) + m
                            last = nc.tensor.transpose(bt[:, m * SB_DIM:(m + 1) * SB_DIM], vf[low_rows, at * P:(at + 1) * P],
                                                       ident[low_rows, 0:SB_DIM])
                        last.then_inc(v_trans, 1)
                    for n in range(NS):
                        if n + AHEAD < NS:
                            scores(n + AHEAD)
                        transposes(n)
                        if n >= 1:
                            values(n - 1)
                        delta(n % SPREAD, n // SPREAD)
                    values(NS - 1)

            def evacuate(act, head, n):
                i = steps[n][0]
                act.wait_ge(av_done, head * NS + (n + 1))
                nc.scalar.activation(oT[:, (i - 3) * P:(i + 1) * P], bo[low_rows, :], ACT.Copy).then_inc(o_copied, 1)

            @block.scalar
            def _(act):
                act.wait_ge(s["g_copied"], 2)
                nc.scalar.activation(eg[:, :], gc[:, :], ACT.Exp).then_inc(s["g_exp"], 1)
                nc.scalar.activation(egl[:, :], gl[:, :], ACT.Exp).then_inc(s["g_exp"], 1)
                act.wait_ge(s["g_dec"], 1)
                nc.scalar.activation(kdec[:, :], kdec[:, :], ACT.Exp).then_inc(s["g_exp"], 1)
                with act.Fori(0, SB_HEADS) as head:

                    def delta(at, c):
                        before, now = head * 2 + c, head * 2 + (c + 1)
                        if at == 0:
                            act.wait_ge(s["E_ok"], now)
                            act.wait_ge(s["qd_ok"], before)
                            nc.scalar.activation(EG[:, :], b[0][:, :], ACT.Exp).then_inc(s["EG_ok"], 1)
                            act.wait_ge(s["Emm_ok"], head * 4 + 2 * c + 2)
                            nc.scalar.activation(gN[:, :], gN[:, :], ACT.Exp, scale=-1.0).then_inc(s["gNe_ok"], 1)
                            nc.scalar.activation(gT[:, :], gT[:, :], ACT.Exp).then_inc(s["gTe_ok"], 1)
                        elif at in Y_AT:
                            l = Y_AT[at]
                            act.wait_ge(s["Y_mm"], head * (2 * L) + c * L + l)
                            act.wait_ge(s["P3_mm"], head * (2 * L) + c * L + (l - 1))
                            nc.scalar.activation(Y[:, :], b[2][:, :], ACT.Copy).then_inc(s["Y_ok"], 1)
                        elif at == VN_AT:
                            act.wait_ge(s["vn_mm"], now)
                            nc.scalar.activation(vnew[:, :], b[1][:, :], ACT.Copy).then_inc(s["vn_ok"], 1)
                        elif at == DS_AT:
                            act.wait_ge(s["O_mm"], now)
                            act.wait_ge(s["on_ok"], before)
                            nc.scalar.activation(o_raw[:, :], b[3][:, :], ACT.Copy).then_inc(s["o_ok"], 1)
                            act.wait_ge(s["o_ok"], now)
                            nc.scalar.activation(o_sq[:, :], o_raw[:, :], ACT.Square).then_inc(s["osq_ok"], 1)
                        elif at == OSS_AT:
                            act.wait_ge(s["oss_mm"], now)
                            nc.scalar.activation(rB[:, :], b[0][:, :], ACT.Ln, bias=t["eps"][:, 0:1],
                                                 scale=1.0 / DN_DIM).then_inc(s["oln_ok"], 1)
                            act.wait_ge(s["oln_ok"], now)
                            nc.scalar.activation(rB[:, :], rB[:, :], ACT.Exp, scale=-0.5).then_inc(s["or_ok"], 1)

                    def weights(n):
                        w = steps[n][2]
                        act.wait_ge(z_done, head * NS + (n + 1))
                        if n >= NRING:
                            act.wait_ge(scan_done, head * NS + (n + 1 - NRING))
                            act.wait_ge(att_done, head * NS + (n + 1 - NRING))
                        else:
                            act.wait_ge(att_done, head * NS)
                        nc.scalar.activation(keep[n % NRING][:, 0:w], bz[n % NZB][:, 0:w], ACT.Sigmoid,
                                             scale=-SB_DIM ** -0.5).then_inc(keep_done, 1)
                        nc.scalar.activation(sig[n % NRING][:, 0:w], bz[n % NZB][:, 0:w], ACT.Sigmoid,
                                             scale=SB_DIM ** -0.5).then_inc(sig_done, 1)

                    act.wait_ge(z_done, head * NS)
                    act.wait_ge(q_in, head * 32 + 32)
                    nc.scalar.activation(q2[:, :], qf[:, :], ACT.Copy).then_inc(hi_done, 1)
                    act.wait_ge(k_in, head * 32 + 32)
                    nc.scalar.activation(k2_hi[:, :], kf[:, :], ACT.Copy).then_inc(hi_done, 1)
                    for n in range(AHEAD):
                        weights(n)
                    act.wait_ge(o_store, head * 16)
                    for n in range(NS):
                        if n + AHEAD < NS:
                            weights(n + AHEAD)
                        if n >= 2 and steps[n - 2][4] and steps[n - 2][0] % 4 == 3:
                            evacuate(act, head, n - 2)
                        delta(n % SPREAD, n // SPREAD)
                    evacuate(act, head, NS - 1)

            @block.gpsimd
            def _(pool):
                nc.gpsimd.memset(S[0][:, :], 0.0).then_inc(s["S_ok"], 1)
                with pool.Fori(0, SB_HEADS) as head:

                    def cols(ap, c):
                        return ap[:, ds(head * (2 * H) + c * H, H)]

                    def delta_first(at, c):
                        before = head * 2 + c
                        if at == 0:
                            pool.wait_ge(s["GR_ok"], before)
                            nc.gpsimd.tensor_copy(quad(glB[:, :]), bc(cols(glog, c), P)).then_inc(s["glB_ok"], 1)

                    def delta(at, c):
                        before, now = head * 2 + c, head * 2 + (c + 1)
                        if at == 1:
                            pool.wait_ge(s["gNe_ok"], now)
                            nc.gpsimd.tensor_tensor(quad(gN[:, :]), quad(gN[:, :]), bc_mid(low, H), ALU.mult).then_inc(s["gNl_ok"], 1)
                            pool.wait_ge(s["gTe_ok"], now)
                            nc.gpsimd.tensor_tensor(quad(gT[:, :]), quad(gT[:, :]), bc_mid(inc, H), ALU.mult).then_inc(s["gT_ok"], 1)
                            pool.wait_ge(s["gNl_ok"], now)
                            nc.gpsimd.tensor_tensor(quad(gN[:, :]), quad(gN[:, :]), bc(cols(beta, c), P), ALU.mult).then_inc(s["gN_ok"], 1)
                        elif at == 3:
                            pool.wait_ge(s["g_exp"], 3)
                            pool.wait_ge(s["S_ok"], before + 1)
                            nc.gpsimd.tensor_tensor(quad(Sdec[:, :]), quad(S[c][:, :]), bc(cols(egl, c), P), ALU.mult).then_inc(s["Sdec_ok"], 1)
                        elif TA_AT <= at < TA_AT + L // 2:
                            pool.wait_ge(s["AT_ok"], now)
                            for l in (2 * (at - TA_AT) + 1, 2 * (at - TA_AT) + 2):
                                nc.gpsimd.tensor_tensor(quad(ATm[l - 1][:, :]), quad(AT[:, :]), bc_mid(lev(l, 1), H),
                                                        ALU.mult).then_inc(s["ATm_ok"], 1)
                        elif at == OSS_AT:
                            pool.wait_ge(s["on_ok"], now)
                            pool.wait_ge(s["z_in"], head * 32 + 16 * (c + 1))
                            nc.gpsimd.tensor_tensor(o_out[:, :], o_out[:, :], zT[:, :], ALU.mult).then_inc(s["o_done"], 1)
                            pool.wait_ge(s["o_done"], now)
                            pool.dma_start(o_g[:, H:2 * H, ds(head * (2 * P) + c * P, P)], quad(o_out[:, :])).then_inc(o_stored, 16)

                    def weigh(n):
                        i, k0, w, first, last = steps[n]
                        off = END - (i + 1) * P + k0
                        pool.wait_ge(sig_done, head * NS + (n + 1))
                        pool.wait_ge(scan_done, head * NS + (n + 1))
                        pool.wait_ge(trans_done, head * NS + max(0, n + 1 - NRING))
                        nc.gpsimd.tensor_tensor(att[n % NRING][:, 0:w], sig[n % NRING][:, 0:w],
                                                prod[i % 2][:, off + 1:off + 1 + w], ALU.mult).then_inc(att_done, 1)

                    for n in range(AHEAD):
                        weigh(n)
                    for n in range(NS):
                        delta_first(n % SPREAD, n // SPREAD)
                        if n + AHEAD < NS:
                            weigh(n + AHEAD)
                        delta(n % SPREAD, n // SPREAD)
                    pool.wait_ge(o_copied, head * NOQ + NOQ)
                    pool.dma_start(o_heads[ds(head, 1), :, :], oT[:, :]).then_inc(o_store, 16)
                pool.wait_ge(o_store, 16 * SB_HEADS)
                pool.wait_ge(o_stored, 16 * NT)

            @block.vector
            def _(dve):
                dve.wait_ge(s["g_sum"], 1)
                nc.vector.tensor_copy(gc[:, :], b[0][:, 0:NT * H]).then_inc(s["g_copied"], 1)
                nc.vector.tensor_copy(gl[:, :], b[0][:, NT * H:2 * NT * H]).then_inc(s["g_copied"], 1)
                dve.wait_ge(s["g_copied"], 2)
                nc.vector.tensor_tensor(kdec[:, :], gl[:, :], gc[:, :], ALU.subtract).then_inc(s["g_dec"], 1)
                dve.wait_ge(s["g_exp"], 3)
                nc.vector.tensor_tensor(be[:, :], beta, eg[:, :], ALU.mult).then_inc(s["g_dec"], 1)
                dve.wait_ge(s["g_dec"], 2)
                dve.wait_ge(s["gdn_in"], 16)
                for j in range(2):
                    nc.vector.memset(prod[j][:, END:END + 1], 1.0).then_inc(one_set, 1)
                dve.wait_ge(one_set, 2)
                with dve.Fori(0, SB_HEADS) as head:

                    def cols(ap, c):
                        return bc(ap[:, ds(head * (2 * H) + c * H, H)], P)

                    def delta(at, c):
                        v = nc.vector
                        before, now = head * 2 + c, head * 2 + (c + 1)
                        if at == 0:
                            dve.wait_ge(s["Tk_ok"], now)
                            dve.wait_ge(s["dS_mm"], before)
                            v.tensor_tensor(quad(kd[:, :]), quad(b[3][:, :]), cols(kdec, c), ALU.mult).then_inc(s["kd_ok"], 1)
                            dve.wait_ge(s["GR_ok"], now)
                            v.tensor_tensor(quad(E[:, :]), quad(b[0][:, :]), cols(gc, c), ALU.subtract).then_inc(s["E_ok"], 1)
                            dve.wait_ge(s["E_ok"], now)
                            v.tensor_scalar(gN[:, :], E[:, :], 0.0, None, ALU.max).then_inc(s["Emm_ok"], 1)
                            v.tensor_scalar(gT[:, :], E[:, :], 0.0, None, ALU.min).then_inc(s["Emm_ok"], 1)
                        elif at == 1:
                            dve.wait_ge(s["EG_ok"], now)
                            dve.wait_ge(s["O_mm"], before)
                            v.scalar_tensor_tensor(qd[:, :], qkvT[:, 0:W], SCALE, EG[:, :], ALU.mult, ALU.mult).then_inc(s["qd_ok"], 1)
                            dve.wait_ge(s["Tv_ok"], now)
                            v.tensor_tensor(quad(vb[:, :]), quad(b[0][:, :]), cols(beta, c), ALU.mult).then_inc(s["vb_ok"], 1)
                        elif at == A_AT:
                            dve.wait_ge(s["KK_ok"], now)
                            dve.wait_ge(s["gN_ok"], now)
                            v.tensor_tensor(A[:, :], b[1][:, :], gN[:, :], ALU.mult).then_inc(s["A_ok"], 1)
                            dve.wait_ge(s["KQ_ok"], now)
                            dve.wait_ge(s["gT_ok"], now)
                            v.scalar_tensor_tensor(qkT[:, :], b[2][:, :], SCALE, gT[:, :], ALU.mult, ALU.mult).then_inc(s["qkT_ok"], 1)
                        elif at == 3:
                            dve.wait_ge(s["R_mm"], now)
                            v.tensor_tensor(quad(rhs[:, :]), quad(b[0][:, :]), cols(be, c), ALU.mult).then_inc(s["Rb_ok"], 1)
                            dve.wait_ge(s["Rb_ok"], now)
                            v.tensor_tensor(rhs[:, :], vb[:, :], rhs[:, :], ALU.subtract).then_inc(s["rhs_ok"], 1)
                        elif at == TA_AT:
                            dve.wait_ge(s["TA_ok"], now)
                            v.tensor_copy(AT[:, :], b[1][:, :]).then_inc(s["AT_ok"], 1)
                            dve.wait_ge(s["AT_ok"], now)
                            v.tensor_tensor(quad(XT[:, :]), quad(AT[:, :]), bc_mid(lev(0, 1), H), ALU.mult).then_inc(s["Xm_ok"], 1)
                            v.tensor_tensor(quad(X[:, :]), quad(A[:, :]), bc_mid(lev(0, 0), H), ALU.mult).then_inc(s["Xm_ok"], 1)
                            dve.wait_ge(s["Xm_ok"], head * 4 + 2 * c + 2)
                            for y in (XT, X):
                                v.tensor_tensor(quad(y[:, :]), bc_mid(ident, H), quad(y[:, :]), ALU.subtract).then_inc(s["X_ok"], 1)
                        elif at in P_AT:
                            l = P_AT[at]
                            if l < NLEV - 1:
                                dve.wait_ge(s["P2_mm"], head * (2 * L - 2) + c * (L - 1) + l)
                                v.tensor_tensor(X[:, :], X[:, :], b[3][:, :], ALU.subtract).then_inc(s["lev_ok"], 1)
                            dve.wait_ge(s["P3_mm"], head * (2 * L) + c * L + l)
                            v.tensor_tensor(XT[:, :], XT[:, :], b[1][:, :], ALU.subtract).then_inc(s["lev_ok"], 1)
                        elif at == DS_AT:
                            dve.wait_ge(s["dS_mm"], now)
                            dve.wait_ge(s["Sdec_ok"], now)
                            v.tensor_tensor(S[1 - c][:, :], Sdec[:, :], b[2][:, :], ALU.add).then_inc(s["S_ok"], 1)
                        elif at == OSS_AT:
                            dve.wait_ge(s["or_ok"], now)
                            dve.wait_ge(o_stored, before * 16)
                            v.scalar_tensor_tensor(o_out[:, :], o_raw[:, :], gdn[:, 0:1], rB[:, :],
                                                   ALU.mult, ALU.mult).then_inc(s["on_ok"], 1)

                    def scan(n):
                        i, k0, w, first, last = steps[n]
                        off = END - (i + 1) * P + k0
                        dve.wait_ge(keep_done, head * NS + (n + 1))
                        dve.wait_ge(scan_done, head * NS + n)
                        if first:
                            m = next((m for m in range(n - 1, -1, -1) if steps[m][0] == i - 2), -1)
                            dve.wait_ge(att_done, head * NS + (m + 1))
                        nc.vector.tensor_tensor_scan(prod[i % 2][:, off:off + w][:, ::-1], keep[n % NRING][:, 0:w][:, ::-1],
                                                     keep[n % NRING][:, 0:w][:, ::-1], prod[i % 2][:, off + w:off + w + 1],
                                                     ALU.mult, ALU.bypass).then_inc(scan_done, 1)

                    def copy(n):
                        w = steps[n][2]
                        dve.wait_ge(trans_done, head * NS + (n + 1))
                        dve.wait_ge(av_done, head * NS + max(0, n - 1))
                        nc.vector.tensor_copy(attT[n % 2][:, 0:w], bt[:, 0:w]).then_inc(attT_done, 1)

                    dve.wait_ge(hi_done, head * 2 + 1)
                    nc.vector.tensor_tensor(q2[high_rows, :], qf[high_rows, :], q2[high_rows, :].bitcast(F32),
                                            ALU.subtract).then_inc(split, 1)
                    dve.wait_ge(hi_done, head * 2 + 2)
                    nc.vector.tensor_tensor(k2_lo[:, 0:SEQ // 2], kf[:, 0:SEQ // 2], k2_hi[:, 0:SEQ // 2].bitcast(F32), ALU.subtract).then_inc(split, 1)
                    nc.vector.tensor_tensor(k2_lo[:, SEQ // 2:], kf[:, SEQ // 2:], k2_hi[:, SEQ // 2:].bitcast(F32), ALU.subtract).then_inc(split, 1)
                    for n in range(AHEAD):
                        scan(n)
                    for j in range(NVT):
                        dve.wait_ge(v_trans, head * NVT + (j + 1))
                        nc.vector.tensor_copy(vn[:, j * (NT // NVT):(j + 1) * (NT // NVT), :], quad(bt[:, :], SB_DIM)).then_inc(v_copied, 1)
                    for n in range(NS):
                        copy(n)
                        if n + AHEAD < NS:
                            scan(n + AHEAD)
                        delta(n % SPREAD, n // SPREAD)


def phase_merge(nc, t):
    with Phase(nc, "E") as ph:
        HM = KD // 2
        XW = XA_HEADS * XA_DIM
        XC = XW // P
        MC = MEM // P
        TB = BLK // P
        w_out, wq = ph.sb("w_out", [P, KD, D]), ph.sb("wq", [P, KD, XW])
        wo, w_r = ph.sb("wo", [P, XC, D]), ph.sb("w_r", [P, KD, NR])
        bias_r = ph.sb("bias_r", [P, NR])
        gx, gm, gf = (ph.sb(s, [P, KD]) for s in ("gx", "gm", "gf"))
        oT_in, gates = ph.sb("oT_in", [P, KD, BLK]), ph.sb("gates", [P, 2 * KD, BLK])
        xm, xT, sq, hT = (ph.sb(s, [P, KD, BLK]) for s in ("xm", "xT", "sq", "hT"))
        rB = ph.sb("rB", [P, BLK])
        qT, kT, vm = ph.sb("qT", [P, XC, BLK]), ph.sb("kT", [P, XC, MEM]), ph.sb("vm", [P, MC, XW])
        p, pT = ph.sb("p", [P, TB, MEM]), ph.sb("pT", [P, MC, BLK])
        aT = ph.sb("aT", [P, XC, BLK])
        mx, nmx, ssum, rsum = (ph.sb(s, [P, XA_HEADS, TB]) for s in ("mx", "nmx", "ssum", "rsum"))
        x2n = [ph.sb(f"x2n{i}", [P, D]) for i in range(2)]
        mss, mr = ph.sb("mss", [P, MC]), ph.sb("mr", [P, MC])
        b = [ph.bank(f"b{i}") for i in range(8)]
        wkv = xT
        mem_n = x2n
        memT = hT[:, :, 0:MEM]
        mem_sq = sq[:, 0:2 * MC, :].rearrange("p (c a) n -> p c (a n)", c=MC)
        const = t["const"]
        ident, ones = const[:, K_ID:K_ID + P], const[:, K_ONE:K_ONE + P]
        names = ("w_in", "w_out_in", "gm_in", "mem_in", "wkv_in", "o_in", "g_in0", "g_in1", "x_in0", "x_in1", "m_sq", "m_ln", "m_r", "m_n", "m_T", "m_Tc",
                 "m_k", "m_kc", "m_v", "m_vc", "ab_mm", "a_g", "b_g", "ab", "x_add", "sq1", "ss1", "ln1", "r1", "h1",
                 "q_mm", "q_ok", "s_mm", "mx_ok", "nmx_ok", "exp_ok", "rs_ok", "p_ok", "pT_mm", "pT_ok", "pv_mm",
                 "aT_ok", "wo_mm", "x_add2", "sq2", "ss2", "ln2", "r2", "h2", "nat_mm", "nat_ok", "lg_mm", "lg_ok")
        s = {n: ph.sem(n) for n in names}
        x2_out = [ph.sem(f"x2_out{i}") for i in range(2)]
        o_d = t["o_d"].rearrange("g p n -> p g n")
        proj = t["proj_d"].rearrange("g p n -> p g n")
        xT_d = t["xT_d"].rearrange("g p n -> p g n")
        x2_d = t["x2_d"].rearrange("(j p) d -> j p d", p=P)
        cols_of = lambda w: w.rearrange("o (k p) n -> p (o k) n", p=P)

        with nc.Block() as block:

            @block.sync
            def _(sp):
                def x_in(cols, half):
                    chunks = slice(half * HM, (half + 1) * HM)
                    sp.dma_start(xm[:, chunks, :], xT_d[:, chunks, cols]).then_inc(s[f"x_in{half}"], 16)

                def gates_in(cols, half):
                    for at in (half * HM, KD + half * HM):
                        sp.dma_start(gates[:, at:at + HM, :], proj[:, G_GA + at:G_GA + at + HM, cols]).then_inc(s[f"g_in{half}"], 16)

                def store(i):
                    for j in range(TB):
                        sp.wait_ge(s["nat_ok"], i * (2 * TB) + 2 * (j + 1))
                        sp.dma_start(x2_d[ds(i * TB + j, 1), :, :], x2n[j % 2][:, :]).then_inc(x2_out[j % 2], 16)

                for c in range(MC):
                    sp.dma_start(mem_n[c][:, :], t["mem"][0, c * P:(c + 1) * P, :]).then_inc(s["mem_in"], 16)
                sp.dma_start(gm[:, :], t["g_mem"].rearrange("o (k p) -> p (o k)", p=P)).then_inc(s["gm_in"], 16)
                sp.dma_start(wkv[:, :, :], cols_of(t["xa_wkv"])).then_inc(s["wkv_in"], 16)
                sp.dma_start(oT_in[:, :, :], o_d[:, :, 0:BLK]).then_inc(s["o_in"], 16)
                sp.dma_start(w_out[:, :, :], cols_of(t["w_out"])).then_inc(s["w_out_in"], 16)
                gates_in(ds(0, BLK), 0)
                gates_in(ds(0, BLK), 1)
                for half in range(2):
                    x_in(ds(0, BLK), half)
                weights = [(wq[:, :, :], cols_of(t["xa_wq"])),
                           (wo[:, :, :], cols_of(t["xa_wo"])), (w_r[:, :, 0:N_GRP], cols_of(t["w_grp"])),
                           (w_r[:, :, N_GRP:NR], cols_of(t["w_exp"])),
                           (bias_r[:, 0:N_GRP], t["b_grp"].to_broadcast([P, N_GRP])),
                           (bias_r[:, N_GRP:NR], t["b_exp"].to_broadcast([P, NE])),
                           (gx[:, :], t["g_xattn"].rearrange("o (k p) -> p (o k)", p=P)),
                           (gf[:, :], t["g_ffn"].rearrange("o (k p) -> p (o k)", p=P))]
                for dst, src in weights:
                    sp.dma_start(dst, src).then_inc(s["w_in"], 16)
                with sp.Fori(0, NBLK - 1) as i:
                    nxt = ds(i * BLK + BLK, BLK)
                    sp.wait_ge(s["x_add"], i * KD + HM)
                    gates_in(nxt, 0)
                    sp.wait_ge(s["ab_mm"], i * (2 * KD) + 2 * KD)
                    sp.dma_start(oT_in[:, :, :], o_d[:, :, nxt]).then_inc(s["o_in"], 16)
                    sp.wait_ge(s["x_add"], i * KD + KD)
                    gates_in(nxt, 1)
                    for half in range(2):
                        sp.wait_ge(s["x_add2"], i * KD + HM * (half + 1))
                        x_in(nxt, half)
                    store(i)
                store(NBLK - 1)
                for j in range(2):
                    sp.wait_ge(x2_out[j], 16 * NT // 2)

            @block.tensor
            def _(pe):
                for k in range(KD):
                    pe.wait_ge(s["m_n"], MC)
                    if k >= 2:
                        pe.wait_ge(s["m_Tc"], k - 1)
                    for c in range(MC):
                        last = nc.tensor.transpose(b[k % 2][:, c * P:(c + 1) * P], mem_n[c][:, k * P:(k + 1) * P], ident)
                    last.then_inc(s["m_T"], 1)
                pe.wait_ge(s["m_Tc"], KD)
                pe.wait_ge(s["wkv_in"], 16)
                for c in range(XC):
                    for k in range(KD):
                        last = nc.tensor.matmul(b[2][:, c * MEM:(c + 1) * MEM], wkv[:, k, c * P:(c + 1) * P], memT[:, k, :],
                                                start=(k == 0), stop=(k == KD - 1))
                last.then_inc(s["m_k"], 1)
                for c in range(MC):
                    for k in range(KD):
                        last = nc.tensor.matmul(b[3][:, c * XW:(c + 1) * XW], memT[:, k, c * P:(c + 1) * P], wkv[:, k, XW:2 * XW],
                                                start=(k == 0), stop=(k == KD - 1))
                last.then_inc(s["m_v"], 1)
                pe.wait_ge(s["m_kc"], 1)
                pe.wait_ge(s["m_vc"], 1)
                pe.wait_ge(s["w_out_in"], 16)

                def branch(i, unit):
                    m, br = unit // 2, unit % 2
                    if unit == 0:
                        pe.wait_ge(s["o_in"], i * 16 + 16)
                    pe.wait_ge(s["b_g" if br else "a_g"], i * KD + m)
                    for k in range(HM):
                        last = nc.tensor.matmul(b[br][:, :], w_out[:, br * HM + k, m * P:(m + 1) * P],
                                                oT_in[:, br * HM + k, :], start=(k == 0), stop=(k == HM - 1))
                    last.then_inc(s["ab_mm"], 1)

                def body(i, more):
                    def next_units(first, n):
                        for unit in range(first, first + n) if more else ():
                            branch(i + 1, unit)

                    def scores(h):
                        rows = slice((h % 2) * XA_DIM, (h % 2 + 1) * XA_DIM)
                        if h >= 1:
                            pe.wait_ge(s["exp_ok"], i * (XA_HEADS * TB) + TB * h)
                        for j in range(TB):
                            last = nc.tensor.matmul(b[3 + j // 2][:, (j % 2) * MEM:(j % 2 + 1) * MEM],
                                                    qT[rows, h // 2, j * P:(j + 1) * P], kT[rows, h // 2, :], start=True, stop=True)
                        last.then_inc(s["s_mm"], 1)

                    def turned(h):
                        pe.wait_ge(s["p_ok"], i * XA_HEADS + (h + 1))
                        for c in range(MC):
                            if h >= 1:
                                pe.wait_ge(s["pT_ok"], i * (XA_HEADS * MC) + MC * (h - 1) + c + 1)
                            for j in range(TB):
                                last = nc.tensor.transpose(b[5 + c][:, j * P:(j + 1) * P], p[:, j, c * P:(c + 1) * P], ident)
                            last.then_inc(s["pT_mm"], 1)

                    def values(h):
                        rows = slice((h % 2) * XA_DIM, (h % 2 + 1) * XA_DIM)
                        if h == 0:
                            pe.wait_ge(s["lg_ok"], i)
                        elif h % 2 == 0:
                            pe.wait_ge(s["aT_ok"], i * XC + h // 2)
                        for c in range(MC):
                            pe.wait_ge(s["pT_ok"], i * (XA_HEADS * MC) + MC * h + c + 1)
                            last = nc.tensor.matmul(b[7][rows, :], vm[:, c, h * XA_DIM:(h + 1) * XA_DIM], pT[:, c, :],
                                                    start=(c == 0), stop=(c == MC - 1))
                        last.then_inc(s["pv_mm"], 1)

                    for k in range(KD):
                        pe.wait_ge(s["sq1"], i * KD + (k + 1))
                        last = nc.tensor.matmul(b[2][:, :], ones, sq[:, k, :], start=(k == 0), stop=(k == KD - 1))
                    last.then_inc(s["ss1"], 1)
                    next_units(0, 2)
                    pe.wait_ge(s["nat_ok"], i * (2 * TB))
                    for c in range(XC):
                        for k in range(KD):
                            if c == 0:
                                pe.wait_ge(s["h1"], i * KD + (k + 1))
                            last = nc.tensor.matmul(b[5 + c][:, :], wq[:, k, c * P:(c + 1) * P], hT[:, k, :],
                                                    start=(k == 0), stop=(k == KD - 1))
                        last.then_inc(s["q_mm"], 1)
                    next_units(2, 2)
                    pe.wait_ge(s["q_ok"], i * XC + XC)
                    scores(0)
                    next_units(4, 2)
                    for h in range(XA_HEADS):
                        turned(h)
                        if h + 1 < XA_HEADS:
                            scores(h + 1)
                        next_units(6 + 2 * h, 1)
                        values(h)
                        next_units(7 + 2 * h, 1)
                    pe.wait_ge(s["aT_ok"], i * XC + XC)
                    for m in range(KD):
                        if m >= 4:
                            pe.wait_ge(s["x_add2"], i * KD + (m - 3))
                        for c in range(XC):
                            last = nc.tensor.matmul(b[3 + m % 4][:, :], wo[:, c, m * P:(m + 1) * P], aT[:, c, :],
                                                    start=(c == 0), stop=(c == XC - 1))
                        last.then_inc(s["wo_mm"], 1)
                    for k in range(KD):
                        pe.wait_ge(s["sq2"], i * KD + (k + 1))
                        last = nc.tensor.matmul(b[2][:, :], ones, sq[:, k, :], start=(k == 0), stop=(k == KD - 1))
                    last.then_inc(s["ss2"], 1)
                    for n in range(2 * TB):
                        j, half = n // 2, n % 2
                        if n >= 4:
                            pe.wait_ge(s["nat_ok"], i * (2 * TB) + (n - 3))
                        for m in range(4):
                            last = nc.tensor.transpose(b[3 + n % 4][:, m * P:(m + 1) * P], xT[:, 4 * half + m, j * P:(j + 1) * P], ident)
                        last.then_inc(s["nat_mm"], 1)
                    next_units(14, 2)
                    pe.wait_ge(s["h2"], i * KD + KD)
                    for j in range(TB):
                        for k in range(KD):
                            last = nc.tensor.matmul(b[7][:, j * NR:(j + 1) * NR], hT[:, k, j * P:(j + 1) * P], w_r[:, k, :],
                                                    start=(k == 0), stop=(k == KD - 1))
                    last.then_inc(s["lg_mm"], 1)

                for unit in range(2 * KD):
                    branch(0, unit)
                pe.wait_ge(s["w_in"], 16 * 8)
                with pe.Fori(0, NBLK - 1) as i:
                    body(i, more=True)
                body(NBLK - 1, more=False)

            @block.scalar
            def _(act):
                act.wait_ge(s["mem_in"], 16 * MC)
                for c in range(MC):
                    nc.scalar.activation(mem_sq[:, c, :], mem_n[c][:, :], ACT.Square, accum_out=mss[:, c:c + 1]).then_inc(s["m_sq"], 1)
                act.wait_ge(s["m_sq"], MC)
                nc.scalar.activation(mr[:, :], mss[:, :], ACT.Ln, bias=t["eps"][:, 0:1], scale=1.0 / D).then_inc(s["m_ln"], 1)
                act.wait_ge(s["m_ln"], 1)
                nc.scalar.activation(mr[:, :], mr[:, :], ACT.Exp, scale=-0.5).then_inc(s["m_r"], 1)
                act.wait_ge(s["m_r"], 1)
                for c in range(MC):
                    nc.scalar.activation(mem_n[c][:, :], mem_n[c][:, :], ACT.Copy, scale=mr[:, c:c + 1]).then_inc(s["m_n"], 1)
                act.wait_ge(s["m_k"], 1)
                nc.scalar.activation(kT[:, :, :], quad(b[2][:, :], MEM), ACT.Copy).then_inc(s["m_kc"], 1)
                act.wait_ge(s["m_v"], 1)
                nc.scalar.activation(vm[:, :, :], quad(b[3][:, :], XW), ACT.Copy).then_inc(s["m_vc"], 1)

                def body(i):
                    for m in range(KD):
                        act.wait_ge(s["x_add"], i * KD + (m + 1))
                        act.wait_ge(s["ss2"], i)
                        nc.scalar.activation(sq[:, m, :], xm[:, m, :], ACT.Square).then_inc(s["sq1"], 1)
                    act.wait_ge(s["ss1"], i + 1)
                    act.wait_ge(s["h2"], i * KD)
                    nc.scalar.activation(rB[:, :], b[2][:, :], ACT.Ln, bias=t["eps"][:, 0:1], scale=1.0 / D).then_inc(s["ln1"], 1)
                    act.wait_ge(s["ln1"], i + 1)
                    nc.scalar.activation(rB[:, :], rB[:, :], ACT.Exp, scale=-0.5).then_inc(s["r1"], 1)
                    for c in range(XC):
                        act.wait_ge(s["q_mm"], i * XC + (c + 1))
                        nc.scalar.activation(qT[:, c, :], b[5 + c][:, :], ACT.Copy).then_inc(s["q_ok"], 1)

                    def exps(h):
                        act.wait_ge(s["nmx_ok"], i * XA_HEADS + (h + 1))
                        if h >= 1:
                            act.wait_ge(s["pT_mm"], i * (XA_HEADS * MC) + MC * h)
                        for j in range(TB):
                            nc.scalar.activation(p[:, j, :], b[3 + j // 2][:, (j % 2) * MEM:(j % 2 + 1) * MEM],
                                                 ACT.Exp, bias=nmx[:, h, j:j + 1], scale=XA_DIM ** -0.5,
                                                 accum_out=ssum[:, h, j:j + 1]).then_inc(s["exp_ok"], 1)

                    exps(0)
                    for h in range(XA_HEADS):
                        for c in range(MC):
                            act.wait_ge(s["pT_mm"], i * (XA_HEADS * MC) + MC * h + c + 1)
                            act.wait_ge(s["pv_mm"], i * XA_HEADS + h)
                            nc.scalar.activation(pT[:, c, :], b[5 + c][:, :], ACT.Copy).then_inc(s["pT_ok"], 1)
                        if h + 1 < XA_HEADS:
                            exps(h + 1)
                        if h % 2 == 1:
                            act.wait_ge(s["pv_mm"], i * XA_HEADS + (h + 1))
                            nc.scalar.activation(aT[:, h // 2, :], b[7][:, :], ACT.Copy).then_inc(s["aT_ok"], 1)
                    for m in range(KD):
                        act.wait_ge(s["x_add2"], i * KD + (m + 1))
                        nc.scalar.activation(sq[:, m, :], xT[:, m, :], ACT.Square).then_inc(s["sq2"], 1)
                    act.wait_ge(s["ss2"], i + 1)
                    act.wait_ge(s["h1"], i * KD + KD)
                    nc.scalar.activation(rB[:, :], b[2][:, :], ACT.Ln, bias=t["eps"][:, 0:1], scale=1.0 / D).then_inc(s["ln2"], 1)
                    act.wait_ge(s["ln2"], i + 1)
                    nc.scalar.activation(rB[:, :], rB[:, :], ACT.Exp, scale=-0.5).then_inc(s["r2"], 1)

                with act.Fori(0, NBLK) as i:
                    body(i)

            @block.gpsimd
            def _(pool):

                def merge(i, chunks):
                    for m in chunks:
                        pool.wait_ge(s["a_g"], i * KD + (m + 1))
                        pool.wait_ge(s["b_g"], i * KD + (m + 1))
                        nc.gpsimd.tensor_tensor(gates[:, m, :], gates[:, m, :], gates[:, KD + m, :], ALU.add).then_inc(s["ab"], 1)

                def residual(i, chunks):
                    for m in chunks:
                        pool.wait_ge(s[f"x_in{m // HM}"], i * 16 + 16)
                        pool.wait_ge(s["ab"], i * KD + (m + 1))
                        nc.gpsimd.tensor_tensor(xm[:, m, :], xm[:, m, :], gates[:, m, :], ALU.add).then_inc(s["x_add"], 1)

                merge(0, range(KD))
                residual(0, range(KD))
                with pool.Fori(0, NBLK - 1) as i:
                    merge(i + 1, range(KD - 1))
                    residual(i + 1, range(KD - 1))
                    merge(i + 1, range(KD - 1, KD))
                    residual(i + 1, range(KD - 1, KD))

            @block.vector
            def _(dve):
                for k in range(KD):
                    dve.wait_ge(s["m_T"], k + 1)
                    dve.wait_ge(s["gm_in"], 16)
                    nc.vector.tensor_scalar(memT[:, k, :], b[k % 2][:, 0:MEM], gm[:, k:k + 1], None, ALU.mult).then_inc(s["m_Tc"], 1)

                def gated(i, unit):
                    m, br = unit // 2, unit % 2
                    if m % HM == 0 and br == 0:
                        dve.wait_ge(s[f"g_in{m // HM}"], i * 32 + 32)
                    dve.wait_ge(s["ab_mm"], i * (2 * KD) + (unit + 1))
                    at = br * KD + m
                    nc.vector.tensor_tensor(gates[:, at, :], b[br][:, :], gates[:, at, :], ALU.mult).then_inc(s["b_g" if br else "a_g"], 1)

                def body(i, more):
                    def next_units(first, n):
                        for unit in range(first, first + n) if more else ():
                            gated(i + 1, unit)

                    def peak(h):
                        dve.wait_ge(s["s_mm"], i * XA_HEADS + (h + 1))
                        if h == 0:
                            dve.wait_ge(s["exp_ok"], i * (XA_HEADS * TB))
                        for a in range(2):
                            nc.vector.tensor_reduce(mx[:, h, 2 * a:2 * a + 2], quad(b[3 + a][:, :], MEM), axis=AX.X,
                                                    op=ALU.max).then_inc(s["mx_ok"], 1)
                        dve.wait_ge(s["mx_ok"], i * (2 * XA_HEADS) + 2 * (h + 1))
                        nc.vector.tensor_scalar(nmx[:, h, :], mx[:, h, :], -XA_DIM ** -0.5, None, ALU.mult).then_inc(s["nmx_ok"], 1)

                    def norm(h):
                        dve.wait_ge(s["exp_ok"], i * (XA_HEADS * TB) + TB * (h + 1))
                        nc.vector.reciprocal(rsum[:, h, :], ssum[:, h, :]).then_inc(s["rs_ok"], 1)
                        dve.wait_ge(s["rs_ok"], i * XA_HEADS + (h + 1))
                        nc.vector.tensor_tensor(p[:, :, :], p[:, :, :], bc(rsum[:, h, :], MEM), ALU.mult).then_inc(s["p_ok"], 1)

                    dve.wait_ge(s["r1"], i + 1)
                    dve.wait_ge(s["lg_mm"], i)
                    for m in range(KD):
                        nc.vector.scalar_tensor_tensor(hT[:, m, :], xm[:, m, :], gx[:, m:m + 1], rB[:, :],
                                                       ALU.mult, ALU.mult).then_inc(s["h1"], 1)
                    next_units(0, 4)
                    peak(0)
                    next_units(4, 1)
                    norm(0)
                    next_units(5, 1)
                    for h in range(XA_HEADS):
                        if h + 1 < XA_HEADS:
                            peak(h + 1)
                        next_units(6 + 2 * h, 1)
                        if h + 1 < XA_HEADS:
                            norm(h + 1)
                        next_units(7 + 2 * h, 1)
                    for m in range(KD):
                        dve.wait_ge(s["wo_mm"], i * KD + (m + 1))
                        nc.vector.tensor_tensor(xT[:, m, :], xm[:, m, :], b[3 + m % 4][:, :], ALU.add).then_inc(s["x_add2"], 1)
                    for n in range(2 * TB):
                        j, half = n // 2, n % 2
                        if half == 0:
                            dve.wait_ge(x2_out[j % 2], i * 32 + 16 * (j // 2))
                        dve.wait_ge(s["nat_mm"], i * (2 * TB) + (n + 1))
                        nc.vector.tensor_copy(x2n[j % 2][:, half * BLK:(half + 1) * BLK], b[3 + n % 4][:, :]).then_inc(s["nat_ok"], 1)
                    next_units(14, 1)
                    dve.wait_ge(s["r2"], i + 1)
                    dve.wait_ge(s["q_mm"], i * XC + XC)
                    dve.wait_ge(s["x_add2"], i * KD + KD)
                    for m in range(KD):
                        nc.vector.scalar_tensor_tensor(hT[:, m, :], xT[:, m, :], gf[:, m:m + 1], rB[:, :],
                                                       ALU.mult, ALU.mult).then_inc(s["h2"], 1)
                    next_units(15, 1)
                    dve.wait_ge(s["lg_mm"], i + 1)
                    nc.vector.tensor_tensor(t["logits"][:, ds(i * TB, TB), :], quad(b[7][:, 0:TB * NR], NR), bc_mid(bias_r[:, :], TB),
                                            ALU.add).then_inc(s["lg_ok"], 1)

                for unit in range(2 * KD):
                    gated(0, unit)
                dve.wait_ge(s["w_in"], 16 * 8)
                with dve.Fori(0, NBLK - 1) as i:
                    body(i, more=True)
                body(NBLK - 1, more=False)
                dve.wait_ge(s["lg_ok"], NBLK)


W_SLOTS = 3
SLOT_BLOCKS = MAX_MOE + 2


def load_expert(sp, t, e, slot):
    for name, src in (("wg", "we_gate"), ("wu", "we_up"), ("wd", "we_down")):
        rows = t[src][0].rearrange("e (k p) n -> e p k n", p=P)[ds(e, 1), :, :, :]
        sp.dma_start(t[name][slot][:, :, :], rows.rearrange("e p k n -> p (e k) n")).then_inc(t[name + "_in"][slot], 16)


def phase_route(nc, t):
    with Phase(nc, "F") as ph:
        NEG = -3.0e38
        lg = t["logits"]
        g8, gv, gi = ph.sb("g8", [P, NT, 8]), ph.sb("gv", [P, NT, 8]), ph.sb("gi", [P, NT, 8], U32)
        gif = ph.sb("gif", [P, NT])
        ohg, e4 = ph.sb("ohg", [P, NT, N_GRP]), ph.sb("e4", [P, NT, N_GRP])
        esum, pg = ph.sb("esum", [P, NT]), ph.sb("pg", [P, NT])
        le = ph.sb("le", [P, NT, NE])
        ev, ei = ph.sb("ev", [P, NT, 8]), ph.sb("ei", [P, NT, 8], U32)
        eif = ph.sb("eif", [P, NT, TOP_K])
        oh = [ph.sb(f"oh{j}", [P, NT, NE]) for j in range(TOP_K)]
        both, pos, tmp = ph.sb("both", [P, NT, NE]), ph.sb("pos", [P, NT, NE]), ph.sb("tmp", [P, NT, NE])
        tot, run = ph.sb("tot", [P, NT, NE]), ph.sb("run", [P, NT + 1, NE])
        cmp = ph.sb("cmp", [P, NE, NT])
        blocks, ends, base = ph.sb("blocks", [P, NE]), ph.sb("ends", [P, NE]), ph.sb("base", [P, NE])
        dst = ph.sb("dst", [P, NT, TOP_K])
        e1, w1 = ph.sb("e1", [P, NT]), ph.sb("w1", [P, NT])
        rows_f, over = ph.sb("rows_f", [P, SLOT_BLOCKS]), ph.sb("over", [P, SLOT_BLOCKS])
        slots = ph.sb("slots", [SLOT_BLOCKS, P])
        pc = [ph.bank(f"c{i}") for i in range(3)]
        const = t["const"]
        ident, ones, exc = (const[:, k:k + P] for k in (K_ID, K_ONE, K_EXC))
        iota = const[:, K_IOTA:K_IOTA + 32]
        step, mm, act_done, dst_ok = (ph.sem(s) for s in ("step", "mm", "act_done", "dst_ok"))
        cleared, scattered, slots_in = (ph.pool_dma_sem(s) for s in ("cleared", "scattered", "slots_in"))

        with nc.Block() as block:
            mark = {}

            @block.vector
            def _(dve):
                count = [0]

                def link(ins):
                    count[0] += 1
                    ins.then_inc(step, 1)
                    dve.wait_ge(step, count[0])

                v = nc.vector
                link(v.memset(g8[:, :, :], NEG))
                link(v.tensor_copy(g8[:, :, 0:N_GRP], lg[:, :, 0:N_GRP]))
                for i in range(NT):
                    link(v.max(gv[:, i, :], g8[:, i, :]))
                    link(v.max_index(gi[:, i, :], gv[:, i, :], g8[:, i, :]))
                link(v.tensor_copy(gif[:, :], gi[:, :, 0]))
                link(v.tensor_tensor(ohg[:, :, :], bc_mid(iota[:, 0:N_GRP], NT), bc(gif[:, :], N_GRP), ALU.is_equal))
                link(v.tensor_tensor(e4[:, :, :], lg[:, :, 0:N_GRP], bc(gv[:, :, 0], N_GRP), ALU.subtract))
                mark["e4"] = count[0]
                four = le[:, :, :].rearrange("p t (g e) -> p (t g) e", g=N_GRP)
                flat = ohg[:, :, :].rearrange("p t g -> p (t g)")
                for g in range(N_GRP):
                    link(v.tensor_tensor(le[:, :, g * PER_GRP:(g + 1) * PER_GRP], lg[:, :, N_GRP + g * PER_GRP:N_GRP + (g + 1) * PER_GRP],
                                         bc(ohg[:, :, g], PER_GRP), ALU.mult))
                link(v.tensor_scalar(ohg[:, :, :], ohg[:, :, :], -1.0, -NEG / 2, ALU.add, ALU.mult))
                link(v.tensor_tensor(four, four, bc(flat, PER_GRP), ALU.add))
                for i in range(NT):
                    link(v.max(ev[:, i, :], le[:, i, :]))
                    link(v.max_index(ei[:, i, :], ev[:, i, :], le[:, i, :]))
                link(v.tensor_copy(eif[:, :, :], ei[:, :, 0:TOP_K]))
                for j in range(TOP_K):
                    link(v.tensor_tensor(oh[j][:, :, :], bc_mid(iota, NT), bc(eif[:, :, j], NE), ALU.is_equal))
                link(v.tensor_tensor(both[:, :, :], oh[0][:, :, :], oh[1][:, :, :], ALU.add))
                link(v.tensor_tensor(e1[:, :], ev[:, :, 1], ev[:, :, 0], ALU.subtract))
                mark["both"] = count[0]
                dve.wait_ge(mm, 1)
                link(v.tensor_copy(pos[:, :, :], quad(pc[0][:, :], NE)))
                link(v.tensor_copy(tot[:, :, :], quad(pc[1][:, :], NE)))
                link(v.memset(run[:, 0, :], 0.0))
                for i in range(NT):
                    link(v.tensor_tensor(run[:, i + 1, :], run[:, i, :], tot[:, i, :], ALU.add))
                link(v.tensor_scalar(tmp[:, 0, 0:NT], iota[:, 0:NT], float(P), None, ALU.mult))
                link(v.tensor_tensor(cmp[:, :, :], bc(run[:, NT, :], NT), bc_mid(tmp[:, 0, 0:NT], NE), ALU.is_gt))
                link(v.tensor_reduce(blocks[:, :], cmp[:, :, :], axis=AX.X, op=ALU.add))
                link(v.tensor_scalar(blocks[:, :], blocks[:, :], 1.0, None, ALU.max))
                link(v.tensor_tensor_scan(ends[:, :], blocks[:, :], blocks[:, :], 0.0, ALU.add, ALU.bypass))
                link(v.tensor_tensor(base[:, :], ends[:, :], blocks[:, :], ALU.subtract))
                link(v.tensor_copy(t["n_blocks"][:, 0:NE], blocks[:, :]))
                link(v.tensor_copy(t["n_blocks"][:, NE:2 * NE], base[:, :]))
                link(v.tensor_copy(t["n_blocks"][:, 2 * NE:2 * NE + 1], ends[:, NE - 1:NE]))
                link(v.tensor_scalar(base[:, :], base[:, :], float(P), None, ALU.mult))
                link(v.tensor_tensor(pos[:, :, :], pos[:, :, :], run[:, 0:NT, :], ALU.add))
                link(v.tensor_tensor(pos[:, :, :], pos[:, :, :], bc_mid(base[:, :], NT), ALU.add))
                for j in range(TOP_K):
                    link(v.tensor_tensor(tmp[:, :, :], pos[:, :, :], oh[j][:, :, :], ALU.mult))
                    link(v.tensor_reduce(dst[:, :, j:j + 1], tmp[:, :, :], axis=AX.X, op=ALU.add))
                v.tensor_copy(t["dest"][:, :, :], dst[:, :, :]).then_inc(dst_ok, 1)
                dve.wait_ge(act_done, 2)
                link(v.tensor_reduce(esum[:, :].unsqueeze(2), e4[:, :, :], axis=AX.X, op=ALU.add))
                link(v.reciprocal(pg[:, :], esum[:, :]))
                link(v.tensor_scalar(w1[:, :], e1[:, :], 1.0, None, ALU.add))
                link(v.reciprocal(w1[:, :], w1[:, :]))
                link(v.tensor_tensor(w1[:, :], w1[:, :], pg[:, :], ALU.mult))
                link(v.tensor_copy(t["wts"][:, :, 0], w1[:, :]))
                link(v.tensor_tensor(t["wts"][:, :, 1], w1[:, :], e1[:, :], ALU.mult))
                dve.wait_ge(mm, 2)
                link(v.tensor_copy(rows_f[:, :], pc[2][:, 0:SLOT_BLOCKS]))
                link(v.tensor_copy(t["slot_row"][:, :], rows_f[:, :]))
                for j in range(TOP_K):
                    link(v.tensor_scalar(over[:, :], rows_f[:, :], float(SEQ), float(SEQ), ALU.is_ge, ALU.mult))
                    link(v.tensor_tensor(rows_f[:, :], rows_f[:, :], over[:, :], ALU.subtract))
                link(v.tensor_copy(t["slot_tok"][:, :], rows_f[:, :]))

            @block.sync
            def _(sp):
                load_expert(sp, t, 0, 0)

            @block.scalar
            def _(act):
                act.wait_ge(step, mark["e4"])
                nc.scalar.activation(e4[:, :, :], e4[:, :, :], ACT.Exp).then_inc(act_done, 1)
                act.wait_ge(step, mark["both"])
                nc.scalar.activation(e1[:, :], e1[:, :], ACT.Exp).then_inc(act_done, 1)

            @block.tensor
            def _(pe):
                pe.wait_ge(step, mark["both"])
                flat = both[:, :, :].rearrange("p t e -> p (t e)")
                nc.tensor.matmul(pc[0][:, :], exc, flat, start=True, stop=True)
                nc.tensor.matmul(pc[1][:, :], ones, flat, start=True, stop=True).then_inc(mm, 1)
                pe.wait_ge(slots_in, 16)
                nc.tensor.transpose(pc[2][:, 0:SLOT_BLOCKS], slots[:, :], ident[0:SLOT_BLOCKS, 0:SLOT_BLOCKS]).then_inc(mm, 1)

            @block.gpsimd
            def _(pool):
                pool.dma_start(t["slot_d"].rearrange("(b p) o -> b (p o)", p=P), const[0:SLOT_BLOCKS, K_PAD:K_PAD + P]).then_inc(cleared, 16)
                pool.wait_ge(cleared, 16)
                pool.wait_ge(dst_ok, 1)
                for i in range(NT):
                    for j in range(TOP_K):
                        pool.indirect_dma_start(t["slot_d"], bass.IndirectOffsetOnAxis(ap=t["dest"][:, i, j:j + 1], axis=0),
                                                const[:, K_TOK + j * NT + i:K_TOK + j * NT + i + 1], None).then_inc(scattered, 16)
                pool.wait_ge(scattered, 16 * NT * TOP_K)
                pool.dma_start(slots[:, :], t["slot_d"].rearrange("(b p) o -> b (p o)", p=P)).then_inc(slots_in, 16)
                pool.wait_ge(slots_in, 16)


def phase_experts(nc, t):
    with Phase(nc, "G") as ph:
        KE = DE // P
        wg, wu, wd = t["wg"], t["wu"], t["wd"]
        TURNS, REST = divmod(NE, W_SLOTS)
        tok, row = ph.sb("tok", [P, 1], I32), ph.sb("row", [P, 1], I32)
        xg, xn = ph.sb("xg", [P, D]), ph.sb("xn", [P, D])
        xsq = ph.sb("xsq", [P, D])
        ss, lnr, r = (ph.sb(s, [P, 1]) for s in ("ss", "lnr", "r"))
        hT = ph.sb("hT", [P, KD, P])
        sg, a, aT = ph.sb("sg", [P, DE]), ph.sb("a", [P, DE]), ph.sb("aT", [P, KE, P])
        y = ph.sb("y", [P, D])
        gf = ph.sb("gf", [P, KD])
        bx = [ph.bank(f"x{i}") for i in range(2)]
        bg, bu, ba = ph.bank("g"), ph.bank("u"), ph.bank("a")
        by = [ph.bank(f"y{i}") for i in range(2)]
        w_used = [ph.sem(f"w_used{i}") for i in range(W_SLOTS)]
        names = ("gf_in", "tok_ok", "row_ok", "indices_set", "expert_begun", "sq_ok", "ln_ok", "r_ok", "xn_ok", "xT_mm", "hT_ok", "g_mm", "u_mm", "sg_ok", "a_ok",
                 "aT_mm", "aT_ok", "y_mm", "y0_ok", "y1_ok")
        s = {n: ph.sem(n) for n in names} | {n: ph.pool_dma_sem(n) for n in ("xg_in", "y_out")}
        ident = t["const"][:, K_ID:K_ID + P]
        x_rows = t["x2_d"]
        nb = t["n_blocks"]
        def all_blocks(eng):
            return eng.value_load(nb[0:1, 2 * NE:2 * NE + 1], min_val=NE, max_val=MAX_MOE)

        with nc.Block() as block:

            @block.sync
            def _(sp):
                sp.dma_start(gf[:, :], t["g_ffn"].rearrange("o (k p) -> p (o k)", p=P)).then_inc(s["gf_in"], 16)
                for e in range(1, W_SLOTS):
                    load_expert(sp, t, e, e)
                with sp.Fori(1, TURNS) as i:
                    for q in range(W_SLOTS):
                        sp.wait_ge(w_used[q], i)
                        load_expert(sp, t, i * W_SLOTS + q, q)
                for q in range(REST):
                    sp.wait_ge(w_used[q], TURNS)
                    load_expert(sp, t, TURNS * W_SLOTS + q, q)

            @block.gpsimd
            def _(pool):
                n = all_blocks(pool)

                def gather(i):
                    nc.gpsimd.tensor_copy(tok[:, :], t["slot_tok"][:, ds(i, 1)]).then_inc(s["tok_ok"], 1)
                    pool.wait_ge(s["tok_ok"], i + 1)
                    pool.sem_inc(s["indices_set"], 1)
                    pool.indirect_dma_start(xg[:, :], None, x_rows, bass.IndirectOffsetOnAxis(ap=tok[:, 0:1], axis=0)).then_inc(s["xg_in"], 16)

                gather(0)
                pool.wait_ge(s["xn_ok"], 1)
                gather(1)
                with pool.Fori(0, n) as i:
                    pool.wait_ge(s["xn_ok"], i + 2)
                    gather(i + 2)
                    pool.wait_ge(s["y_out"], i * 16)
                    nc.gpsimd.tensor_copy(row[:, :], t["slot_row"][:, ds(i, 1)]).then_inc(s["row_ok"], 1)
                    pool.wait_ge(s["row_ok"], i + 1)
                    pool.wait_ge(s["y0_ok"], i + 1)
                    pool.wait_ge(s["y1_ok"], i + 1)
                    pool.sem_inc(s["indices_set"], 1)
                    pool.indirect_dma_start(t["y_d"], bass.IndirectOffsetOnAxis(ap=row[:, 0:1], axis=0), y[:, :], None).then_inc(s["y_out"], 16)
                pool.wait_ge(s["y_out"], n * 16)
                pool.wait_ge(s["xg_in"], n * 16 + 32)

            @block.scalar
            def _(act):
                n = all_blocks(act)

                def norm(i):
                    act.wait_ge(s["xg_in"], i * 16 + 16)
                    nc.scalar.activation(xsq[:, :], xg[:, :], ACT.Square, accum_out=ss[:, :]).then_inc(s["sq_ok"], 1)
                    act.wait_ge(s["sq_ok"], i + 1)
                    nc.scalar.activation(lnr[:, :], ss[:, :], ACT.Ln, bias=t["eps"][:, 0:1], scale=1.0 / D).then_inc(s["ln_ok"], 1)
                    act.wait_ge(s["ln_ok"], i + 1)
                    nc.scalar.activation(r[:, :], lnr[:, :], ACT.Exp, scale=-0.5).then_inc(s["r_ok"], 1)
                    act.wait_ge(s["r_ok"], i + 1)
                    act.wait_ge(s["xT_mm"], i)
                    nc.scalar.activation(xn[:, :], xg[:, :], ACT.Copy, scale=r[:, 0:1]).then_inc(s["xn_ok"], 1)

                norm(0)
                with act.Fori(0, n) as i:
                    act.wait_ge(s["g_mm"], i + 1)
                    act.wait_ge(s["a_ok"], i)
                    nc.scalar.activation(sg[:, :], bg[:, :], ACT.Silu).then_inc(s["sg_ok"], 1)
                    norm(i + 1)
                    act.wait_ge(s["y_mm"], i + 1)
                    act.wait_ge(s["y_out"], i * 16)
                    nc.scalar.activation(y[:, 0:BLK], by[0][:, :], ACT.Copy).then_inc(s["y0_ok"], 1)

            @block.vector
            def _(dve):
                n = all_blocks(dve)
                dve.wait_ge(s["gf_in"], 16)

                def scaled(i):
                    for c in range(2):
                        dve.wait_ge(s["xT_mm"], i + 1)
                        nc.vector.tensor_tensor(hT[:, 4 * c:4 * c + 4, :], quad(bx[c][:, :]), bc(gf[:, 4 * c:4 * c + 4], P),
                                                ALU.mult).then_inc(s["hT_ok"], 1)

                scaled(0)
                with dve.Fori(0, n) as i:
                    dve.wait_ge(s["sg_ok"], i + 1)
                    dve.wait_ge(s["u_mm"], i + 1)
                    dve.wait_ge(s["aT_mm"], i)
                    nc.vector.tensor_tensor(a[:, :], sg[:, :], bu[:, :], ALU.mult).then_inc(s["a_ok"], 1)
                    dve.wait_ge(s["aT_mm"], i + 1)
                    dve.wait_ge(s["y_mm"], i)
                    nc.vector.tensor_copy(aT[:, :, :], quad(ba[:, :])).then_inc(s["aT_ok"], 1)
                    scaled(i + 1)
                    dve.wait_ge(s["y_mm"], i + 1)
                    dve.wait_ge(s["y_out"], i * 16)
                    nc.vector.tensor_copy(y[:, BLK:D], by[1][:, :]).then_inc(s["y1_ok"], 1)

            @block.tensor
            def _(pe):
                def rows_T(n):
                    pe.wait_ge(s["xn_ok"], n + 1)
                    pe.wait_ge(s["hT_ok"], n * 2)
                    for k in range(KD):
                        last = nc.tensor.transpose(bx[k // 4][:, (k % 4) * P:(k % 4 + 1) * P], xn[:, k * P:(k + 1) * P], ident)
                    last.then_inc(s["xT_mm"], 1)

                def expert(e, q, turn):
                    count = pe.value_load(nb[0:1, ds(e, 1)], min_val=1, max_val=SEQ // P)
                    first = pe.value_load(nb[0:1, ds(e + NE, 1)], min_val=0, max_val=MAX_MOE)
                    for name in ("wg_in", "wu_in", "wd_in"):
                        pe.wait_ge(t[name][q], turn * 16 + 16)
                    pe.sem_inc(s["expert_begun"], 1)
                    with pe.Fori(0, count) as j:
                        n = first + j
                        pe.wait_ge(s["hT_ok"], n * 2 + 2)
                        pe.wait_ge(s["sg_ok"], n)
                        for k in range(KD):
                            last = nc.tensor.matmul(bg[:, :], hT[:, k, :], wg[q][:, k, :], start=(k == 0), stop=(k == KD - 1))
                        last.then_inc(s["g_mm"], 1)
                        pe.wait_ge(s["a_ok"], n)
                        for k in range(KD):
                            last = nc.tensor.matmul(bu[:, :], hT[:, k, :], wu[q][:, k, :], start=(k == 0), stop=(k == KD - 1))
                        last.then_inc(s["u_mm"], 1)
                        rows_T(n + 1)
                        pe.wait_ge(s["a_ok"], n + 1)
                        pe.wait_ge(s["aT_ok"], n)
                        for k in range(KE):
                            last = nc.tensor.transpose(ba[:, k * P:(k + 1) * P], a[:, k * P:(k + 1) * P], ident)
                        last.then_inc(s["aT_mm"], 1)
                        pe.wait_ge(s["aT_ok"], n + 1)
                        pe.wait_ge(s["y0_ok"], n)
                        pe.wait_ge(s["y1_ok"], n)
                        for c in range(2):
                            for k in range(KE):
                                last = nc.tensor.matmul(by[c][:, :], aT[:, k, :], wd[q][:, k, c * BLK:(c + 1) * BLK],
                                                        start=(k == 0), stop=(k == KE - 1))
                        last.then_inc(s["y_mm"], 1)
                    pe.wait_ge(s["y_mm"], first + count)
                    pe.sem_inc(w_used[q], 1)

                rows_T(0)
                with pe.Fori(0, TURNS) as i:
                    for q in range(W_SLOTS):
                        expert(i * W_SLOTS + q, q, i)
                for q in range(REST):
                    expert(TURNS * W_SLOTS + q, q, TURNS)


def phase_combine(nc, t):
    with Phase(nc, "H") as ph:
        def two(name, shape, dt=F32):
            return [ph.sb(f"{name}{c}", shape, dt) for c in range(2)]

        x, o = two("x", [P, D]), two("o", [P, D])
        y = two("y", [P, TOP_K, D])
        ss, r = two("ss", [P, 1]), two("r", [P, 1])
        g = ph.sb("g", [P, D])
        sems = lambda n: [ph.sem(f"{n}{c}") for c in range(2)]
        out_done = [ph.pool_dma_sem(f"out_done{c}") for c in range(2)]
        x_in, y_in, add_ok, sq_ok, ln_ok, r_ok, n_ok = (
            sems(n) for n in ("x_in", "y_in", "add_ok", "sq_ok", "ln_ok", "r_ok", "n_ok"))
        g_in = ph.sem("g_in")
        wts_flat = t["wts"][:, :, :].rearrange("p t j -> p (t j)")
        x_d = t["x2_d"].rearrange("(j p) d -> j p d", p=P)
        y_d = t["y_d"][0:TOP_K * SEQ, :].rearrange("(k j p) d -> j p k d", p=P, k=TOP_K)
        out_d = t["out"].rearrange("b (j p) d -> (b j) p d", p=P)

        with nc.Block() as block:

            @block.sync
            def _(sp):
                sp.dma_start(g[:, :], t["g_final"].rearrange("(o d) -> o d", o=1).to_broadcast([P, D])).then_inc(g_in, 16)
                with sp.Fori(0, NT // 2) as i:
                    for c in range(2):
                        sp.wait_ge(n_ok[c], i)
                        sp.dma_start(x[c][:, :], x_d[ds(i * 2 + c, 1), :, :]).then_inc(x_in[c], 16)
                        sp.dma_start(y[c][:, :, :], y_d[ds(i * 2 + c, 1), :, :, :].rearrange("j p k d -> p (j k) d")).then_inc(y_in[c], 16)

            @block.vector
            def _(dve):
                dve.wait_ge(g_in, 16)
                with dve.Fori(0, NT // 2) as i:
                    for c in range(2):
                        dve.wait_ge(y_in[c], i * 16 + 16)
                        dve.wait_ge(x_in[c], i * 16 + 16)
                        for j in range(TOP_K):
                            if j:
                                dve.wait_ge(add_ok[c], i * TOP_K + j)
                            nc.vector.scalar_tensor_tensor(x[c][:, :], y[c][:, j, :], wts_flat[:, ds(i * (2 * TOP_K) + (c * TOP_K + j), 1)],
                                                           x[c][:, :], ALU.mult, ALU.add).then_inc(add_ok[c], 1)
                    for c in range(2):
                        dve.wait_ge(r_ok[c], i + 1)
                        dve.wait_ge(out_done[c], i * 16)
                        nc.vector.scalar_tensor_tensor(o[c][:, :], x[c][:, :], r[c][:, 0:1], g[:, :], ALU.mult, ALU.mult).then_inc(n_ok[c], 1)

            @block.scalar
            def _(act):
                with act.Fori(0, NT // 2) as i:
                    for c in range(2):
                        act.wait_ge(add_ok[c], i * TOP_K + TOP_K)
                        act.wait_ge(out_done[c], i * 16)
                        nc.scalar.activation(o[c][:, :], x[c][:, :], ACT.Square, accum_out=ss[c][:, :]).then_inc(sq_ok[c], 1)
                        act.wait_ge(sq_ok[c], i + 1)
                        nc.scalar.activation(ss[c][:, :], ss[c][:, :], ACT.Ln, bias=t["eps"][:, 0:1], scale=1.0 / D).then_inc(ln_ok[c], 1)
                        act.wait_ge(ln_ok[c], i + 1)
                        nc.scalar.activation(r[c][:, :], ss[c][:, :], ACT.Exp, scale=-0.5).then_inc(r_ok[c], 1)

            @block.gpsimd
            def _(pool):
                with pool.Fori(0, NT // 2) as i:
                    for c in range(2):
                        pool.wait_ge(n_ok[c], i + 1)
                        pool.dma_start(out_d[ds(i * 2 + c, 1), :, :], o[c][:, :]).then_inc(out_done[c], 16)
                for c in range(2):
                    pool.wait_ge(out_done[c], 16 * NT // 2)


def build(nc, tensors):
    t = dict(tensors)
    for name, shape in (("xT_d", (KD, P, SEQ)), ("proj_d", (NGRP, P, SEQ)), ("o_d", (KD, P, SEQ)),
                        ("x2_d", (SEQ, D)), ("slot_d", (SLOT_BLOCKS * P, 1)), ("y_d", (TOP_K * SEQ + P, D))):
        t[name] = nc.dram_tensor(name, shape, F32, kind="Internal").ap()
    with Phase(nc, "all") as ph, nc.allow_non_contiguous_dma(reason="small vectors, a feature on each partition"):
        t["const"] = ph.sb("const", [P, NCONST])
        t["eps"] = ph.sb("eps", [P, 1])
        t["beta"], t["glog"] = (ph.sb(n, [P, NT, DN_HEADS]) for n in ("beta", "glog"))
        t["logits"] = ph.sb("logits", [P, NT, NR])
        t["dest"], t["wts"] = ph.sb("dest", [P, NT, TOP_K], I32), ph.sb("wts", [P, NT, TOP_K])
        t["n_blocks"] = ph.sb("n_blocks", [P, 2 * NE + 1], I32)
        t["slot_tok"], t["slot_row"] = (ph.sb(n, [P, SLOT_BLOCKS], I32) for n in ("slot_tok", "slot_row"))
        with Phase(nc, "h") as hp:
            h_hi, h_lo = (hp.sb(n, [P, KD, SEQ], F32R) for n in ("h_hi", "h_lo"))
            phase_norm_x(nc, t, h_hi, h_lo)
            phase_project(nc, t, h_hi, h_lo)
        phase_mix(nc, t)
        phase_merge(nc, t)
        with Phase(nc, "w") as wp:
            t["wg"], t["wu"] = ([wp.sb(f"{n}{i}", [P, KD, DE]) for i in range(W_SLOTS)] for n in ("wg", "wu"))
            t["wd"] = [wp.sb(f"wd{i}", [P, DE // P, D]) for i in range(W_SLOTS)]
            for n in ("wg_in", "wu_in", "wd_in"):
                t[n] = [wp.sem(f"{n}{i}") for i in range(W_SLOTS)]
            phase_route(nc, t)
            phase_experts(nc, t)
        phase_combine(nc, t)


_INS = ["x", "mem", "g_mix", "w_in", "dn_conv_w", "dn_a_log", "dn_dt_bias", "dn_norm_g", "w_out", "g_xattn", "g_mem",
        "xa_wq", "xa_wkv", "xa_wo", "g_ffn", "w_grp", "b_grp", "w_exp", "b_exp", "we_gate", "we_up", "we_down",
        "g_final"]


def constants():
    import numpy as np
    c = np.zeros((P, NCONST), np.float32)
    p, f = np.arange(P)[:, None], np.arange(P)[None, :]
    c[:, K_ID:K_ID + P] = p == f
    c[:, K_ONE:K_ONE + P] = 1
    c[:, K_INC:K_INC + P] = p <= f
    c[:, K_EXC:K_EXC + P] = p < f
    c[:, K_LOW:K_LOW + P] = p > f
    c[:, K_NEG:K_NEG + P] = MASKED * (f >= p)
    c[:, K_IOTA:K_IOTA + 32] = np.arange(32)
    c[:, K_TOK:K_TOK + TOP_K * NT] = p + P * np.arange(TOP_K * NT)
    c[:, K_PAD:K_PAD + P] = TOP_K * SEQ + f
    for lev in range(NLEV):
        s = 1 << lev
        m = (p // (2 * s) == f // (2 * s)) & ((p // s) % 2 == 1) & ((f // s) % 2 == 0)
        c[:, K_LEV + 2 * lev * P:K_LEV + (2 * lev + 1) * P] = m
        c[:, K_LEV + (2 * lev + 1) * P:K_LEV + (2 * lev + 2) * P] = m.T
    return c


def kernel(**inputs):
    import numpy as _np
    import concourse.bacc as _bacc
    from concourse import mybir as _mybir
    from concourse.bass_utils import run_bass_kernel_spmd as _run

    nc = _bacc.Bacc("TRN2", target_bir_lowering=False, num_devices=1)
    arrays, tensors = {"const_dram": constants()}, {}
    for name in _INS:
        a = _np.ascontiguousarray(inputs[name])
        arrays[f"in_{name}_dram"] = a
        tensors[name] = nc.dram_tensor(f"in_{name}_dram", a.shape, _mybir.dt.from_np(a.dtype), kind="ExternalInput").ap()
    tensors["const_d"] = nc.dram_tensor("const_dram", (P, NCONST), _mybir.dt.float32, kind="ExternalInput").ap()
    tensors["out"] = nc.dram_tensor("out_dram", (1, SEQ, D), _mybir.dt.float32, kind="ExternalOutput").ap()
    build(nc, tensors)
    r = _run(nc, [arrays], core_ids=[0])
    return r.results[0]["out_dram"]
```

```python
import concourse.bass as bass
from concourse import mybir
from contextlib import ExitStack

F32 = mybir.dt.float32
F32R = mybir.dt.float32r
I32 = mybir.dt.int32
U32 = mybir.dt.uint32
ALU = mybir.AluOpType
ACT = mybir.ActivationFunctionType
AX = mybir.AxisListType
ds = bass.ds

P = 128
SEQ, D, MEM = 2048, 1024, 256
KD = D // P
BLK = 512
NBLK = SEQ // BLK
NT = SEQ // P
EPS = 1e-6
SB_HEADS, SB_DIM = 8, 64
DN_HEADS, DN_DIM, DN_CONV = 4, 128, 4
XA_HEADS, XA_DIM = 4, 64
N_GRP, PER_GRP, DE = 4, 8, 512
NE = N_GRP * PER_GRP
NR = N_GRP + NE
TOP_K = 2
MAX_MOE = SEQ * TOP_K // P + NE
NLEV = 7

G_DNQ, G_DNK, G_DNV, G_SBQ, G_SBK, G_SBV, G_Z, G_GA, G_GB, NGRP = 0, 4, 8, 12, 16, 20, 24, 28, 36, 44
C_DN = 3 * SB_HEADS * SB_DIM
C_BA = C_DN + 3 * DN_HEADS * DN_DIM
C_Z = C_BA + 2 * DN_HEADS
IN_W = C_Z + DN_HEADS * DN_DIM + 2 * D

K_ID, K_ONE, K_INC, K_EXC, K_LOW, K_NEG, K_IOTA, K_TOK, K_PAD, K_LEV = 0, 128, 256, 384, 512, 640, 768, 800, 832, 960
NCONST = K_LEV + 2 * NLEV * P
MASKED = -1.0e5


class Phase:

    def __init__(self, nc, name):
        self.nc, self.name, self.stack, self.sems = nc, name, ExitStack(), []

    def __enter__(self):
        return self

    def __exit__(self, *a):
        if self.sems and not a[0]:
            with self.nc.Block() as block:

                @block.gpsimd
                def _(pool):
                    ids = sorted(sem.num for sem in self.sems)
                    first = ids[0]
                    for at, after in zip(ids, ids[1:] + [None]):
                        if after != at + 1:
                            pool.sem_clear(range(first, at + 1))
                            first = after

        self.stack.close()

    def sb(self, name, shape, dt=F32):
        return self.stack.enter_context(self.nc.sbuf_tensor(f"{self.name}_{name}", shape, dt))

    def bank(self, name):
        return self.stack.enter_context(self.nc.psum_tensor(f"{self.name}_bank_{name}", [P, BLK], F32))

    def sem(self, name):
        sem = self.stack.enter_context(self.nc.semaphore(f"{self.name}_{name}"))
        self.sems.append(sem)
        return sem

    def pool_dma_sem(self, name):
        return self.nc.alloc_semaphore(f"{self.name}_{name}")


def bc(ap, n):
    return ap.unsqueeze(2).to_broadcast([ap.shape[0], ap.shape[1], n])


def bc_mid(ap, n):
    return ap.unsqueeze(1).to_broadcast([ap.shape[0], n, ap.shape[1]])


def quad(ap, n=P):
    return ap.rearrange("p (h f) -> p h f", f=n)


def phase_norm_x(nc, t, h_hi, h_lo):
    with Phase(nc, "A") as ph:
        TB = BLK // P
        x_in = [ph.sb(f"x{i}", [P, D]) for i in range(TB)]
        xT = [ph.sb(f"xT{i}", [P, KD, BLK]) for i in range(2)]
        NR_H = 4
        sq = [ph.sb(f"sq{i}", [P, BLK]) for i in range(2)]
        h = [ph.sb(f"h{i}", [P, BLK]) for i in range(NR_H)]
        lnr, rB, g = ph.sb("lnr", [P, BLK]), ph.sb("rB", [P, BLK]), ph.sb("g", [P, KD])
        pT = [ph.bank(f"pT{i}") for i in range(4)]
        pS = [ph.bank(f"pS{i}") for i in range(2)]
        w_ba = ph.sb("w_ba", [P, KD, 2 * DN_HEADS])
        ba_hi, ba_lo, cw, alog, dtb = (t[n] for n in ("ba_hi", "ba_lo", "cw", "alog", "dtb"))
        w_d = t["w_in"].rearrange("o (k p) n -> p (o k) n", p=P)
        misc_in, ba_split = ph.sem("misc_in"), ph.sem("ba_split")
        const_in, g_in = ph.sem("const_in"), ph.sem("g_in")
        x_loaded = [ph.sem(f"x_loaded{i}") for i in range(TB)]
        xT_stored = [ph.pool_dma_sem(f"xT_stored{i}") for i in range(2)]
        trans, copied, squared, summed, ln_done, r_done, h_done, hi_done, lo_done = (
            ph.sem(s) for s in ("trans", "copied", "squared", "summed", "ln_done", "r_done", "h_done", "hi_done", "lo_done"))
        ident, ones = t["const"][:, K_ID:K_ID + P], t["const"][:, K_ONE:K_ONE + P]
        x_d = t["x"].rearrange("b (j p) d -> (b j) p d", p=P)
        xT_d = t["xT_d"].rearrange("k p (c n) -> c p k n", n=BLK)

        with nc.Block() as block:

            @block.sync
            def _(sp):
                sp.dma_start(x_in[0][:, :], x_d[0]).then_inc(x_loaded[0], 16)
                sp.dma_start(t["const"][:, :], t["const_d"]).then_inc(const_in, 16)
                for j in range(1, NT):
                    if j >= TB:
                        sp.wait_ge(trans, 2 * (j - TB + 1))
                    sp.dma_start(x_in[j % TB][:, :], x_d[j]).then_inc(x_loaded[j % TB], 16)
                    if j == 1:
                        sp.dma_start(g[:, :], t["g_mix"].rearrange("o (k p) -> p (o k)", p=P)).then_inc(g_in, 16)
                sp.dma_start(w_ba[:, :, :], w_d[:, :, C_BA:C_Z]).then_inc(misc_in, 16)
                for c in range(12):
                    sp.dma_start(cw[:, c, :], t["dn_conv_w"][0, :, c * P:(c + 1) * P].rearrange("j p -> p j")).then_inc(misc_in, 16)
                sp.dma_start(alog[:, :], t["dn_a_log"].to_broadcast([P, DN_HEADS])).then_inc(misc_in, 16)
                sp.dma_start(dtb[:, :], t["dn_dt_bias"].to_broadcast([P, DN_HEADS])).then_inc(misc_in, 16)
                sp.wait_ge(misc_in, 240)

            @block.tensor
            def _(pe):
                pe.wait_ge(const_in, 16)

                def transposes(b):
                    for j in range(TB * b, TB * b + TB):
                        pe.wait_ge(x_loaded[j % TB], 16 * (j // TB + 1))
                        for half in range(2):
                            n = 2 * j + half
                            if n >= 4:
                                pe.wait_ge(copied, n - 3)
                            for m in range(4):
                                k = 4 * half + m
                                last = nc.tensor.transpose(pT[n % 4][:, m * P:(m + 1) * P], x_in[j % TB][:, k * P:(k + 1) * P], ident)
                            last.then_inc(trans, 1)

                transposes(0)
                for b in range(NBLK):
                    if b >= 2:
                        pe.wait_ge(ln_done, b - 1)
                    for k in range(KD):
                        pe.wait_ge(squared, KD * b + k + 1)
                        last = nc.tensor.matmul(pS[b % 2][:, :], ones, sq[k % 2][:, :], start=(k == 0), stop=(k == KD - 1))
                        last.then_inc(summed, 1)
                    if b + 1 < NBLK:
                        transposes(b + 1)

            @block.scalar
            def _(act):
                def square(b, k):
                    n = KD * b + k
                    act.wait_ge(copied, KD * (b + 1))
                    if n >= 2:
                        act.wait_ge(summed, n - 1)
                    nc.scalar.activation(sq[k % 2][:, :], xT[b % 2][:, k, :], ACT.Square).then_inc(squared, 1)

                def inverse_root(b):
                    act.wait_ge(summed, KD * (b + 1))
                    nc.scalar.activation(lnr[:, :], pS[b % 2][:, :], ACT.Ln, bias=t["eps"][:, 0:1],
                                         scale=1.0 / D).then_inc(ln_done, 1)
                    act.wait_ge(ln_done, b + 1)
                    act.wait_ge(h_done, KD * b)
                    nc.scalar.activation(rB[:, :], lnr[:, :], ACT.Exp, scale=-0.5).then_inc(r_done, 1)

                for k in range(KD):
                    square(0, k)
                inverse_root(0)
                for b in range(NBLK):
                    for k in range(KD):
                        n = KD * b + k
                        act.wait_ge(h_done, n + 1)
                        nc.scalar.activation(h_hi[:, k, b * BLK:(b + 1) * BLK], h[n % NR_H][:, :], ACT.Copy).then_inc(hi_done, 1)
                        if b + 1 < NBLK:
                            square(b + 1, k)
                    if b + 1 < NBLK:
                        inverse_root(b + 1)

            @block.gpsimd
            def _(pool):
                def store(b):
                    pool.wait_ge(copied, KD * (b + 1))
                    pool.dma_start(xT_d[b], xT[b % 2][:, :, :]).then_inc(xT_stored[b % 2], 16)

                store(0)
                for n in range(KD * NBLK):
                    b, k = divmod(n, KD)
                    if k == 0 and b + 1 < NBLK:
                        store(b + 1)
                    part = slice(b * BLK, (b + 1) * BLK)
                    pool.wait_ge(hi_done, n + 1)
                    nc.gpsimd.tensor_tensor(h_lo[:, k, part], h[n % NR_H][:, :], h_hi[:, k, part].bitcast(F32),
                                            ALU.subtract).then_inc(lo_done, 1)
                pool.wait_ge(misc_in, 240)
                nc.gpsimd.tensor_copy(ba_hi[:, :, :], w_ba[:, :, :]).then_inc(ba_split, 1)
                pool.wait_ge(ba_split, 1)
                nc.gpsimd.tensor_tensor(ba_lo[:, :, :], w_ba[:, :, :], ba_hi[:, :, :].bitcast(F32), ALU.subtract).then_inc(ba_split, 1)
                for i in range(2):
                    pool.wait_ge(xT_stored[i], 16 * NBLK // 2)

            @block.vector
            def _(dve):
                nc.vector.memset(t["eps"][:, :], EPS)

                def copies(b):
                    if b >= 2:
                        dve.wait_ge(xT_stored[b % 2], 16 * (b // 2))
                        dve.wait_ge(squared, KD * (b - 1))
                        dve.wait_ge(h_done, KD * (b - 1))
                    for j in range(TB):
                        for half in range(2):
                            n = 2 * (TB * b + j) + half
                            dve.wait_ge(trans, n + 1)
                            nc.vector.tensor_copy(xT[b % 2][:, 4 * half:4 * half + 4, j * P:(j + 1) * P],
                                                  quad(pT[n % 4][:, :])).then_inc(copied, 1)

                copies(0)
                copies(1)
                dve.wait_ge(g_in, 16)
                for b in range(NBLK):
                    dve.wait_ge(r_done, b + 1)
                    for k in range(KD):
                        n = KD * b + k
                        if n >= NR_H:
                            dve.wait_ge(lo_done, n - NR_H + 1)
                        nc.vector.scalar_tensor_tensor(h[n % NR_H][:, :], xT[b % 2][:, k, :], g[:, k:k + 1],
                                                       rB[:, :], ALU.mult, ALU.mult).then_inc(h_done, 1)
                    if b + 2 < NBLK:
                        copies(b + 2)


def phase_project(nc, t, h_hi, h_lo):
    with Phase(nc, "B") as ph:
        w = ph.sb("w", [P, KD, P])
        w_hi, w_lo = ([ph.sb(f"{n}{i}", [P, KD, P], F32R) for i in range(2)] for n in ("w_hi", "w_lo"))
        ba_hi, ba_lo, cw, alog, dtb = (t[n] for n in ("ba_hi", "ba_lo", "cw", "alog", "dtb"))
        stage = [ph.sb(f"stage{i}", [P, SEQ]) for i in range(2)]
        PAD = DN_CONV
        raw = ph.sb("raw", [P, PAD + SEQ])
        conv = [ph.sb(f"conv{i}", [P, SEQ]) for i in range(2)]
        cw_flat = cw[:, :, :].rearrange("p g j -> p (g j)")
        expA = ph.sb("expA", [P, DN_HEADS])
        a_in, a_pos, a_abs, e_abs, ln_e = (
            ph.sb(s, [P, NT, DN_HEADS]) for s in ("a_in", "a_pos", "a_abs", "e_abs", "ln_e"))
        acc = [[ph.bank(f"acc{i}{j}") for j in range(NBLK)] for i in range(2)]
        def per_slot(name):
            return [ph.sem(f"{name}{i}") for i in range(2)]

        mm_done, evac_done, staged, stored = (per_slot(s) for s in ("mm_done", "evac_done", "staged", "stored"))
        split_begun, w_loaded, w_hi_done, w_split = (ph.sem(s) for s in ("split_begun", "w_loaded", "w_hi_done", "w_split"))
        conv_step, conv_done, silu_done, sq_done, ssq_done, ln_done, r_done = (
            per_slot(s) for s in ("conv_step", "conv_done", "silu_done", "sq_done", "ssq_done", "ln_done", "r_done"))
        padded, ba_done, ba_act, ba_dve = (
            ph.sem(s) for s in ("padded", "ba_done", "ba_act", "ba_dve"))
        ones = t["const"][:, K_ONE:K_ONE + P]
        w_d = t["w_in"].rearrange("o (k p) n -> p (o k) n", p=P)
        proj_d = t["proj_d"]
        QK, V, SBG, Z, GT = "qk", "v", "copy", ACT.Silu, ACT.Sigmoid
        runs = [(QK, C_DN, 4), (V, C_DN + 8 * P, 2), (SBG, 0, 6), (Z, C_Z, 2), (GT, C_Z + 4 * P, 8)]
        before = [sum(r[2] for r in runs[:i]) for i in range(len(runs))]
        RUNS = [(*r, b) for r, b in zip(runs, before)]

        with nc.Block() as block:

            @block.sync
            def _(sp):
                def store(turn, s):
                    sp.wait_ge(staged[s], turn * NBLK + NBLK)
                    sp.dma_start(proj_d[ds(turn * 2 + s, 1), :, :], stage[s][:, :]).then_inc(stored[s], 16)

                for kind, col, turns, at in RUNS:
                    first = 1 if at == 0 else 0
                    if first:
                        for s in range(2):
                            sp.wait_ge(w_split, s)
                            sp.dma_start(w[:, :, :], w_d[:, :, col + s * P:col + (s + 1) * P]).then_inc(w_loaded, 16)
                    with sp.Fori(first, turns) as i:
                        for s in range(2):
                            sp.wait_ge(w_split, i * 2 + (2 * at + s))
                            sp.dma_start(w[:, :, :], w_d[:, :, ds(i * (2 * P) + (col + s * P), P)]).then_inc(w_loaded, 16)
                        for s in range(2):
                            store(i + (at - 1), s)
                for s in range(2):
                    store(NGRP // 2 - 1, s)
                for s in range(2):
                    sp.wait_ge(stored[s], 16 * NGRP // 2)

            @block.gpsimd
            def _(pool):
                with pool.Fori(0, NGRP // 2) as i:
                    for s in range(2):
                        pool.wait_ge(w_loaded, i * 32 + 16 * (s + 1))
                        pool.wait_ge(mm_done[s], i)
                        pool.sem_inc(split_begun, 1)
                        nc.gpsimd.tensor_copy(w_hi[s][:, :, :], w[:, :, :]).then_inc(w_hi_done, 1)
                        pool.wait_ge(w_hi_done, i * 2 + (s + 1))
                        nc.gpsimd.tensor_tensor(w_lo[s][:, :, :], w[:, :, :], w_hi[s][:, :, :].bitcast(F32),
                                                ALU.subtract).then_inc(w_split, 1)

            @block.tensor
            def _(pe):
                for j in range(NT):
                    for k in range(KD):
                        for n, (x, y) in enumerate(((h_hi, ba_hi), (h_hi, ba_lo), (h_lo, ba_hi))):
                            last = nc.tensor.matmul(acc[1][3][:, j * 8:(j + 1) * 8], x[:, k, j * P:(j + 1) * P], y[:, k, :],
                                                    start=(k == 0 and n == 0), stop=(k == KD - 1 and n == 2))
                last.then_inc(ba_done, 1)
                pe.wait_ge(ba_dve, 1)
                def product(kind, at, i, s):
                    pe.wait_ge(w_split, i * 2 + (2 * at + s + 1))
                    pe.wait_ge((evac_done if kind in (QK, V) else staged)[s], i * NBLK + NBLK * at)
                    if kind == QK:
                        pe.wait_ge(ln_done[s], i * NBLK)
                    elif kind == V:
                        pe.wait_ge(ln_done[s], NBLK * at)
                    for k in range(KD):
                        for n, (x, y) in enumerate(((w_hi, h_hi), (w_hi, h_lo), (w_lo, h_hi))):
                            for j in range(NBLK):
                                last = nc.tensor.matmul(acc[s][j][:, :], x[s][:, k, :], y[:, k, j * BLK:(j + 1) * BLK],
                                                        start=(k == 0 and n == 0), stop=(k == KD - 1 and n == 2))
                    last.then_inc(mm_done[s], 1)

                def square_sums(i, s):
                    pe.wait_ge(evac_done[s], i * NBLK + NBLK)
                    for j in range(NBLK):
                        pe.wait_ge(sq_done[s], i * NBLK + (j + 1))
                        nc.tensor.matmul(acc[s][j][:, :], ones, stage[s][:, j * BLK:(j + 1) * BLK],
                                         start=True, stop=True).then_inc(ssq_done[s], 1)

                for kind, col, turns, at in RUNS:
                    if kind == QK:
                        for s in range(2):
                            product(kind, at, 0, s)
                        square_sums(0, 0)
                        with pe.Fori(0, turns - 1) as i:
                            product(kind, at, i + 1, 0)
                            square_sums(i, 1)
                            product(kind, at, i + 1, 1)
                            square_sums(i + 1, 0)
                        square_sums(turns - 1, 1)
                    else:
                        with pe.Fori(0, turns) as i:
                            for s in range(2):
                                product(kind, at, i, s)

            @block.scalar
            def _(act):
                b_cols = quad(acc[1][3][:, 0:NT * 8], 8)[:, :, 0:DN_HEADS]
                act.wait_ge(ba_done, 1)
                nc.scalar.activation(t["beta"][:, :, :], b_cols, ACT.Sigmoid).then_inc(ba_act, 1)
                nc.scalar.activation(expA[:, :], alog[:, :], ACT.Exp).then_inc(ba_act, 1)
                act.wait_ge(ba_dve, 3)
                nc.scalar.activation(e_abs[:, :, :], a_abs[:, :, :], ACT.Exp, scale=-1.0).then_inc(ba_act, 1)
                act.wait_ge(ba_act, 3)
                nc.scalar.activation(ln_e[:, :, :], e_abs[:, :, :], ACT.Ln, bias=1.0).then_inc(ba_act, 1)
                act.wait_ge(padded, 1)
                def evacuate(at, i, s):
                    act.wait_ge(mm_done[s], i + (at + 1))
                    act.wait_ge(conv_done[1 - s], i + (at + s))
                    for j in range(NBLK):
                        nc.scalar.activation(raw[:, PAD + j * BLK:PAD + (j + 1) * BLK], acc[s][j][:, :],
                                             ACT.Copy).then_inc(evac_done[s], 1)

                def activate(kind, at, i, s):
                    act.wait_ge(conv_done[s], i + (at + 1))
                    act.wait_ge(stored[s], i * 16 + 16 * at)
                    for j in range(NBLK):
                        part = slice(j * BLK, (j + 1) * BLK)
                        if kind == V:
                            nc.scalar.activation(stage[s][:, part], conv[s][:, part], ACT.Silu).then_inc(staged[s], 1)
                        else:
                            nc.scalar.activation(conv[s][:, part], conv[s][:, part], ACT.Silu).then_inc(silu_done[s], 1)
                            act.wait_ge(silu_done[s], i * NBLK + (j + 1))
                            nc.scalar.activation(stage[s][:, part], conv[s][:, part], ACT.Square).then_inc(sq_done[s], 1)

                def inverse_roots(i, s):
                    for j in range(NBLK):
                        act.wait_ge(ssq_done[s], i * NBLK + (j + 1))
                        nc.scalar.activation(stage[s][:, j * BLK:(j + 1) * BLK], acc[s][j][:, :], ACT.Ln,
                                             bias=t["eps"][:, 0:1]).then_inc(ln_done[s], 1)
                    for j in range(NBLK):
                        part = slice(j * BLK, (j + 1) * BLK)
                        act.wait_ge(ln_done[s], i * NBLK + (j + 1))
                        nc.scalar.activation(stage[s][:, part], stage[s][:, part], ACT.Exp, scale=-0.5).then_inc(r_done[s], 1)

                for kind, col, turns, at in RUNS:
                    if kind == QK:
                        evacuate(at, 0, 0)
                        activate(kind, at, 0, 0)
                        evacuate(at, 0, 1)
                        inverse_roots(0, 0)
                        activate(kind, at, 0, 1)
                        with act.Fori(0, turns - 1) as i:
                            evacuate(at, i + 1, 0)
                            inverse_roots(i, 1)
                            activate(kind, at, i + 1, 0)
                            evacuate(at, i + 1, 1)
                            inverse_roots(i + 1, 0)
                            activate(kind, at, i + 1, 1)
                        inverse_roots(turns - 1, 1)
                    elif kind == V:
                        with act.Fori(0, turns) as i:
                            for s in range(2):
                                evacuate(at, i, s)
                                activate(kind, at, i, s)
                    else:
                        with act.Fori(0, turns) as i:
                            for s in range(2):
                                act.wait_ge(mm_done[s], i + (at + 1))
                                act.wait_ge(stored[s], i * 16 + 16 * at)
                                for j in range(NBLK):
                                    nc.scalar.activation(stage[s][:, j * BLK:(j + 1) * BLK], acc[s][j][:, :],
                                                         ACT.Copy if kind == SBG else kind).then_inc(staged[s], 1)

            @block.vector
            def _(dve):
                nc.vector.memset(raw[:, 0:PAD], 0.0).then_inc(padded, 1)
                a_cols = quad(acc[1][3][:, 0:NT * 8], 8)[:, :, DN_HEADS:2 * DN_HEADS]
                dve.wait_ge(ba_done, 1)
                dve.wait_ge(ba_act, 1)
                nc.vector.tensor_tensor(a_in[:, :, :], a_cols, bc_mid(dtb[:, :], NT), ALU.add).then_inc(ba_dve, 1)
                dve.wait_ge(ba_dve, 1)
                nc.vector.tensor_scalar(a_pos[:, :, :], a_in[:, :, :], 0.0, None, ALU.max).then_inc(ba_dve, 1)
                nc.vector.scalar_tensor_tensor(a_abs[:, :, :], a_in[:, :, :], -1.0, a_in[:, :, :], ALU.mult, ALU.max).then_inc(ba_dve, 1)
                dve.wait_ge(ba_act, 4)
                dve.wait_ge(ba_dve, 3)
                nc.vector.tensor_tensor(a_in[:, :, :], a_pos[:, :, :], ln_e[:, :, :], ALU.add).then_inc(ba_dve, 1)
                dve.wait_ge(ba_dve, 4)
                nc.vector.scalar_tensor_tensor(t["glog"][:, :, :], a_in[:, :, :], -1.0, bc_mid(expA[:, :], NT),
                                               ALU.mult, ALU.mult).then_inc(ba_dve, 1)
                def convolve(at, i, s):
                    dve.wait_ge(evac_done[s], i * NBLK + NBLK * (at + 1))
                    dve.wait_ge(staged[s], i * NBLK + NBLK * at)
                    for j in range(DN_CONV):
                        src = raw[:, PAD - DN_CONV + 1 + j:PAD - DN_CONV + 1 + j + SEQ]
                        wj = cw_flat[:, ds(i * (2 * DN_CONV) + ((2 * at + s) * DN_CONV + j), 1)]
                        if j == 0:
                            ins = nc.vector.tensor_scalar(conv[s][:, :], src, wj, None, ALU.mult)
                        else:
                            dve.wait_ge(conv_step[s], i * 3 + (3 * at + j))
                            ins = nc.vector.scalar_tensor_tensor(conv[s][:, :], src, wj, conv[s][:, :],
                                                                 ALU.mult, ALU.add)
                        ins.then_inc(conv_done[s] if j == DN_CONV - 1 else conv_step[s], 1)

                def normalise(i, s):
                    for j in range(NBLK):
                        part = slice(j * BLK, (j + 1) * BLK)
                        dve.wait_ge(r_done[s], i * NBLK + (j + 1))
                        nc.vector.tensor_tensor(stage[s][:, part], conv[s][:, part], stage[s][:, part],
                                                ALU.mult).then_inc(staged[s], 1)

                for kind, col, turns, at in RUNS[0:2]:
                    if kind == QK:
                        convolve(at, 0, 0)
                        convolve(at, 0, 1)
                        normalise(0, 0)
                        with dve.Fori(0, turns - 1) as i:
                            convolve(at, i + 1, 0)
                            normalise(i, 1)
                            convolve(at, i + 1, 1)
                            normalise(i + 1, 0)
                        normalise(turns - 1, 1)
                    else:
                        with dve.Fori(0, turns) as i:
                            for s in range(2):
                                convolve(at, i, s)


def phase_mix(nc, t):
    with Phase(nc, "C") as ph:
        qf, kf, vf = (ph.sb(s, [P, SEQ]) for s in ("qf", "kf", "vf"))
        q2, k2_hi, k2_lo = (ph.sb(s, [P, SEQ], F32R) for s in ("q2", "k2_hi", "k2_lo"))
        vn = ph.sb("vn", [P, NT, SB_DIM])
        oT = ph.sb("oT", [SB_DIM, SEQ])
        NZB, NRING = 2, 4
        keep = [ph.sb(f"keep{i}", [P, BLK]) for i in range(NRING)]
        sig = [ph.sb(f"sig{i}", [P, BLK]) for i in range(NRING)]
        prod = [ph.sb(f"prod{i}", [P, SEQ + 4]) for i in range(2)]
        att = [ph.sb(f"att{i}", [P, BLK]) for i in range(NRING)]
        attT = [ph.sb(f"attT{i}", [P, BLK]) for i in range(2)]
        bz = [ph.bank(f"z{i}") for i in range(NZB)]
        bt, bo = ph.bank("t"), ph.bank("o")
        (q_in, k_in, v_in, hi_done, split, turn, v_trans, v_copied, z_done, keep_done, sig_done, scan_done, att_done, trans_done,
         attT_done, av_done, o_copied, one_set) = (
            ph.sem(s) for s in ("q_in", "k_in", "v_in", "hi_done", "split", "turn", "v_trans", "v_copied", "z_done", "keep_done", "sig_done",
                                "scan_done", "att_done", "trans_done", "attT_done", "av_done", "o_copied",
                                "one_set"))
        o_store, o_stored = ph.pool_dma_sem("o_store"), ph.pool_dma_sem("o_stored")
        neg = t["const"][:, K_NEG:K_NEG + P]
        proj, o_d = t["proj_d"], t["o_d"]
        o_heads = o_d.rearrange("g (a p) n -> (g a) p n", p=SB_DIM)
        END = SEQ
        HALF = SB_DIM
        low_rows, high_rows = slice(0, HALF), slice(HALF, P)

        steps = []
        for i in range(NT):
            n = (i + 1) * P
            starts = list(range(0, n, BLK))[::-1]
            steps += [(i, k0, min(BLK, n - k0), k0 == starts[0], k0 == 0) for k0 in starts]
        NS = len(steps)
        AHEAD = 3
        PARTS = SEQ // BLK
        PART_AT = {0: 1, 5: 2, 12: 3}
        V_AT = 6
        NOQ = NT // 4
        NVT = NT * SB_DIM // BLK
        SPREAD = NS // 2

        H, W = DN_HEADS, DN_HEADS * P
        SCALE = DN_DIM ** -0.5
        L = NLEV - 1

        def tile(name):
            return ph.sb("d_" + name, [P, W])

        qkvT = ph.sb("d_qkvT", [P, 3 * W])
        zT, glB, E, gN, gT, EG, A, AT, X, XT, Y = (tile(n) for n in ("zT", "glB", "E", "gN", "gT", "EG", "A", "AT", "X", "XT", "Y"))
        ATm = [tile(f"ATm{l}") for l in range(1, NLEV)]
        qkT, qd, kd, vb, rhs, vnew, Sdec, o_raw, o_sq, rB, o_out = (
            tile(n) for n in ("qkT", "qd", "kd", "vb", "rhs", "vnew", "Sdec", "o_raw", "o_sq", "rB", "o_out"))
        S = [tile("S0"), tile("S1")]
        gc, gl, eg, egl, kdec, be = (ph.sb(s, [P, NT * H]) for s in ("gc", "gl", "eg", "egl", "kdec", "be"))
        gdn = ph.sb("gdn", [P, 1])
        b = [ph.bank(f"b{j}") for j in range(4)]
        const = t["const"]
        ident, ones = const[:, K_ID:K_ID + P], const[:, K_ONE:K_ONE + P]
        inc, low = const[:, K_INC:K_INC + P], const[:, K_LOW:K_LOW + P]

        def lev(l, transposed):
            at = K_LEV + (2 * l + transposed) * P
            return const[:, at:at + P]

        glog, beta = (t[s][:, :, :].rearrange("p t h -> p (t h)") for s in ("glog", "beta"))
        proj_g = t["proj_d"].rearrange("g p n -> p g n")
        o_g = t["o_d"].rearrange("g p n -> p g n")
        names = ("in", "z_in", "gdn_in", "g_sum", "g_copied", "g_exp", "g_dec", "glB_ok", "GR_ok", "E_ok", "EG_ok", "Emm_ok", "gNe_ok",
                 "gTe_ok", "gNl_ok", "gN_ok", "gT_ok", "KK_ok", "KQ_ok", "Tk_ok", "Tv_ok", "A_ok", "qkT_ok", "qd_ok", "kd_ok",
                 "vb_ok", "TA_ok", "AT_ok", "ATm_ok", "Xm_ok", "X_ok", "Y_mm", "Y_ok", "P2_mm", "P3_mm", "lev_ok",
                 "R_mm", "Rb_ok", "rhs_ok", "vn_mm", "vn_ok", "Sdec_ok", "dS_mm", "S_ok", "O_mm", "o_ok", "osq_ok",
                 "oss_mm", "oln_ok", "or_ok", "on_ok", "o_done")
        s = {n: ph.sem("d_" + n) for n in names}

        Y_AT = {5 + 2 * (l - 1): l for l in range(1, NLEV)}
        P_AT = {6 + 2 * (l - 1): l for l in range(1, NLEV)}
        R_AT, A_AT, TA_AT, VN_AT, DS_AT, OSS_AT, OUT_AT = 2, 2, 4, 17, 18, 19, 7
        assert OSS_AT < SPREAD

        def stages(delta, n):
            at, c = n % SPREAD, n // SPREAD
            if (at, c) != (OSS_AT, 0):
                delta(at, c)
            if (at, c) == (OUT_AT, 1):
                delta(OSS_AT, 0)


        def hs(tile, h, at=0):
            return tile[:, at + h * P:at + (h + 1) * P]

        with nc.Block() as block:

            @block.sync
            def _(sp):
                sp.dma_start(gdn[:, :], t["dn_norm_g"].rearrange("o p -> p o")).then_inc(s["gdn_in"], 16)
                with sp.Fori(0, SB_HEADS // 2) as pair:
                    for h in range(2):
                        rows = slice(h * HALF, (h + 1) * HALF)
                        head = pair * 2 + h
                        sp.wait_ge(split, head * (2 * PARTS))
                        for half in (low_rows, high_rows):
                            sp.dma_start(qf[half, :], proj[ds(pair + G_SBQ, 1), rows, :]).then_inc(q_in, 16)
                            sp.dma_start(kf[half, :], proj[ds(pair + G_SBK, 1), rows, :]).then_inc(k_in, 16)
                        sp.wait_ge(v_trans, head * NVT)
                        sp.dma_start(vf[low_rows, :], proj[ds(pair + G_SBV, 1), rows, :]).then_inc(v_in, 16)
                        for c in range(2):
                            chunk = head * 2 + c
                            sp.wait_ge(s["R_mm"], chunk)
                            sp.wait_ge(s["qd_ok"], chunk)
                            cols = ds(pair * (4 * P) + (2 * h + c) * P, P)
                            sp.dma_start(quad(qkvT[:, :]), proj_g[:, G_DNQ:G_DNQ + 12, cols]).then_inc(s["in"], 16)
                            sp.wait_ge(s["o_done"], chunk)
                            sp.dma_start(quad(zT[:, :]), proj_g[:, G_Z:G_Z + H, cols]).then_inc(s["z_in"], 16)

            @block.tensor
            def _(pe):
                nc.tensor.matmul(b[0][:, 0:NT * H], inc, glog, start=True, stop=True)
                nc.tensor.matmul(b[0][:, NT * H:2 * NT * H], ones, glog, start=True, stop=True).then_inc(s["g_sum"], 1)
                pe.wait_ge(s["g_copied"], 2)
                with pe.Fori(0, SB_HEADS) as head:

                    def heads(j, lhs, rhs_of):
                        for h in range(H):
                            last = nc.tensor.matmul(b[j][:, h * P:(h + 1) * P], lhs(h), rhs_of(h), start=True, stop=True)
                        return last

                    def turned(j, src):
                        for h in range(H):
                            last = nc.tensor.transpose(hs(b[j], h), src(h), ident)
                        return last

                    kT = lambda h: hs(qkvT, h, W)

                    def delta(at, c):
                        before, now = head * 2 + c, head * 2 + (c + 1)
                        if at == 0:
                            pe.wait_ge(s["in"], head * 32 + 16 * (c + 1))
                            pe.wait_ge(s["vn_ok"], before)
                            heads(1, kT, kT).then_inc(s["KK_ok"], 1)
                            pe.wait_ge(s["S_ok"], before + 1)
                            heads(2, kT, lambda h: hs(qkvT, h)).then_inc(s["KQ_ok"], 1)
                            pe.wait_ge(s["o_ok"], before)
                            turned(3, kT).then_inc(s["Tk_ok"], 1)
                            pe.wait_ge(s["glB_ok"], now)
                            pe.wait_ge(s["oln_ok"], head * 2)
                            heads(0, lambda h: hs(glB, h), lambda h: inc).then_inc(s["GR_ok"], 1)
                        elif at == 1:
                            pe.wait_ge(s["E_ok"], now)
                            pe.wait_ge(s["EG_ok"], now)
                            turned(0, lambda h: hs(qkvT, h, 2 * W)).then_inc(s["Tv_ok"], 1)
                        elif at == R_AT:
                            pe.wait_ge(s["vb_ok"], now)
                            heads(0, kT, lambda h: hs(S[c], h)).then_inc(s["R_mm"], 1)
                        elif at == TA_AT:
                            pe.wait_ge(s["A_ok"], now)
                            turned(1, lambda h: hs(A, h)).then_inc(s["TA_ok"], 1)
                        elif at in Y_AT:
                            l = Y_AT[at]
                            pe.wait_ge(s["ATm_ok"], head * (2 * L) + c * L + l)
                            if l == 1:
                                pe.wait_ge(s["X_ok"], head * 4 + 2 * c + 2)
                                pe.wait_ge(s["qkT_ok"], now)
                            else:
                                pe.wait_ge(s["lev_ok"], head * (4 * L - 2) + (2 * L - 1) * c + 2 * (l - 1))
                            heads(2, lambda h: hs(ATm[l - 1], h), lambda h: hs(X, h)).then_inc(s["Y_mm"], 1)
                        elif at in P_AT:
                            l = P_AT[at]
                            pe.wait_ge(s["Y_ok"], head * (2 * L) + c * L + l)
                            if l == 1:
                                pe.wait_ge(s["kd_ok"], now)
                                pe.wait_ge(s["AT_ok"], now)
                            if l < NLEV - 1:
                                heads(3, lambda h: hs(XT, h), lambda h: hs(Y, h)).then_inc(s["P2_mm"], 1)
                            heads(1, lambda h: hs(Y, h), lambda h: hs(XT, h)).then_inc(s["P3_mm"], 1)
                        elif at == VN_AT:
                            pe.wait_ge(s["rhs_ok"], now)
                            pe.wait_ge(s["lev_ok"], head * (4 * L - 2) + (2 * L - 1) * (c + 1))
                            heads(1, lambda h: hs(XT, h), lambda h: hs(rhs, h)).then_inc(s["vn_mm"], 1)
                        elif at == DS_AT:
                            pe.wait_ge(s["vn_ok"], now)
                            heads(2, lambda h: hs(kd, h), lambda h: hs(vnew, h)).then_inc(s["dS_mm"], 1)
                            for h in range(H):
                                nc.tensor.matmul(hs(b[3], h), hs(S[c], h), hs(qd, h), start=True, stop=False)
                                last = nc.tensor.matmul(hs(b[3], h), hs(vnew, h), hs(qkT, h), start=False, stop=True)
                            last.then_inc(s["O_mm"], 1)
                        elif at == OSS_AT:
                            pe.wait_ge(s["osq_ok"], now)
                            pe.wait_ge(s["Rb_ok"], head * 2 + 2)
                            nc.tensor.matmul(b[0][:, :], ones, o_sq[:, :], start=True, stop=True).then_inc(s["oss_mm"], 1)

                    def scores(n):
                        i, k0, w, first, last = steps[n]
                        if first and i % (BLK // P) == 0:
                            pe.wait_ge(split, head * (2 * PARTS) + 2 * (i * P // BLK + 1))
                        if n >= NZB:
                            pe.wait_ge(sig_done, head * NS + (n + 1 - NZB))
                            pe.wait_ge(keep_done, head * NS + (n + 1 - NZB))
                        tile_q = q2[:, i * P:(i + 1) * P]
                        nc.tensor.matmul(bz[n % NZB][:, 0:w], tile_q, k2_hi[:, k0:k0 + w], start=True, stop=False)
                        ins = nc.tensor.matmul(bz[n % NZB][:, 0:w], tile_q, k2_lo[:, k0:k0 + w], start=False, stop=not first)
                        if first:
                            ins = nc.tensor.matmul(bz[n % NZB][:, w - P:w], ident, neg, start=False, stop=True)
                        ins.then_inc(z_done, 1)

                    def transposes(n):
                        w = steps[n][2]
                        pe.wait_ge(att_done, head * NS + (n + 1))
                        if n == 0 or n == V_AT:
                            pe.wait_ge(v_copied, head * NVT + (1 if n == 0 else 2))
                        else:
                            pe.wait_ge(attT_done, head * NS + n)
                        for m in range(w // P):
                            ins = nc.tensor.transpose(bt[:, m * P:(m + 1) * P], att[n % NRING][:, m * P:(m + 1) * P], ident)
                        ins.then_inc(trans_done, 1)

                    def values(n):
                        i, k0, w, first, last = steps[n]
                        pe.wait_ge(attT_done, head * NS + (n + 1))
                        if first and i % 4 == 0:
                            pe.wait_ge(o_copied, head * NOQ + i // 4)
                        for m in range(w // P):
                            ins = nc.tensor.matmul(bo[low_rows, (i % 4) * P:(i % 4 + 1) * P], vn[:, k0 // P + m, :],
                                                   attT[n % 2][:, m * P:(m + 1) * P],
                                                   start=first and m == 0, stop=last and m == w // P - 1)
                        ins.then_inc(av_done, 1)

                    def v_turned(j, n):
                        pe.wait_ge(attT_done, head * NS + n)
                        pe.sem_inc(turn, 1)
                        for m in range(NT // NVT):
                            at = j * (NT // NVT) + m
                            last = nc.tensor.transpose(bt[:, m * SB_DIM:(m + 1) * SB_DIM], vf[low_rows, at * P:(at + 1) * P],
                                                       ident[low_rows, 0:SB_DIM])
                        last.then_inc(v_trans, 1)

                    pe.wait_ge(sig_done, head * NS)
                    for n in range(AHEAD):
                        scores(n)
                    pe.wait_ge(v_in, head * 16 + 16)
                    v_turned(0, 0)
                    for n in range(NS):
                        if n + AHEAD < NS:
                            scores(n + AHEAD)
                        if n == V_AT:
                            v_turned(1, n)
                        transposes(n)
                        if n >= 1:
                            values(n - 1)
                        stages(delta, n)
                    values(NS - 1)

            def evacuate(act, head, n):
                i = steps[n][0]
                act.wait_ge(av_done, head * NS + (n + 1))
                nc.scalar.activation(oT[:, (i - 3) * P:(i + 1) * P], bo[low_rows, :], ACT.Copy).then_inc(o_copied, 1)

            @block.scalar
            def _(act):
                act.wait_ge(s["g_copied"], 2)
                nc.scalar.activation(eg[:, :], gc[:, :], ACT.Exp).then_inc(s["g_exp"], 1)
                nc.scalar.activation(egl[:, :], gl[:, :], ACT.Exp).then_inc(s["g_exp"], 1)
                act.wait_ge(s["g_dec"], 1)
                nc.scalar.activation(kdec[:, :], kdec[:, :], ACT.Exp).then_inc(s["g_exp"], 1)
                with act.Fori(0, SB_HEADS) as head:

                    def delta(at, c):
                        before, now = head * 2 + c, head * 2 + (c + 1)
                        if at == 0:
                            act.wait_ge(s["E_ok"], now)
                            act.wait_ge(s["qd_ok"], before)
                            nc.scalar.activation(EG[:, :], b[0][:, :], ACT.Exp).then_inc(s["EG_ok"], 1)
                            act.wait_ge(s["Emm_ok"], head * 4 + 2 * c + 2)
                            nc.scalar.activation(gN[:, :], gN[:, :], ACT.Exp, scale=-1.0).then_inc(s["gNe_ok"], 1)
                            nc.scalar.activation(gT[:, :], gT[:, :], ACT.Exp).then_inc(s["gTe_ok"], 1)
                        elif at in Y_AT:
                            l = Y_AT[at]
                            act.wait_ge(s["Y_mm"], head * (2 * L) + c * L + l)
                            act.wait_ge(s["P3_mm"], head * (2 * L) + c * L + (l - 1))
                            nc.scalar.activation(Y[:, :], b[2][:, :], ACT.Copy).then_inc(s["Y_ok"], 1)
                        elif at == VN_AT:
                            act.wait_ge(s["vn_mm"], now)
                            nc.scalar.activation(vnew[:, :], b[1][:, :], ACT.Copy).then_inc(s["vn_ok"], 1)
                        elif at == DS_AT:
                            act.wait_ge(s["O_mm"], now)
                            act.wait_ge(s["on_ok"], before)
                            nc.scalar.activation(o_raw[:, :], b[3][:, :], ACT.Copy).then_inc(s["o_ok"], 1)
                            act.wait_ge(s["o_ok"], now)
                            nc.scalar.activation(o_sq[:, :], o_raw[:, :], ACT.Square).then_inc(s["osq_ok"], 1)
                        elif at == OSS_AT:
                            act.wait_ge(s["oss_mm"], now)
                            nc.scalar.activation(rB[:, :], b[0][:, :], ACT.Ln, bias=t["eps"][:, 0:1],
                                                 scale=1.0 / DN_DIM).then_inc(s["oln_ok"], 1)
                            act.wait_ge(s["oln_ok"], now)
                            nc.scalar.activation(rB[:, :], rB[:, :], ACT.Exp, scale=-0.5).then_inc(s["or_ok"], 1)

                    def weights(n):
                        w = steps[n][2]
                        act.wait_ge(z_done, head * NS + (n + 1))
                        if n >= NRING:
                            act.wait_ge(scan_done, head * NS + (n + 1 - NRING))
                            act.wait_ge(att_done, head * NS + (n + 1 - NRING))
                        else:
                            act.wait_ge(att_done, head * NS)
                        nc.scalar.activation(keep[n % NRING][:, 0:w], bz[n % NZB][:, 0:w], ACT.Sigmoid,
                                             scale=-SB_DIM ** -0.5).then_inc(keep_done, 1)
                        nc.scalar.activation(sig[n % NRING][:, 0:w], bz[n % NZB][:, 0:w], ACT.Sigmoid,
                                             scale=SB_DIM ** -0.5).then_inc(sig_done, 1)

                    def high_parts(j):
                        part = slice(j * BLK, (j + 1) * BLK)
                        nc.scalar.activation(q2[:, part], qf[:, part], ACT.Copy).then_inc(hi_done, 1)
                        nc.scalar.activation(k2_hi[:, part], kf[:, part], ACT.Copy).then_inc(hi_done, 1)

                    act.wait_ge(z_done, head * NS)
                    act.wait_ge(q_in, head * 32 + 32)
                    act.wait_ge(k_in, head * 32 + 32)
                    high_parts(0)
                    for n in range(AHEAD):
                        weights(n)
                    act.wait_ge(o_store, head * 16)
                    for n in range(NS):
                        if n + AHEAD < NS:
                            weights(n + AHEAD)
                        if n >= 2 and steps[n - 2][4] and steps[n - 2][0] % 4 == 3:
                            evacuate(act, head, n - 2)
                        if n in PART_AT:
                            high_parts(PART_AT[n])
                        stages(delta, n)
                    evacuate(act, head, NS - 1)

            @block.gpsimd
            def _(pool):
                nc.gpsimd.memset(S[0][:, :], 0.0).then_inc(s["S_ok"], 1)
                with pool.Fori(0, SB_HEADS) as head:

                    def cols(ap, c):
                        return ap[:, ds(head * (2 * H) + c * H, H)]

                    def log_decay(c):
                        pool.wait_ge(s["GR_ok"], head * 2 + c)
                        nc.gpsimd.tensor_copy(quad(glB[:, :]), bc(cols(glog, c), P)).then_inc(s["glB_ok"], 1)

                    def delta(at, c):
                        before, now = head * 2 + c, head * 2 + (c + 1)
                        if at == 1:
                            pool.wait_ge(s["gNe_ok"], now)
                            nc.gpsimd.tensor_tensor(quad(gN[:, :]), quad(gN[:, :]), bc_mid(low, H), ALU.mult).then_inc(s["gNl_ok"], 1)
                            pool.wait_ge(s["gTe_ok"], now)
                            nc.gpsimd.tensor_tensor(quad(gT[:, :]), quad(gT[:, :]), bc_mid(inc, H), ALU.mult).then_inc(s["gT_ok"], 1)
                            pool.wait_ge(s["gNl_ok"], now)
                            nc.gpsimd.tensor_tensor(quad(gN[:, :]), quad(gN[:, :]), bc(cols(beta, c), P), ALU.mult).then_inc(s["gN_ok"], 1)
                        elif at == 3:
                            pool.wait_ge(s["g_exp"], 3)
                            pool.wait_ge(s["S_ok"], before + 1)
                            nc.gpsimd.tensor_tensor(quad(Sdec[:, :]), quad(S[c][:, :]), bc(cols(egl, c), P), ALU.mult).then_inc(s["Sdec_ok"], 1)
                        elif TA_AT <= at < TA_AT + L // 2:
                            pool.wait_ge(s["AT_ok"], now)
                            for l in (2 * (at - TA_AT) + 1, 2 * (at - TA_AT) + 2):
                                nc.gpsimd.tensor_tensor(quad(ATm[l - 1][:, :]), quad(AT[:, :]), bc_mid(lev(l, 1), H),
                                                        ALU.mult).then_inc(s["ATm_ok"], 1)
                        elif at == OSS_AT:
                            pool.wait_ge(s["on_ok"], now)
                            pool.wait_ge(s["z_in"], head * 32 + 16 * (c + 1))
                            nc.gpsimd.tensor_tensor(o_out[:, :], o_out[:, :], zT[:, :], ALU.mult).then_inc(s["o_done"], 1)
                            pool.wait_ge(s["o_done"], now)
                            pool.dma_start(o_g[:, H:2 * H, ds(head * (2 * P) + c * P, P)], quad(o_out[:, :])).then_inc(o_stored, 16)

                    def weigh(n):
                        i, k0, w, first, last = steps[n]
                        off = END - (i + 1) * P + k0
                        pool.wait_ge(sig_done, head * NS + (n + 1))
                        pool.wait_ge(scan_done, head * NS + (n + 1))
                        pool.wait_ge(trans_done, head * NS + max(0, n + 1 - NRING))
                        nc.gpsimd.tensor_tensor(att[n % NRING][:, 0:w], sig[n % NRING][:, 0:w],
                                                prod[i % 2][:, off + 1:off + 1 + w], ALU.mult).then_inc(att_done, 1)

                    log_decay(0)
                    for n in range(AHEAD):
                        weigh(n)
                    for n in range(NS):
                        if n == SPREAD - 3:
                            log_decay(1)
                        if n + AHEAD < NS:
                            weigh(n + AHEAD)
                        stages(delta, n)
                    pool.wait_ge(o_copied, head * NOQ + NOQ)
                    pool.dma_start(o_heads[ds(head, 1), :, :], oT[:, :]).then_inc(o_store, 16)
                pool.wait_ge(o_store, 16 * SB_HEADS)
                pool.wait_ge(o_stored, 16 * NT)

            @block.vector
            def _(dve):
                dve.wait_ge(s["g_sum"], 1)
                nc.vector.tensor_copy(gc[:, :], b[0][:, 0:NT * H]).then_inc(s["g_copied"], 1)
                nc.vector.tensor_copy(gl[:, :], b[0][:, NT * H:2 * NT * H]).then_inc(s["g_copied"], 1)
                dve.wait_ge(s["g_copied"], 2)
                nc.vector.tensor_tensor(kdec[:, :], gl[:, :], gc[:, :], ALU.subtract).then_inc(s["g_dec"], 1)
                dve.wait_ge(s["g_exp"], 3)
                nc.vector.tensor_tensor(be[:, :], beta, eg[:, :], ALU.mult).then_inc(s["g_dec"], 1)
                dve.wait_ge(s["g_dec"], 2)
                dve.wait_ge(s["gdn_in"], 16)
                for j in range(2):
                    nc.vector.memset(prod[j][:, END:END + 1], 1.0).then_inc(one_set, 1)
                dve.wait_ge(one_set, 2)
                with dve.Fori(0, SB_HEADS) as head:

                    def cols(ap, c):
                        return bc(ap[:, ds(head * (2 * H) + c * H, H)], P)

                    def delta(at, c):
                        v = nc.vector
                        before, now = head * 2 + c, head * 2 + (c + 1)
                        if at == 0:
                            dve.wait_ge(s["Tk_ok"], now)
                            dve.wait_ge(s["dS_mm"], before)
                            v.tensor_tensor(quad(kd[:, :]), quad(b[3][:, :]), cols(kdec, c), ALU.mult).then_inc(s["kd_ok"], 1)
                            dve.wait_ge(s["GR_ok"], now)
                            v.tensor_tensor(quad(E[:, :]), quad(b[0][:, :]), cols(gc, c), ALU.subtract).then_inc(s["E_ok"], 1)
                            dve.wait_ge(s["E_ok"], now)
                            v.tensor_scalar(gN[:, :], E[:, :], 0.0, None, ALU.max).then_inc(s["Emm_ok"], 1)
                            v.tensor_scalar(gT[:, :], E[:, :], 0.0, None, ALU.min).then_inc(s["Emm_ok"], 1)
                        elif at == 1:
                            dve.wait_ge(s["EG_ok"], now)
                            dve.wait_ge(s["O_mm"], before)
                            v.scalar_tensor_tensor(qd[:, :], qkvT[:, 0:W], SCALE, EG[:, :], ALU.mult, ALU.mult).then_inc(s["qd_ok"], 1)
                            dve.wait_ge(s["Tv_ok"], now)
                            v.tensor_tensor(quad(vb[:, :]), quad(b[0][:, :]), cols(beta, c), ALU.mult).then_inc(s["vb_ok"], 1)
                        elif at == A_AT:
                            dve.wait_ge(s["KK_ok"], now)
                            dve.wait_ge(s["gN_ok"], now)
                            v.tensor_tensor(A[:, :], b[1][:, :], gN[:, :], ALU.mult).then_inc(s["A_ok"], 1)
                            dve.wait_ge(s["KQ_ok"], now)
                            dve.wait_ge(s["gT_ok"], now)
                            v.scalar_tensor_tensor(qkT[:, :], b[2][:, :], SCALE, gT[:, :], ALU.mult, ALU.mult).then_inc(s["qkT_ok"], 1)
                        elif at == 3:
                            dve.wait_ge(s["R_mm"], now)
                            v.tensor_tensor(quad(rhs[:, :]), quad(b[0][:, :]), cols(be, c), ALU.mult).then_inc(s["Rb_ok"], 1)
                            dve.wait_ge(s["Rb_ok"], now)
                            v.tensor_tensor(rhs[:, :], vb[:, :], rhs[:, :], ALU.subtract).then_inc(s["rhs_ok"], 1)
                        elif at == TA_AT:
                            dve.wait_ge(s["TA_ok"], now)
                            v.tensor_copy(AT[:, :], b[1][:, :]).then_inc(s["AT_ok"], 1)
                            dve.wait_ge(s["AT_ok"], now)
                            v.tensor_tensor(quad(XT[:, :]), quad(AT[:, :]), bc_mid(lev(0, 1), H), ALU.mult).then_inc(s["Xm_ok"], 1)
                            v.tensor_tensor(quad(X[:, :]), quad(A[:, :]), bc_mid(lev(0, 0), H), ALU.mult).then_inc(s["Xm_ok"], 1)
                            dve.wait_ge(s["Xm_ok"], head * 4 + 2 * c + 2)
                            for y in (XT, X):
                                v.tensor_tensor(quad(y[:, :]), bc_mid(ident, H), quad(y[:, :]), ALU.subtract).then_inc(s["X_ok"], 1)
                        elif at in P_AT:
                            l = P_AT[at]
                            if l < NLEV - 1:
                                dve.wait_ge(s["P2_mm"], head * (2 * L - 2) + c * (L - 1) + l)
                                v.tensor_tensor(X[:, :], X[:, :], b[3][:, :], ALU.subtract).then_inc(s["lev_ok"], 1)
                            dve.wait_ge(s["P3_mm"], head * (2 * L) + c * L + l)
                            v.tensor_tensor(XT[:, :], XT[:, :], b[1][:, :], ALU.subtract).then_inc(s["lev_ok"], 1)
                        elif at == DS_AT:
                            dve.wait_ge(s["dS_mm"], now)
                            dve.wait_ge(s["Sdec_ok"], now)
                            v.tensor_tensor(S[1 - c][:, :], Sdec[:, :], b[2][:, :], ALU.add).then_inc(s["S_ok"], 1)
                        elif at == OSS_AT:
                            dve.wait_ge(s["or_ok"], now)
                            dve.wait_ge(o_stored, before * 16)
                            v.scalar_tensor_tensor(o_out[:, :], o_raw[:, :], gdn[:, 0:1], rB[:, :],
                                                   ALU.mult, ALU.mult).then_inc(s["on_ok"], 1)

                    def scan(n):
                        i, k0, w, first, last = steps[n]
                        off = END - (i + 1) * P + k0
                        dve.wait_ge(keep_done, head * NS + (n + 1))
                        dve.wait_ge(scan_done, head * NS + n)
                        if first:
                            m = next((m for m in range(n - 1, -1, -1) if steps[m][0] == i - 2), -1)
                            dve.wait_ge(att_done, head * NS + (m + 1))
                        nc.vector.tensor_tensor_scan(prod[i % 2][:, off:off + w][:, ::-1], keep[n % NRING][:, 0:w][:, ::-1],
                                                     keep[n % NRING][:, 0:w][:, ::-1], prod[i % 2][:, off + w:off + w + 1],
                                                     ALU.mult, ALU.bypass).then_inc(scan_done, 1)

                    def copy(n):
                        w = steps[n][2]
                        dve.wait_ge(trans_done, head * NS + (n + 1))
                        dve.wait_ge(av_done, head * NS + max(0, n - 1))
                        nc.vector.tensor_copy(attT[n % 2][:, 0:w], bt[:, 0:w]).then_inc(attT_done, 1)

                    def low_parts(j):
                        part = slice(j * BLK, (j + 1) * BLK)
                        dve.wait_ge(hi_done, head * (2 * PARTS) + (2 * j + 1))
                        nc.vector.tensor_tensor(q2[high_rows, part], qf[high_rows, part], q2[high_rows, part].bitcast(F32),
                                                ALU.subtract).then_inc(split, 1)
                        dve.wait_ge(hi_done, head * (2 * PARTS) + (2 * j + 2))
                        nc.vector.tensor_tensor(k2_lo[:, part], kf[:, part], k2_hi[:, part].bitcast(F32),
                                                ALU.subtract).then_inc(split, 1)

                    def v_copy(j):
                        dve.wait_ge(v_trans, head * NVT + (j + 1))
                        nc.vector.tensor_copy(vn[:, j * (NT // NVT):(j + 1) * (NT // NVT), :], quad(bt[:, :], SB_DIM)).then_inc(v_copied, 1)

                    low_parts(0)
                    for n in range(AHEAD):
                        scan(n)
                    v_copy(0)
                    for n in range(NS):
                        if n == V_AT:
                            v_copy(1)
                        copy(n)
                        if n in PART_AT:
                            low_parts(PART_AT[n])
                        if n + AHEAD < NS:
                            scan(n + AHEAD)
                        stages(delta, n)


def phase_merge(nc, t):
    with Phase(nc, "E") as ph:
        HM = KD // 2
        XW = XA_HEADS * XA_DIM
        XC = XW // P
        MC = MEM // P
        TB = BLK // P
        w_out, wq = ph.sb("w_out", [P, KD, D]), ph.sb("wq", [P, KD, XW])
        wo, w_r = ph.sb("wo", [P, XC, D]), ph.sb("w_r", [P, KD, NR])
        bias_r = ph.sb("bias_r", [P, NR])
        gx, gm, gf = (ph.sb(s, [P, KD]) for s in ("gx", "gm", "gf"))
        oT_in, gates = ph.sb("oT_in", [P, KD, BLK]), ph.sb("gates", [P, 2 * KD, BLK])
        xm, xT, sq, hT = (ph.sb(s, [P, KD, BLK]) for s in ("xm", "xT", "sq", "hT"))
        rB = ph.sb("rB", [P, BLK])
        qT, kT, vm = ph.sb("qT", [P, XC, BLK]), ph.sb("kT", [P, XC, MEM]), ph.sb("vm", [P, MC, XW])
        p, pT = ph.sb("p", [P, TB, MEM]), ph.sb("pT", [P, MC, BLK])
        aT = ph.sb("aT", [P, XC, BLK])
        mx, nmx, ssum, rsum = (ph.sb(s, [P, XA_HEADS, TB]) for s in ("mx", "nmx", "ssum", "rsum"))
        x2n = [ph.sb(f"x2n{i}", [P, D]) for i in range(2)]
        mss, mr = ph.sb("mss", [P, MC]), ph.sb("mr", [P, MC])
        b = [ph.bank(f"b{i}") for i in range(8)]
        wkv = xT
        mem_n = x2n
        memT = hT[:, :, 0:MEM]
        mem_sq = sq[:, 0:2 * MC, :].rearrange("p (c a) n -> p c (a n)", c=MC)
        const = t["const"]
        ident, ones = const[:, K_ID:K_ID + P], const[:, K_ONE:K_ONE + P]
        names = ("w_in", "w_out_in", "gm_in", "mem_in", "wkv_in", "o_in", "g_in0", "g_in1", "x_in0", "x_in1", "m_sq", "m_ln", "m_r", "m_n", "m_T", "m_Tc",
                 "m_k", "m_kc", "m_v", "m_vc", "ab_mm", "a_g", "b_g", "ab", "x_add", "sq1", "sum1", "ss1", "ln1", "r1", "h1",
                 "q_mm", "q_ok", "s_mm", "mx_ok", "nmx_ok", "exp_ok", "rs_ok", "p_ok", "pT_mm", "pT_ok", "pv_mm",
                 "aT_ok", "wo_mm", "x_add2", "sq2", "sum2", "ss2", "ln2", "r2", "h2", "nat_mm", "nat_ok", "lg_mm", "lg_ok")
        s = {n: ph.sem(n) for n in names}
        x2_out = [ph.sem(f"x2_out{i}") for i in range(2)]
        o_d = t["o_d"].rearrange("g p n -> p g n")
        proj = t["proj_d"].rearrange("g p n -> p g n")
        xT_d = t["xT_d"].rearrange("g p n -> p g n")
        x2_d = t["x2_d"].rearrange("(j p) d -> j p d", p=P)
        cols_of = lambda w: w.rearrange("o (k p) n -> p (o k) n", p=P)

        with nc.Block() as block:

            @block.sync
            def _(sp):
                def x_in(cols, half):
                    chunks = slice(half * HM, (half + 1) * HM)
                    sp.dma_start(xm[:, chunks, :], xT_d[:, chunks, cols]).then_inc(s[f"x_in{half}"], 16)

                def gates_in(cols, half):
                    for at in (half * HM, KD + half * HM):
                        sp.dma_start(gates[:, at:at + HM, :], proj[:, G_GA + at:G_GA + at + HM, cols]).then_inc(s[f"g_in{half}"], 16)

                def store(i):
                    for j in range(TB):
                        sp.wait_ge(s["nat_ok"], i * (2 * TB) + 2 * (j + 1))
                        sp.dma_start(x2_d[ds(i * TB + j, 1), :, :], x2n[j % 2][:, :]).then_inc(x2_out[j % 2], 16)

                for c in range(MC):
                    sp.dma_start(mem_n[c][:, :], t["mem"][0, c * P:(c + 1) * P, :]).then_inc(s["mem_in"], 16)
                sp.dma_start(gm[:, :], t["g_mem"].rearrange("o (k p) -> p (o k)", p=P)).then_inc(s["gm_in"], 16)
                sp.dma_start(wkv[:, :, :], cols_of(t["xa_wkv"])).then_inc(s["wkv_in"], 16)
                sp.dma_start(oT_in[:, :, :], o_d[:, :, 0:BLK]).then_inc(s["o_in"], 16)
                sp.dma_start(w_out[:, :, :], cols_of(t["w_out"])).then_inc(s["w_out_in"], 16)
                gates_in(ds(0, BLK), 0)
                gates_in(ds(0, BLK), 1)
                for half in range(2):
                    x_in(ds(0, BLK), half)
                weights = [(wq[:, :, :], cols_of(t["xa_wq"])),
                           (wo[:, :, :], cols_of(t["xa_wo"])), (w_r[:, :, 0:N_GRP], cols_of(t["w_grp"])),
                           (w_r[:, :, N_GRP:NR], cols_of(t["w_exp"])),
                           (bias_r[:, 0:N_GRP], t["b_grp"].to_broadcast([P, N_GRP])),
                           (bias_r[:, N_GRP:NR], t["b_exp"].to_broadcast([P, NE])),
                           (gx[:, :], t["g_xattn"].rearrange("o (k p) -> p (o k)", p=P)),
                           (gf[:, :], t["g_ffn"].rearrange("o (k p) -> p (o k)", p=P))]
                for dst, src in weights:
                    sp.dma_start(dst, src).then_inc(s["w_in"], 16)
                with sp.Fori(0, NBLK - 1) as i:
                    nxt = ds(i * BLK + BLK, BLK)
                    sp.wait_ge(s["x_add"], i * KD + HM)
                    gates_in(nxt, 0)
                    sp.wait_ge(s["ab_mm"], i * (2 * KD) + 2 * KD)
                    sp.dma_start(oT_in[:, :, :], o_d[:, :, nxt]).then_inc(s["o_in"], 16)
                    sp.wait_ge(s["x_add"], i * KD + KD)
                    gates_in(nxt, 1)
                    for half in range(2):
                        sp.wait_ge(s["x_add2"], i * KD + HM * (half + 1))
                        x_in(nxt, half)
                    store(i)
                store(NBLK - 1)
                for j in range(2):
                    sp.wait_ge(x2_out[j], 16 * NT // 2)

            @block.tensor
            def _(pe):
                for k in range(KD):
                    pe.wait_ge(s["m_n"], MC)
                    if k >= 2:
                        pe.wait_ge(s["m_Tc"], k - 1)
                    for c in range(MC):
                        last = nc.tensor.transpose(b[k % 2][:, c * P:(c + 1) * P], mem_n[c][:, k * P:(k + 1) * P], ident)
                    last.then_inc(s["m_T"], 1)
                pe.wait_ge(s["m_Tc"], KD)
                pe.wait_ge(s["wkv_in"], 16)
                for c in range(XC):
                    for k in range(KD):
                        last = nc.tensor.matmul(b[2][:, c * MEM:(c + 1) * MEM], wkv[:, k, c * P:(c + 1) * P], memT[:, k, :],
                                                start=(k == 0), stop=(k == KD - 1))
                last.then_inc(s["m_k"], 1)
                for c in range(MC):
                    for k in range(KD):
                        last = nc.tensor.matmul(b[3][:, c * XW:(c + 1) * XW], memT[:, k, c * P:(c + 1) * P], wkv[:, k, XW:2 * XW],
                                                start=(k == 0), stop=(k == KD - 1))
                last.then_inc(s["m_v"], 1)
                pe.wait_ge(s["m_kc"], 1)
                pe.wait_ge(s["m_vc"], 1)
                pe.wait_ge(s["w_out_in"], 16)

                def branch(i, unit):
                    m, br = unit // 2, unit % 2
                    if unit == 0:
                        pe.wait_ge(s["o_in"], i * 16 + 16)
                    pe.wait_ge(s["b_g" if br else "a_g"], i * KD + m)
                    for k in range(HM):
                        last = nc.tensor.matmul(b[br][:, :], w_out[:, br * HM + k, m * P:(m + 1) * P],
                                                oT_in[:, br * HM + k, :], start=(k == 0), stop=(k == HM - 1))
                    last.then_inc(s["ab_mm"], 1)

                def body(i, more):
                    def next_units(first, n):
                        for unit in range(first, first + n) if more else ():
                            branch(i + 1, unit)

                    def scores(h):
                        rows = slice((h % 2) * XA_DIM, (h % 2 + 1) * XA_DIM)
                        if h >= 1:
                            pe.wait_ge(s["exp_ok"], i * (XA_HEADS * TB) + TB * h)
                        for j in range(TB):
                            last = nc.tensor.matmul(b[3 + j // 2][:, (j % 2) * MEM:(j % 2 + 1) * MEM],
                                                    qT[rows, h // 2, j * P:(j + 1) * P], kT[rows, h // 2, :], start=True, stop=True)
                        last.then_inc(s["s_mm"], 1)

                    def turned(h):
                        pe.wait_ge(s["p_ok"], i * XA_HEADS + (h + 1))
                        for c in range(MC):
                            if h >= 1:
                                pe.wait_ge(s["pT_ok"], i * (XA_HEADS * MC) + MC * (h - 1) + c + 1)
                            for j in range(TB):
                                last = nc.tensor.transpose(b[5 + c][:, j * P:(j + 1) * P], p[:, j, c * P:(c + 1) * P], ident)
                            last.then_inc(s["pT_mm"], 1)

                    def values(h):
                        rows = slice((h % 2) * XA_DIM, (h % 2 + 1) * XA_DIM)
                        if h == 0:
                            pe.wait_ge(s["lg_ok"], i)
                        elif h % 2 == 0:
                            pe.wait_ge(s["aT_ok"], i * XC + h // 2)
                        for c in range(MC):
                            pe.wait_ge(s["pT_ok"], i * (XA_HEADS * MC) + MC * h + c + 1)
                            last = nc.tensor.matmul(b[7][rows, :], vm[:, c, h * XA_DIM:(h + 1) * XA_DIM], pT[:, c, :],
                                                    start=(c == 0), stop=(c == MC - 1))
                        last.then_inc(s["pv_mm"], 1)

                    pe.wait_ge(s["sum1"], i * (KD - 1) + (KD - 1))
                    nc.tensor.matmul(b[2][:, :], ones, sq[:, 0, :], start=True, stop=True).then_inc(s["ss1"], 1)
                    next_units(0, 2)
                    pe.wait_ge(s["nat_ok"], i * (2 * TB))
                    for c in range(XC):
                        for k in range(KD):
                            if c == 0:
                                pe.wait_ge(s["h1"], i * KD + (k + 1))
                            last = nc.tensor.matmul(b[5 + c][:, :], wq[:, k, c * P:(c + 1) * P], hT[:, k, :],
                                                    start=(k == 0), stop=(k == KD - 1))
                        last.then_inc(s["q_mm"], 1)
                    next_units(2, 2)
                    pe.wait_ge(s["q_ok"], i * XC + XC)
                    scores(0)
                    next_units(4, 2)
                    for h in range(XA_HEADS):
                        turned(h)
                        if h + 1 < XA_HEADS:
                            scores(h + 1)
                        next_units(6 + 2 * h, 1)
                        values(h)
                        next_units(7 + 2 * h, 1)
                    pe.wait_ge(s["aT_ok"], i * XC + XC)
                    for m in range(KD):
                        if m >= 4:
                            pe.wait_ge(s["x_add2"], i * KD + (m - 3))
                        for c in range(XC):
                            last = nc.tensor.matmul(b[3 + m % 4][:, :], wo[:, c, m * P:(m + 1) * P], aT[:, c, :],
                                                    start=(c == 0), stop=(c == XC - 1))
                        last.then_inc(s["wo_mm"], 1)
                    pe.wait_ge(s["sum2"], i * (KD - 1) + (KD - 1))
                    nc.tensor.matmul(b[2][:, :], ones, sq[:, 0, :], start=True, stop=True).then_inc(s["ss2"], 1)
                    for n in range(2 * TB):
                        j, half = n // 2, n % 2
                        if n >= 4:
                            pe.wait_ge(s["nat_ok"], i * (2 * TB) + (n - 3))
                        for m in range(4):
                            last = nc.tensor.transpose(b[3 + n % 4][:, m * P:(m + 1) * P], xT[:, 4 * half + m, j * P:(j + 1) * P], ident)
                        last.then_inc(s["nat_mm"], 1)
                    next_units(14, 2)
                    pe.wait_ge(s["h2"], i * KD + KD)
                    for j in range(TB):
                        for k in range(KD):
                            last = nc.tensor.matmul(b[7][:, j * NR:(j + 1) * NR], hT[:, k, j * P:(j + 1) * P], w_r[:, k, :],
                                                    start=(k == 0), stop=(k == KD - 1))
                    last.then_inc(s["lg_mm"], 1)

                for unit in range(2 * KD):
                    branch(0, unit)
                pe.wait_ge(s["w_in"], 16 * 8)
                with pe.Fori(0, NBLK - 1) as i:
                    body(i, more=True)
                body(NBLK - 1, more=False)

            @block.scalar
            def _(act):
                act.wait_ge(s["mem_in"], 16 * MC)
                for c in range(MC):
                    nc.scalar.activation(mem_sq[:, c, :], mem_n[c][:, :], ACT.Square, accum_out=mss[:, c:c + 1]).then_inc(s["m_sq"], 1)
                act.wait_ge(s["m_sq"], MC)
                nc.scalar.activation(mr[:, :], mss[:, :], ACT.Ln, bias=t["eps"][:, 0:1], scale=1.0 / D).then_inc(s["m_ln"], 1)
                act.wait_ge(s["m_ln"], 1)
                nc.scalar.activation(mr[:, :], mr[:, :], ACT.Exp, scale=-0.5).then_inc(s["m_r"], 1)
                act.wait_ge(s["m_r"], 1)
                for c in range(MC):
                    nc.scalar.activation(mem_n[c][:, :], mem_n[c][:, :], ACT.Copy, scale=mr[:, c:c + 1]).then_inc(s["m_n"], 1)
                act.wait_ge(s["m_k"], 1)
                nc.scalar.activation(kT[:, :, :], quad(b[2][:, :], MEM), ACT.Copy).then_inc(s["m_kc"], 1)
                act.wait_ge(s["m_v"], 1)
                nc.scalar.activation(vm[:, :, :], quad(b[3][:, :], XW), ACT.Copy).then_inc(s["m_vc"], 1)

                def body(i):
                    for m in range(KD):
                        act.wait_ge(s["x_add"], i * KD + (m + 1))
                        act.wait_ge(s["ss2"], i)
                        nc.scalar.activation(sq[:, m, :], xm[:, m, :], ACT.Square).then_inc(s["sq1"], 1)
                    act.wait_ge(s["ss1"], i + 1)
                    act.wait_ge(s["h2"], i * KD)
                    nc.scalar.activation(rB[:, :], b[2][:, :], ACT.Ln, bias=t["eps"][:, 0:1], scale=1.0 / D).then_inc(s["ln1"], 1)
                    act.wait_ge(s["ln1"], i + 1)
                    nc.scalar.activation(rB[:, :], rB[:, :], ACT.Exp, scale=-0.5).then_inc(s["r1"], 1)
                    for c in range(XC):
                        act.wait_ge(s["q_mm"], i * XC + (c + 1))
                        nc.scalar.activation(qT[:, c, :], b[5 + c][:, :], ACT.Copy).then_inc(s["q_ok"], 1)

                    def exps(h):
                        act.wait_ge(s["nmx_ok"], i * XA_HEADS + (h + 1))
                        if h >= 1:
                            act.wait_ge(s["pT_mm"], i * (XA_HEADS * MC) + MC * h)
                        for j in range(TB):
                            nc.scalar.activation(p[:, j, :], b[3 + j // 2][:, (j % 2) * MEM:(j % 2 + 1) * MEM],
                                                 ACT.Exp, bias=nmx[:, h, j:j + 1], scale=XA_DIM ** -0.5,
                                                 accum_out=ssum[:, h, j:j + 1]).then_inc(s["exp_ok"], 1)

                    exps(0)
                    for h in range(XA_HEADS):
                        for c in range(MC):
                            act.wait_ge(s["pT_mm"], i * (XA_HEADS * MC) + MC * h + c + 1)
                            act.wait_ge(s["pv_mm"], i * XA_HEADS + h)
                            nc.scalar.activation(pT[:, c, :], b[5 + c][:, :], ACT.Copy).then_inc(s["pT_ok"], 1)
                        if h + 1 < XA_HEADS:
                            exps(h + 1)
                        if h % 2 == 1:
                            act.wait_ge(s["pv_mm"], i * XA_HEADS + (h + 1))
                            nc.scalar.activation(aT[:, h // 2, :], b[7][:, :], ACT.Copy).then_inc(s["aT_ok"], 1)
                    for m in range(KD):
                        act.wait_ge(s["x_add2"], i * KD + (m + 1))
                        nc.scalar.activation(sq[:, m, :], xT[:, m, :], ACT.Square).then_inc(s["sq2"], 1)
                    act.wait_ge(s["ss2"], i + 1)
                    act.wait_ge(s["h1"], i * KD + KD)
                    nc.scalar.activation(rB[:, :], b[2][:, :], ACT.Ln, bias=t["eps"][:, 0:1], scale=1.0 / D).then_inc(s["ln2"], 1)
                    act.wait_ge(s["ln2"], i + 1)
                    nc.scalar.activation(rB[:, :], rB[:, :], ACT.Exp, scale=-0.5).then_inc(s["r2"], 1)

                with act.Fori(0, NBLK) as i:
                    body(i)

            @block.gpsimd
            def _(pool):

                def merge(i, chunks):
                    for m in chunks:
                        pool.wait_ge(s["a_g"], i * KD + (m + 1))
                        pool.wait_ge(s["b_g"], i * KD + (m + 1))
                        nc.gpsimd.tensor_tensor(gates[:, m, :], gates[:, m, :], gates[:, KD + m, :], ALU.add).then_inc(s["ab"], 1)

                def residual(i, chunks):
                    for m in chunks:
                        pool.wait_ge(s[f"x_in{m // HM}"], i * 16 + 16)
                        pool.wait_ge(s["ab"], i * KD + (m + 1))
                        nc.gpsimd.tensor_tensor(xm[:, m, :], xm[:, m, :], gates[:, m, :], ALU.add).then_inc(s["x_add"], 1)

                for m in range(KD):
                    merge(0, range(m, m + 1))
                    residual(0, range(m, m + 1))
                with pool.Fori(0, NBLK - 1) as i:
                    merge(i + 1, range(KD - 1))
                    residual(i + 1, range(KD - 1))
                    merge(i + 1, range(KD - 1, KD))
                    residual(i + 1, range(KD - 1, KD))

            @block.vector
            def _(dve):
                for k in range(KD):
                    dve.wait_ge(s["m_T"], k + 1)
                    dve.wait_ge(s["gm_in"], 16)
                    nc.vector.tensor_scalar(memT[:, k, :], b[k % 2][:, 0:MEM], gm[:, k:k + 1], None, ALU.mult).then_inc(s["m_Tc"], 1)

                def gated(i, unit):
                    m, br = unit // 2, unit % 2
                    if m % HM == 0 and br == 0:
                        dve.wait_ge(s[f"g_in{m // HM}"], i * 32 + 32)
                    dve.wait_ge(s["ab_mm"], i * (2 * KD) + (unit + 1))
                    at = br * KD + m
                    nc.vector.tensor_tensor(gates[:, at, :], b[br][:, :], gates[:, at, :], ALU.mult).then_inc(s["b_g" if br else "a_g"], 1)

                def add_squares(i, which, m):
                    dve.wait_ge(s[f"sq{which}"], i * KD + (m + 1))
                    dve.wait_ge(s[f"sum{which}"], i * (KD - 1) + (m - 1))
                    nc.vector.tensor_tensor(sq[:, 0, :], sq[:, 0, :], sq[:, m, :], ALU.add).then_inc(s[f"sum{which}"], 1)

                def body(i, more):
                    def next_units(first, n):
                        for unit in range(first, first + n) if more else ():
                            gated(i + 1, unit)

                    def peak(h):
                        dve.wait_ge(s["s_mm"], i * XA_HEADS + (h + 1))
                        if h == 0:
                            dve.wait_ge(s["exp_ok"], i * (XA_HEADS * TB))
                        for a in range(2):
                            nc.vector.tensor_reduce(mx[:, h, 2 * a:2 * a + 2], quad(b[3 + a][:, :], MEM), axis=AX.X,
                                                    op=ALU.max).then_inc(s["mx_ok"], 1)
                        dve.wait_ge(s["mx_ok"], i * (2 * XA_HEADS) + 2 * (h + 1))
                        nc.vector.tensor_scalar(nmx[:, h, :], mx[:, h, :], -XA_DIM ** -0.5, None, ALU.mult).then_inc(s["nmx_ok"], 1)

                    def norm(h):
                        dve.wait_ge(s["exp_ok"], i * (XA_HEADS * TB) + TB * (h + 1))
                        nc.vector.reciprocal(rsum[:, h, :], ssum[:, h, :]).then_inc(s["rs_ok"], 1)
                        dve.wait_ge(s["rs_ok"], i * XA_HEADS + (h + 1))
                        nc.vector.tensor_tensor(p[:, :, :], p[:, :, :], bc(rsum[:, h, :], MEM), ALU.mult).then_inc(s["p_ok"], 1)

                    add_squares(i, 1, KD - 1)
                    dve.wait_ge(s["r1"], i + 1)
                    dve.wait_ge(s["lg_mm"], i)
                    for m in range(KD):
                        nc.vector.scalar_tensor_tensor(hT[:, m, :], xm[:, m, :], gx[:, m:m + 1], rB[:, :],
                                                       ALU.mult, ALU.mult).then_inc(s["h1"], 1)
                    next_units(0, 4)
                    peak(0)
                    next_units(4, 1)
                    norm(0)
                    next_units(5, 1)
                    for h in range(XA_HEADS):
                        if h + 1 < XA_HEADS:
                            peak(h + 1)
                        next_units(6 + 2 * h, 1)
                        if h + 1 < XA_HEADS:
                            norm(h + 1)
                        next_units(7 + 2 * h, 1)
                    for m in range(KD):
                        dve.wait_ge(s["wo_mm"], i * KD + (m + 1))
                        nc.vector.tensor_tensor(xT[:, m, :], xm[:, m, :], b[3 + m % 4][:, :], ALU.add).then_inc(s["x_add2"], 1)
                        if m >= 2:
                            add_squares(i, 2, m - 1)
                    add_squares(i, 2, KD - 1)
                    for n in range(2 * TB):
                        j, half = n // 2, n % 2
                        if half == 0:
                            dve.wait_ge(x2_out[j % 2], i * 32 + 16 * (j // 2))
                        dve.wait_ge(s["nat_mm"], i * (2 * TB) + (n + 1))
                        nc.vector.tensor_copy(x2n[j % 2][:, half * BLK:(half + 1) * BLK], b[3 + n % 4][:, :]).then_inc(s["nat_ok"], 1)
                    next_units(14, 1)
                    dve.wait_ge(s["r2"], i + 1)
                    dve.wait_ge(s["q_mm"], i * XC + XC)
                    dve.wait_ge(s["x_add2"], i * KD + KD)
                    for m in range(KD):
                        nc.vector.scalar_tensor_tensor(hT[:, m, :], xT[:, m, :], gf[:, m:m + 1], rB[:, :],
                                                       ALU.mult, ALU.mult).then_inc(s["h2"], 1)
                    next_units(15, 1)
                    for m in range(1, KD - 1) if more else ():
                        add_squares(i + 1, 1, m)
                    dve.wait_ge(s["lg_mm"], i + 1)
                    nc.vector.tensor_tensor(t["logits"][:, ds(i * TB, TB), :], quad(b[7][:, 0:TB * NR], NR), bc_mid(bias_r[:, :], TB),
                                            ALU.add).then_inc(s["lg_ok"], 1)

                for unit in range(2 * KD):
                    gated(0, unit)
                for m in range(1, KD - 1):
                    add_squares(0, 1, m)
                dve.wait_ge(s["w_in"], 16 * 8)
                with dve.Fori(0, NBLK - 1) as i:
                    body(i, more=True)
                body(NBLK - 1, more=False)
                dve.wait_ge(s["lg_ok"], NBLK)


W_SLOTS = 3
SLOT_BLOCKS = MAX_MOE + 2


def load_expert(sp, t, e, slot):
    for name, src in (("wg", "we_gate"), ("wu", "we_up"), ("wd", "we_down")):
        rows = t[src][0].rearrange("e (k p) n -> e p k n", p=P)[ds(e, 1), :, :, :]
        sp.dma_start(t[name][slot][:, :, :], rows.rearrange("e p k n -> p (e k) n")).then_inc(t[name + "_in"][slot], 16)


def phase_route(nc, t):
    with Phase(nc, "F") as ph:
        NEG = -3.0e38
        lg = t["logits"]
        g8, gv, gi = ph.sb("g8", [P, NT, 8]), ph.sb("gv", [P, NT, 8]), ph.sb("gi", [P, NT, 8], U32)
        gif = ph.sb("gif", [P, NT])
        ohg, e4 = ph.sb("ohg", [P, NT, N_GRP]), ph.sb("e4", [P, NT, N_GRP])
        esum, pg = ph.sb("esum", [P, NT]), ph.sb("pg", [P, NT])
        le = ph.sb("le", [P, NT, NE])
        ev, ei = ph.sb("ev", [P, NT, 8]), ph.sb("ei", [P, NT, 8], U32)
        eif = ph.sb("eif", [P, NT, TOP_K])
        oh = [ph.sb(f"oh{j}", [P, NT, NE]) for j in range(TOP_K)]
        both, pos, tmp = ph.sb("both", [P, NT, NE]), ph.sb("pos", [P, NT, NE]), ph.sb("tmp", [P, NT, NE])
        tot, run = ph.sb("tot", [P, NT, NE]), ph.sb("run", [P, NT + 1, NE])
        cmp = ph.sb("cmp", [P, NE, NT])
        blocks, ends, base = ph.sb("blocks", [P, NE]), ph.sb("ends", [P, NE]), ph.sb("base", [P, NE])
        dst = ph.sb("dst", [P, NT, TOP_K])
        e1, w1 = ph.sb("e1", [P, NT]), ph.sb("w1", [P, NT])
        rows_f, over = ph.sb("rows_f", [P, SLOT_BLOCKS]), ph.sb("over", [P, SLOT_BLOCKS])
        CH = NT * TOP_K
        PLACED = CH // 4
        above, starts = ph.sb("above", [P, CH, SLOT_BLOCKS + 1]), ph.sb("starts", [P, SLOT_BLOCKS + 1])
        n_above, place = ph.sb("n_above", [P, CH]), ph.sb("place", [P, CH])
        of_place = [ph.sb(f"of_place{i}", [P, PLACED, P]) for i in range(2)]
        of_block = ph.sb("of_block", [P, CH, SLOT_BLOCKS])
        pad = ph.sb("pad", [P, 1])
        pc = [ph.bank(f"c{i}") for i in range(3)]
        const = t["const"]
        ones, exc = (const[:, k:k + P] for k in (K_ONE, K_EXC))
        iota = const[:, K_IOTA:K_IOTA + 32]
        step, mm, act_done, placed, place_used = (ph.sem(s) for s in ("step", "mm", "act_done", "placed", "place_used"))

        with nc.Block() as block:
            mark = {}

            @block.vector
            def _(dve):
                count = [0]

                def note(ins):
                    count[0] += 1
                    ins.then_inc(step, 1)

                def link(ins):
                    note(ins)
                    dve.wait_ge(step, count[0])

                v = nc.vector
                link(v.memset(g8[:, :, :], NEG))
                link(v.tensor_copy(g8[:, :, 0:N_GRP], lg[:, :, 0:N_GRP]))
                for i in range(NT):
                    (link if i == NT - 1 else note)(v.max(gv[:, i, :], g8[:, i, :]))
                for i in range(NT):
                    (link if i == NT - 1 else note)(v.max_index(gi[:, i, :], gv[:, i, :], g8[:, i, :]))
                link(v.tensor_copy(gif[:, :], gi[:, :, 0]))
                link(v.tensor_tensor(ohg[:, :, :], bc_mid(iota[:, 0:N_GRP], NT), bc(gif[:, :], N_GRP), ALU.is_equal))
                link(v.tensor_tensor(e4[:, :, :], lg[:, :, 0:N_GRP], bc(gv[:, :, 0], N_GRP), ALU.subtract))
                mark["e4"] = count[0]
                four = le[:, :, :].rearrange("p t (g e) -> p (t g) e", g=N_GRP)
                flat = ohg[:, :, :].rearrange("p t g -> p (t g)")
                for g in range(N_GRP):
                    (link if g == N_GRP - 1 else note)(v.tensor_tensor(le[:, :, g * PER_GRP:(g + 1) * PER_GRP], lg[:, :, N_GRP + g * PER_GRP:N_GRP + (g + 1) * PER_GRP],
                                         bc(ohg[:, :, g], PER_GRP), ALU.mult))
                link(v.tensor_scalar(ohg[:, :, :], ohg[:, :, :], -1.0, -NEG / 2, ALU.add, ALU.mult))
                link(v.tensor_tensor(four, four, bc(flat, PER_GRP), ALU.add))
                for i in range(NT):
                    (link if i == NT - 1 else note)(v.max(ev[:, i, :], le[:, i, :]))
                for i in range(NT):
                    (link if i == NT - 1 else note)(v.max_index(ei[:, i, :], ev[:, i, :], le[:, i, :]))
                link(v.tensor_copy(eif[:, :, :], ei[:, :, 0:TOP_K]))
                for j in range(TOP_K):
                    link(v.tensor_tensor(oh[j][:, :, :], bc_mid(iota, NT), bc(eif[:, :, j], NE), ALU.is_equal))
                link(v.tensor_tensor(both[:, :, :], oh[0][:, :, :], oh[1][:, :, :], ALU.add))
                link(v.tensor_tensor(e1[:, :], ev[:, :, 1], ev[:, :, 0], ALU.subtract))
                mark["both"] = count[0]
                dve.wait_ge(mm, 1)
                note(v.tensor_copy(pos[:, :, :], quad(pc[0][:, :], NE)))
                note(v.tensor_copy(tot[:, :, :], quad(pc[1][:, :], NE)))
                link(v.memset(run[:, 0, :], 0.0))
                for i in range(NT):
                    link(v.tensor_tensor(run[:, i + 1, :], run[:, i, :], tot[:, i, :], ALU.add))
                link(v.tensor_scalar(tmp[:, 0, 0:NT], iota[:, 0:NT], float(P), None, ALU.mult))
                link(v.tensor_tensor(cmp[:, :, :], bc(run[:, NT, :], NT), bc_mid(tmp[:, 0, 0:NT], NE), ALU.is_gt))
                link(v.tensor_reduce(blocks[:, :], cmp[:, :, :], axis=AX.X, op=ALU.add))
                link(v.tensor_scalar(blocks[:, :], blocks[:, :], 1.0, None, ALU.max))
                link(v.tensor_tensor_scan(ends[:, :], blocks[:, :], blocks[:, :], 0.0, ALU.add, ALU.bypass))
                link(v.tensor_tensor(base[:, :], ends[:, :], blocks[:, :], ALU.subtract))
                note(v.tensor_copy(t["n_blocks"][:, 0:NE], blocks[:, :]))
                note(v.tensor_copy(t["n_blocks"][:, NE:2 * NE], base[:, :]))
                link(v.tensor_copy(t["n_blocks"][:, 2 * NE:2 * NE + 1], ends[:, NE - 1:NE]))
                link(v.tensor_scalar(base[:, :], base[:, :], float(P), None, ALU.mult))
                link(v.tensor_tensor(pos[:, :, :], pos[:, :, :], run[:, 0:NT, :], ALU.add))
                link(v.tensor_tensor(pos[:, :, :], pos[:, :, :], bc_mid(base[:, :], NT), ALU.add))
                for j in range(TOP_K):
                    link(v.tensor_tensor(tmp[:, :, :], pos[:, :, :], oh[j][:, :, :], ALU.mult))
                    link(v.tensor_reduce(dst[:, :, j:j + 1], tmp[:, :, :], axis=AX.X, op=ALU.add))
                d = dst[:, :, :].rearrange("p t j -> p (t j)")
                link(v.tensor_scalar(starts[:, :], const[:, K_PAD:K_PAD + SLOT_BLOCKS + 1], -float(TOP_K * SEQ), float(P), ALU.add, ALU.mult))
                link(v.tensor_tensor(above[:, :, :], bc(d, SLOT_BLOCKS + 1), bc_mid(starts[:, :], CH), ALU.is_ge))
                link(v.tensor_reduce(n_above[:, :].unsqueeze(2), above[:, :, :], axis=AX.X, op=ALU.add))
                link(v.scalar_tensor_tensor(place[:, :], n_above[:, :], -float(P), d, ALU.mult, ALU.add))
                link(v.tensor_scalar(place[:, :], place[:, :], float(P + TOP_K * SEQ), None, ALU.add))
                link(v.tensor_tensor(of_block[:, :, :], above[:, :, 0:SLOT_BLOCKS], above[:, :, 1:SLOT_BLOCKS + 1], ALU.subtract))
                for j in range(TOP_K):
                    rows_of, mine = const[:, K_TOK + j * NT:K_TOK + (j + 1) * NT], of_block[:, j::TOP_K, :]
                    link(v.scalar_tensor_tensor(mine, bc(rows_of, SLOT_BLOCKS), 1.0, mine, ALU.add, ALU.mult))
                for c in range(CH // PLACED):
                    if c >= 2:
                        dve.wait_ge(place_used, c - 1)
                    v.tensor_tensor(of_place[c % 2][:, :, :], bc_mid(const[:, K_PAD:K_PAD + P], PLACED),
                                    bc(place[:, c * PLACED:(c + 1) * PLACED], P), ALU.is_equal).then_inc(placed, 1)
                dve.wait_ge(act_done, 2)
                link(v.tensor_reduce(esum[:, :].unsqueeze(2), e4[:, :, :], axis=AX.X, op=ALU.add))
                link(v.reciprocal(pg[:, :], esum[:, :]))
                link(v.tensor_scalar(w1[:, :], e1[:, :], 1.0, None, ALU.add))
                link(v.reciprocal(w1[:, :], w1[:, :]))
                link(v.tensor_tensor(w1[:, :], w1[:, :], pg[:, :], ALU.mult))
                link(v.tensor_copy(t["wts"][:, :, 0], w1[:, :]))
                link(v.tensor_tensor(t["wts"][:, :, 1], w1[:, :], e1[:, :], ALU.mult))
                link(v.tensor_scalar(pad[:, :], const[:, K_TOK:K_TOK + 1], float(TOP_K * SEQ + 1), None, ALU.add))
                dve.wait_ge(place_used, CH // PLACED)
                link(v.tensor_scalar(over[:, :], pc[2][:, 0:SLOT_BLOCKS], 0.5, None, ALU.is_lt))
                link(v.tensor_scalar(over[:, :], over[:, :], pad[:, 0:1], None, ALU.mult))
                link(v.scalar_tensor_tensor(rows_f[:, :], pc[2][:, 0:SLOT_BLOCKS], -1.0, over[:, :], ALU.add, ALU.add))
                link(v.tensor_copy(t["slot_row"][:, :], rows_f[:, :]))
                for j in range(TOP_K):
                    link(v.tensor_scalar(over[:, :], rows_f[:, :], float(SEQ), float(SEQ), ALU.is_ge, ALU.mult))
                    link(v.tensor_tensor(rows_f[:, :], rows_f[:, :], over[:, :], ALU.subtract))
                link(v.tensor_copy(t["slot_tok"][:, :], rows_f[:, :]))

            @block.sync
            def _(sp):
                for e in range(W_SLOTS):
                    load_expert(sp, t, e, e)

            @block.scalar
            def _(act):
                act.wait_ge(step, mark["e4"])
                nc.scalar.activation(e4[:, :, :], e4[:, :, :], ACT.Exp).then_inc(act_done, 1)
                act.wait_ge(step, mark["both"])
                nc.scalar.activation(e1[:, :], e1[:, :], ACT.Exp).then_inc(act_done, 1)

            @block.tensor
            def _(pe):
                pe.wait_ge(step, mark["both"])
                flat = both[:, :, :].rearrange("p t e -> p (t e)")
                nc.tensor.matmul(pc[0][:, :], exc, flat, start=True, stop=True)
                nc.tensor.matmul(pc[1][:, :], ones, flat, start=True, stop=True).then_inc(mm, 1)
                for n in range(CH):
                    c = n // PLACED
                    if n % PLACED == 0:
                        pe.wait_ge(placed, c + 1)
                    last = nc.tensor.matmul(pc[2][:, 0:SLOT_BLOCKS], of_place[c % 2][:, n % PLACED, :], of_block[:, n, :],
                                            start=(n == 0), stop=(n == CH - 1))
                    if n % PLACED == PLACED - 1:
                        last.then_inc(place_used, 1)


def phase_experts(nc, t):
    with Phase(nc, "G") as ph:
        KE = DE // P
        wg, wu, wd = t["wg"], t["wu"], t["wd"]
        TURNS, REST = divmod(NE, W_SLOTS)
        tok, row = ph.sb("tok", [P, 1], I32), ph.sb("row", [P, 1], I32)
        xg, xn = ph.sb("xg", [P, D]), ph.sb("xn", [P, D])
        xsq = ph.sb("xsq", [P, D])
        ss, lnr, r = (ph.sb(s, [P, 1]) for s in ("ss", "lnr", "r"))
        hT = ph.sb("hT", [P, KD, P])
        sg, a, aT = ph.sb("sg", [P, DE]), ph.sb("a", [P, DE]), ph.sb("aT", [P, KE, P])
        y = ph.sb("y", [P, D])
        gf = ph.sb("gf", [P, KD])
        bx = [ph.bank(f"x{i}") for i in range(2)]
        bg, ba = ph.bank("g"), ph.bank("a")
        bu = [ph.bank(f"u{i}") for i in range(2)]
        HALF = DE // 2
        KH = HALF // P
        by = [ph.bank(f"y{i}") for i in range(2)]
        w_used = [ph.sem(f"w_used{i}") for i in range(W_SLOTS)]
        names = ("gf_in", "tok_ok", "row_ok", "indices_set", "expert_begun", "sq_ok", "ln_ok", "r_ok", "xn_ok", "xT_mm", "hT_ok", "g_mm", "u_mm", "sg_ok", "a_ok",
                 "aT_mm", "aT_ok", "y_mm", "y0_ok", "y1_ok")
        s = {n: ph.sem(n) for n in names} | {n: ph.pool_dma_sem(n) for n in ("xg_in", "y_out")}
        ident = t["const"][:, K_ID:K_ID + P]
        x_rows = t["x2_d"]
        nb = t["n_blocks"]
        def all_blocks(eng):
            return eng.value_load(nb[0:1, 2 * NE:2 * NE + 1], min_val=NE, max_val=MAX_MOE)

        with nc.Block() as block:

            @block.sync
            def _(sp):
                sp.dma_start(gf[:, :], t["g_ffn"].rearrange("o (k p) -> p (o k)", p=P)).then_inc(s["gf_in"], 16)
                with sp.Fori(1, TURNS) as i:
                    for q in range(W_SLOTS):
                        sp.wait_ge(w_used[q], i)
                        load_expert(sp, t, i * W_SLOTS + q, q)
                for q in range(REST):
                    sp.wait_ge(w_used[q], TURNS)
                    load_expert(sp, t, TURNS * W_SLOTS + q, q)

            @block.gpsimd
            def _(pool):
                n = all_blocks(pool)

                def gather(i):
                    nc.gpsimd.tensor_copy(tok[:, :], t["slot_tok"][:, ds(i, 1)]).then_inc(s["tok_ok"], 1)
                    pool.wait_ge(s["tok_ok"], i + 1)
                    pool.sem_inc(s["indices_set"], 1)
                    pool.indirect_dma_start(xg[:, :], None, x_rows, bass.IndirectOffsetOnAxis(ap=tok[:, 0:1], axis=0)).then_inc(s["xg_in"], 16)

                gather(0)
                pool.wait_ge(s["xn_ok"], 1)
                gather(1)
                with pool.Fori(0, n) as i:
                    pool.wait_ge(s["xn_ok"], i + 2)
                    gather(i + 2)
                    pool.wait_ge(s["y_out"], i * 16)
                    nc.gpsimd.tensor_copy(row[:, :], t["slot_row"][:, ds(i, 1)]).then_inc(s["row_ok"], 1)
                    pool.wait_ge(s["row_ok"], i + 1)
                    pool.wait_ge(s["y0_ok"], i + 1)
                    pool.wait_ge(s["y1_ok"], i + 1)
                    pool.sem_inc(s["indices_set"], 1)
                    pool.indirect_dma_start(t["y_d"], bass.IndirectOffsetOnAxis(ap=row[:, 0:1], axis=0), y[:, :], None).then_inc(s["y_out"], 16)
                pool.wait_ge(s["y_out"], n * 16)
                pool.wait_ge(s["xg_in"], n * 16 + 32)

            @block.scalar
            def _(act):
                n = all_blocks(act)

                def norm(i):
                    act.wait_ge(s["xg_in"], i * 16 + 16)
                    nc.scalar.activation(xsq[:, :], xg[:, :], ACT.Square, accum_out=ss[:, :]).then_inc(s["sq_ok"], 1)
                    act.wait_ge(s["sq_ok"], i + 1)
                    nc.scalar.activation(lnr[:, :], ss[:, :], ACT.Ln, bias=t["eps"][:, 0:1], scale=1.0 / D).then_inc(s["ln_ok"], 1)
                    act.wait_ge(s["ln_ok"], i + 1)
                    nc.scalar.activation(r[:, :], lnr[:, :], ACT.Exp, scale=-0.5).then_inc(s["r_ok"], 1)
                    act.wait_ge(s["r_ok"], i + 1)
                    act.wait_ge(s["xT_mm"], i)
                    nc.scalar.activation(xn[:, :], xg[:, :], ACT.Copy, scale=r[:, 0:1]).then_inc(s["xn_ok"], 1)

                norm(0)
                with act.Fori(0, n) as i:
                    act.wait_ge(s["g_mm"], i + 1)
                    act.wait_ge(s["a_ok"], i * 2)
                    nc.scalar.activation(sg[:, :], bg[:, :], ACT.Silu).then_inc(s["sg_ok"], 1)
                    norm(i + 1)
                    act.wait_ge(s["y_mm"], i + 1)
                    act.wait_ge(s["y_out"], i * 16)
                    nc.scalar.activation(y[:, 0:BLK], by[0][:, :], ACT.Copy).then_inc(s["y0_ok"], 1)

            @block.vector
            def _(dve):
                n = all_blocks(dve)
                dve.wait_ge(s["gf_in"], 16)

                def scaled(i):
                    for c in range(2):
                        dve.wait_ge(s["xT_mm"], i + 1)
                        nc.vector.tensor_tensor(hT[:, 4 * c:4 * c + 4, :], quad(bx[c][:, :]), bc(gf[:, 4 * c:4 * c + 4], P),
                                                ALU.mult).then_inc(s["hT_ok"], 1)

                scaled(0)
                with dve.Fori(0, n) as i:
                    dve.wait_ge(s["sg_ok"], i + 1)
                    dve.wait_ge(s["aT_mm"], i * 2)
                    for c in range(2):
                        cols = slice(c * HALF, (c + 1) * HALF)
                        dve.wait_ge(s["u_mm"], i * 2 + (c + 1))
                        nc.vector.tensor_tensor(a[:, cols], sg[:, cols], bu[c][:, 0:HALF], ALU.mult).then_inc(s["a_ok"], 1)
                    dve.wait_ge(s["y_mm"], i)
                    for c in range(2):
                        dve.wait_ge(s["aT_mm"], i * 2 + (c + 1))
                        nc.vector.tensor_copy(aT[:, c * KH:(c + 1) * KH, :], quad((bg if c else ba)[:, 0:HALF])).then_inc(s["aT_ok"], 1)
                    scaled(i + 1)
                    dve.wait_ge(s["y_mm"], i + 1)
                    dve.wait_ge(s["y_out"], i * 16)
                    nc.vector.tensor_copy(y[:, BLK:D], by[1][:, :]).then_inc(s["y1_ok"], 1)

            @block.tensor
            def _(pe):
                def rows_T(n):
                    pe.wait_ge(s["xn_ok"], n + 1)
                    pe.wait_ge(s["hT_ok"], n * 2)
                    for k in range(KD):
                        last = nc.tensor.transpose(bx[k // 4][:, (k % 4) * P:(k % 4 + 1) * P], xn[:, k * P:(k + 1) * P], ident)
                    last.then_inc(s["xT_mm"], 1)

                def counts(e):
                    return (pe.value_load(nb[0:1, ds(e, 1)], min_val=1, max_val=SEQ // P),
                            pe.value_load(nb[0:1, ds(e + NE, 1)], min_val=0, max_val=MAX_MOE))

                def half_T(n, c):
                    pe.wait_ge(s["a_ok"], n * 2 + (c + 1))
                    pe.wait_ge(s["aT_ok"], n * 2)
                    for k in range(KH):
                        at = c * KH + k
                        last = nc.tensor.transpose((bg if c else ba)[:, k * P:(k + 1) * P], a[:, at * P:(at + 1) * P], ident)
                    last.then_inc(s["aT_mm"], 1)

                def expert(q, turn, count, first, following=None):
                    for name in ("wg_in", "wu_in", "wd_in"):
                        pe.wait_ge(t[name][q], turn * 16 + 16)
                    pe.sem_inc(s["expert_begun"], 1)
                    with pe.Fori(0, count) as j:
                        n = first + j
                        pe.wait_ge(s["hT_ok"], n * 2 + 2)
                        pe.wait_ge(s["aT_ok"], n * 2)
                        for k in range(KD):
                            last = nc.tensor.matmul(bg[:, :], hT[:, k, :], wg[q][:, k, :], start=(k == 0), stop=(k == KD - 1))
                        last.then_inc(s["g_mm"], 1)
                        pe.wait_ge(s["a_ok"], n * 2)
                        for c in range(2):
                            for k in range(KD):
                                last = nc.tensor.matmul(bu[c][:, 0:HALF], hT[:, k, :], wu[q][:, k, c * HALF:(c + 1) * HALF],
                                                        start=(k == 0), stop=(k == KD - 1))
                            last.then_inc(s["u_mm"], 1)
                        half_T(n, 0)
                        rows_T(n + 1)
                        half_T(n, 1)
                        pe.wait_ge(s["y0_ok"], n)
                        pe.wait_ge(s["y1_ok"], n)
                        for part in range(2):
                            pe.wait_ge(s["aT_ok"], n * 2 + (part + 1))
                            for c in range(2):
                                for k in range(part * KH, (part + 1) * KH):
                                    last = nc.tensor.matmul(by[c][:, :], aT[:, k, :], wd[q][:, k, c * BLK:(c + 1) * BLK],
                                                            start=(k == 0), stop=(k == KE - 1))
                        last.then_inc(s["y_mm"], 1)
                    after = None if following is None else counts(following)
                    pe.wait_ge(s["y_mm"], first + count)
                    pe.sem_inc(w_used[q], 1)
                    return after

                rows_T(0)
                with pe.Fori(0, TURNS) as i:
                    of_next = counts(i * W_SLOTS)
                    for q in range(W_SLOTS):
                        of_next = expert(q, i, *of_next, following=i * W_SLOTS + (q + 1) if q + 1 < W_SLOTS else None)
                of_next = counts(TURNS * W_SLOTS)
                for q in range(REST):
                    of_next = expert(q, TURNS, *of_next, following=TURNS * W_SLOTS + q + 1 if q + 1 < REST else None)


def phase_combine(nc, t):
    with Phase(nc, "H") as ph:
        PER_TURN = 8
        TURNS = NT // PER_TURN

        def tiles(name, shape, dt=F32):
            return [ph.sb(f"{name}{c}", shape, dt) for c in range(PER_TURN)]

        x, o = tiles("x", [P, D]), tiles("o", [P, D])
        y = tiles("y", [P, TOP_K, D])
        ss, r = tiles("ss", [P, 1]), tiles("r", [P, 1])
        g = ph.sb("g", [P, D])
        sems = lambda n: [ph.sem(f"{n}{c}") for c in range(PER_TURN)]
        out_done = [ph.pool_dma_sem(f"out_done{c}") for c in range(PER_TURN)]
        x_in, y_in, add_ok, sq_ok, ln_ok, r_ok, n_ok = (
            sems(n) for n in ("x_in", "y_in", "add_ok", "sq_ok", "ln_ok", "r_ok", "n_ok"))
        g_in = ph.sem("g_in")
        wts_flat = t["wts"][:, :, :].rearrange("p t j -> p (t j)")
        x_d = t["x2_d"].rearrange("(j p) d -> j p d", p=P)
        y_d = t["y_d"][0:TOP_K * SEQ, :].rearrange("(k j p) d -> j p k d", p=P, k=TOP_K)
        out_d = t["out"].rearrange("b (j p) d -> (b j) p d", p=P)

        with nc.Block() as block:

            @block.sync
            def _(sp):
                sp.dma_start(g[:, :], t["g_final"].rearrange("(o d) -> o d", o=1).to_broadcast([P, D])).then_inc(g_in, 16)
                with sp.Fori(0, TURNS) as i:
                    for c in range(PER_TURN):
                        sp.wait_ge(n_ok[c], i)
                        sp.dma_start(x[c][:, :], x_d[ds(i * PER_TURN + c, 1), :, :]).then_inc(x_in[c], 16)
                        sp.dma_start(y[c][:, :, :], y_d[ds(i * PER_TURN + c, 1), :, :, :].rearrange("j p k d -> p (j k) d")).then_inc(y_in[c], 16)

            @block.vector
            def _(dve):
                dve.wait_ge(g_in, 16)
                with dve.Fori(0, TURNS) as i:

                    def combined(c):
                        dve.wait_ge(y_in[c], i * 16 + 16)
                        dve.wait_ge(x_in[c], i * 16 + 16)
                        for j in range(TOP_K):
                            if j:
                                dve.wait_ge(add_ok[c], i * TOP_K + j)
                            nc.vector.scalar_tensor_tensor(x[c][:, :], y[c][:, j, :], wts_flat[:, ds(i * (PER_TURN * TOP_K) + (c * TOP_K + j), 1)],
                                                           x[c][:, :], ALU.mult, ALU.add).then_inc(add_ok[c], 1)

                    def normed(c):
                        dve.wait_ge(r_ok[c], i + 1)
                        dve.wait_ge(out_done[c], i * 16)
                        nc.vector.scalar_tensor_tensor(o[c][:, :], x[c][:, :], r[c][:, 0:1], g[:, :], ALU.mult, ALU.mult).then_inc(n_ok[c], 1)

                    for c in range(PER_TURN):
                        combined(c)
                        if c >= 1:
                            normed(c - 1)
                    normed(PER_TURN - 1)

            @block.scalar
            def _(act):
                with act.Fori(0, TURNS) as i:
                    for c in range(PER_TURN):
                        act.wait_ge(add_ok[c], i * TOP_K + TOP_K)
                        act.wait_ge(out_done[c], i * 16)
                        nc.scalar.activation(o[c][:, :], x[c][:, :], ACT.Square, accum_out=ss[c][:, :]).then_inc(sq_ok[c], 1)
                        act.wait_ge(sq_ok[c], i + 1)
                        nc.scalar.activation(ss[c][:, :], ss[c][:, :], ACT.Ln, bias=t["eps"][:, 0:1], scale=1.0 / D).then_inc(ln_ok[c], 1)
                        act.wait_ge(ln_ok[c], i + 1)
                        nc.scalar.activation(r[c][:, :], ss[c][:, :], ACT.Exp, scale=-0.5).then_inc(r_ok[c], 1)

            @block.gpsimd
            def _(pool):
                with pool.Fori(0, TURNS) as i:
                    for c in range(PER_TURN):
                        pool.wait_ge(n_ok[c], i + 1)
                        pool.dma_start(out_d[ds(i * PER_TURN + c, 1), :, :], o[c][:, :]).then_inc(out_done[c], 16)
                for c in range(PER_TURN):
                    pool.wait_ge(out_done[c], 16 * TURNS)


def build(nc, tensors):
    t = dict(tensors)
    for name, shape in (("xT_d", (KD, P, SEQ)), ("proj_d", (NGRP, P, SEQ)), ("o_d", (KD, P, SEQ)),
                        ("x2_d", (SEQ, D)), ("y_d", (TOP_K * SEQ + P, D))):
        t[name] = nc.dram_tensor(name, shape, F32, kind="Internal").ap()
    with Phase(nc, "all") as ph, nc.allow_non_contiguous_dma(reason="small vectors, a feature on each partition"):
        t["const"] = ph.sb("const", [P, NCONST])
        t["eps"] = ph.sb("eps", [P, 1])
        t["beta"], t["glog"] = (ph.sb(n, [P, NT, DN_HEADS]) for n in ("beta", "glog"))
        t["logits"] = ph.sb("logits", [P, NT, NR])
        t["wts"] = ph.sb("wts", [P, NT, TOP_K])
        t["n_blocks"] = ph.sb("n_blocks", [P, 2 * NE + 1], I32)
        t["slot_tok"], t["slot_row"] = (ph.sb(n, [P, SLOT_BLOCKS], I32) for n in ("slot_tok", "slot_row"))
        with Phase(nc, "h") as hp:
            h_hi, h_lo = (hp.sb(n, [P, KD, SEQ], F32R) for n in ("h_hi", "h_lo"))
            t["ba_hi"], t["ba_lo"] = (hp.sb(n, [P, KD, 2 * DN_HEADS], F32R) for n in ("ba_hi", "ba_lo"))
            t["cw"] = hp.sb("cw", [P, 12, DN_CONV])
            t["alog"], t["dtb"] = (hp.sb(n, [P, DN_HEADS]) for n in ("alog", "dtb"))
            phase_norm_x(nc, t, h_hi, h_lo)
            phase_project(nc, t, h_hi, h_lo)
        phase_mix(nc, t)
        phase_merge(nc, t)
        with Phase(nc, "w") as wp:
            t["wg"], t["wu"] = ([wp.sb(f"{n}{i}", [P, KD, DE]) for i in range(W_SLOTS)] for n in ("wg", "wu"))
            t["wd"] = [wp.sb(f"wd{i}", [P, DE // P, D]) for i in range(W_SLOTS)]
            for n in ("wg_in", "wu_in", "wd_in"):
                t[n] = [wp.sem(f"{n}{i}") for i in range(W_SLOTS)]
            phase_route(nc, t)
            phase_experts(nc, t)
        phase_combine(nc, t)


_INS = ["x", "mem", "g_mix", "w_in", "dn_conv_w", "dn_a_log", "dn_dt_bias", "dn_norm_g", "w_out", "g_xattn", "g_mem",
        "xa_wq", "xa_wkv", "xa_wo", "g_ffn", "w_grp", "b_grp", "w_exp", "b_exp", "we_gate", "we_up", "we_down",
        "g_final"]


def constants():
    import numpy as np
    c = np.zeros((P, NCONST), np.float32)
    p, f = np.arange(P)[:, None], np.arange(P)[None, :]
    c[:, K_ID:K_ID + P] = p == f
    c[:, K_ONE:K_ONE + P] = 1
    c[:, K_INC:K_INC + P] = p <= f
    c[:, K_EXC:K_EXC + P] = p < f
    c[:, K_LOW:K_LOW + P] = p > f
    c[:, K_NEG:K_NEG + P] = MASKED * (f >= p)
    c[:, K_IOTA:K_IOTA + 32] = np.arange(32)
    c[:, K_TOK:K_TOK + TOP_K * NT] = p + P * np.arange(TOP_K * NT)
    c[:, K_PAD:K_PAD + P] = TOP_K * SEQ + f
    for lev in range(NLEV):
        s = 1 << lev
        m = (p // (2 * s) == f // (2 * s)) & ((p // s) % 2 == 1) & ((f // s) % 2 == 0)
        c[:, K_LEV + 2 * lev * P:K_LEV + (2 * lev + 1) * P] = m
        c[:, K_LEV + (2 * lev + 1) * P:K_LEV + (2 * lev + 2) * P] = m.T
    return c


def kernel(**inputs):
    import numpy as _np
    import concourse.bacc as _bacc
    from concourse import mybir as _mybir
    from concourse.bass_utils import run_bass_kernel_spmd as _run

    nc = _bacc.Bacc("TRN2", target_bir_lowering=False, num_devices=1)
    arrays, tensors = {"const_dram": constants()}, {}
    for name in _INS:
        a = _np.ascontiguousarray(inputs[name])
        arrays[f"in_{name}_dram"] = a
        tensors[name] = nc.dram_tensor(f"in_{name}_dram", a.shape, _mybir.dt.from_np(a.dtype), kind="ExternalInput").ap()
    tensors["const_d"] = nc.dram_tensor("const_dram", (P, NCONST), _mybir.dt.float32, kind="ExternalInput").ap()
    tensors["out"] = nc.dram_tensor("out_dram", (1, SEQ, D), _mybir.dt.float32, kind="ExternalOutput").ap()
    build(nc, tensors)
    r = _run(nc, [arrays], core_ids=[0])
    return r.results[0]["out_dram"]
```
